# Optimizing a Trainium2 kernel written in Bass

```python
import math
import jax, jax.numpy as jnp
from jax import lax
import numpy as np

D_MODEL = 1024
BATCH = 1
SEQ = 256
DEPTH = 2

CHUNK = 64
Q_BLOCK = 128

FOX_HEADS = 4
FOX_HEAD_DIM = 64
SB_HEADS = 4
SB_HEAD_DIM = 64
GDN_HEADS = 4
GDN_KEY_DIM = 128
GDN_VAL_DIM = 128
CONV_WIDTH = 4

FOX_W = FOX_HEADS * FOX_HEAD_DIM
SB_W = SB_HEADS * SB_HEAD_DIM
GDN_KW = GDN_HEADS * GDN_KEY_DIM
GDN_VW = GDN_HEADS * GDN_VAL_DIM
MIX_W = FOX_W + SB_W + GDN_VW
N_BRANCH = 3
FFN_HIDDEN = 2816
N_SUBLAYERS = 3

IN_SIZES = (FOX_W, FOX_W, FOX_W, FOX_HEADS,
            SB_W, SB_W, SB_W,
            2 * GDN_KW + GDN_VW, GDN_HEADS, GDN_HEADS,
            GDN_VW,
            N_BRANCH * D_MODEL)
IN_COLS = sum(IN_SIZES)

DEEPNORM_ALPHA = (2.0 * DEPTH) ** 0.25
DEEPNORM_BETA = (8.0 * DEPTH) ** -0.25
LN_EPS = 1e-5
RMS_EPS = 1e-6

kernel_name = 'hybrid_fox_sb_gdn_macaron_deepnorm'

def _layer_norm(x, g, b):
    xf = x.astype(jnp.float32)
    mu = jnp.mean(xf, -1, keepdims=True)
    var = jnp.mean(jnp.square(xf - mu), -1, keepdims=True)
    return ((xf - mu) * lax.rsqrt(var + LN_EPS) * g.astype(jnp.float32) + b.astype(jnp.float32)).astype(x.dtype)

def _l2norm(t):
    return t * lax.rsqrt(jnp.sum(jnp.square(t), -1, keepdims=True) + RMS_EPS)

def _heads(t, h):
    B, S, _ = t.shape
    return t.reshape(B, S, h, -1).transpose(0, 2, 1, 3)

def _q_blocks(t):
    B, H, S = t.shape[:3]
    t = t.reshape((B, H, S // Q_BLOCK, Q_BLOCK) + t.shape[3:])
    return jnp.moveaxis(t, 2, 0)

def _merge_blocks(o):
    nb, B, H, qb, d = o.shape
    return o.transpose(1, 0, 3, 2, 4).reshape(B, nb * qb, H * d)

def _forgetting_attention(q, k, v, log_f):
    S, d = q.shape[2], q.shape[3]
    scale = d ** -0.5
    cum = jnp.cumsum(log_f, axis=-1)
    key_pos = jnp.arange(S)

    def block(args):
        qb, cq, i = args
        qpos = i * Q_BLOCK + jnp.arange(Q_BLOCK)
        s = jnp.einsum('bhqd,bhkd->bhqk', qb, k).astype(jnp.float32) * scale
        s = s + cq[..., :, None] - cum[..., None, :]
        s = jnp.where(key_pos[None, :] <= qpos[:, None], s, -jnp.inf)
        p = jax.nn.softmax(s, axis=-1)
        return jnp.einsum('bhqk,bhkd->bhqd', p.astype(v.dtype), v)

    nb = S // Q_BLOCK
    o = lax.map(block, (_q_blocks(q), _q_blocks(cum), jnp.arange(nb)))
    return _merge_blocks(o)

def _stick_breaking_attention(q, k, v):
    S, d = q.shape[2], q.shape[3]
    scale = d ** -0.5
    key_pos = jnp.arange(S)

    def block(args):
        qb, i = args
        qpos = i * Q_BLOCK + jnp.arange(Q_BLOCK)
        z = jnp.einsum('bhqd,bhkd->bhqk', qb, k).astype(jnp.float32) * scale
        mask = key_pos[None, :] < qpos[:, None]
        log_beta = jax.nn.log_sigmoid(z)
        log_rem = jnp.where(mask, jax.nn.log_sigmoid(-z), 0.0)
        after = lax.cumsum(log_rem, axis=log_rem.ndim - 1, reverse=True) - log_rem
        w = jnp.where(mask, jnp.exp(log_beta + after), 0.0)
        return jnp.einsum('bhqk,bhkd->bhqd', w.astype(v.dtype), v)

    nb = S // Q_BLOCK
    o = lax.map(block, (_q_blocks(q), jnp.arange(nb)))
    return _merge_blocks(o)

def _gated_delta_rule(q, k, v, g, beta):
    f32 = jnp.float32
    B, H, S, dk = q.shape
    dv = v.shape[-1]
    n = S // CHUNK
    q = q.reshape(B, H, n, CHUNK, dk)
    k = k.reshape(B, H, n, CHUNK, dk)
    v = v.reshape(B, H, n, CHUNK, dv)
    beta = beta.reshape(B, H, n, CHUNK)
    gc = jnp.cumsum(g.reshape(B, H, n, CHUNK), axis=-1)
    tri_incl = jnp.tril(jnp.ones((CHUNK, CHUNK), bool))
    tri_strict = jnp.tril(jnp.ones((CHUNK, CHUNK), bool), -1)
    diff = gc[..., :, None] - gc[..., None, :]
    decay = jnp.where(tri_incl, jnp.exp(jnp.where(tri_incl, diff, 0.0)), 0.0)
    k_beta = k * beta[..., None]
    lower = jnp.where(tri_strict, jnp.einsum('bhnid,bhnjd->bhnij', k_beta, k) * decay, 0.0) + jnp.eye(CHUNK, dtype=f32)
    rhs = jnp.concatenate([v * beta[..., None], k_beta * jnp.exp(gc)[..., None]], axis=-1)
    sol = lax.linalg.triangular_solve(lower, rhs, left_side=True, lower=True, unit_diagonal=True)
    u, w = sol[..., :dv], sol[..., dv:]
    intra = jnp.where(tri_incl, jnp.einsum('bhnid,bhnjd->bhnij', q, k) * decay, 0.0)
    q_dec = q * jnp.exp(gc)[..., None]
    k_dec = k * jnp.exp(gc[..., -1:] - gc)[..., None]
    chunk_decay = jnp.exp(gc[..., -1])

    def step(state, xs):
        u_c, w_c, intra_c, qd_c, kd_c, dec_c = xs
        v_new = u_c - jnp.einsum('bhck,bhkv->bhcv', w_c, state)
        o_c = jnp.einsum('bhck,bhkv->bhcv', qd_c, state) + jnp.einsum('bhij,bhjv->bhiv', intra_c, v_new)
        state = state * dec_c[..., None, None] + jnp.einsum('bhck,bhcv->bhkv', kd_c, v_new)
        return state, o_c

    xs = tuple(jnp.moveaxis(t, 2, 0) for t in (u, w, intra, q_dec, k_dec, chunk_decay))
    _, o = lax.scan(step, jnp.zeros((B, H, dk, dv), f32), xs)
    return o.transpose(1, 0, 3, 2, 4).reshape(B, S, H, dv)

def _causal_conv(x, w):
    ch = x.shape[-1]
    return lax.conv_general_dilated(x, w[:, None, :].astype(x.dtype), window_strides=(1,),
                                    padding=[(CONV_WIDTH - 1, 0)],
                                    dimension_numbers=('NWC', 'WIO', 'NWC'),
                                    feature_group_count=ch)

def _gdn_branch(qkv, beta_logit, a_logit, gate, conv_w, a_log, dt_bias, norm_g):
    f32 = jnp.float32
    B, S, _ = qkv.shape
    out_dtype = qkv.dtype
    qkv = jax.nn.silu(_causal_conv(qkv, conv_w)).astype(f32)
    q, k, v = jnp.split(qkv, [GDN_KW, 2 * GDN_KW], axis=-1)
    q = _l2norm(_heads(q, GDN_HEADS)) * GDN_KEY_DIM ** -0.5
    k = _l2norm(_heads(k, GDN_HEADS))
    v = _heads(v, GDN_HEADS)
    beta = jax.nn.sigmoid(beta_logit.astype(f32)).transpose(0, 2, 1)
    g = (-jnp.exp(a_log.astype(f32)) * jax.nn.softplus(a_logit.astype(f32) + dt_bias.astype(f32))).transpose(0, 2, 1)
    o = _gated_delta_rule(q, k, v, g, beta)
    o = o * lax.rsqrt(jnp.mean(jnp.square(o), -1, keepdims=True) + RMS_EPS) * norm_g.astype(f32)
    o = o.reshape(B, S, GDN_VW) * jax.nn.silu(gate.astype(f32))
    return o.astype(out_dtype)

def _mixer(h, w_in, b_forget, conv_w, gdn_a_log, gdn_dt_bias, gdn_norm_g, w_branch, w_o):
    f32 = jnp.float32
    B, S, _ = h.shape
    split_idx = [int(i) for i in np.cumsum(IN_SIZES)[:-1]]
    (fq, fk, fv, ff, sq, sk, sv, gqkv, gbeta, ga, ggate, bgates) = jnp.split(h @ w_in, split_idx, axis=-1)
    log_f = jax.nn.log_sigmoid(ff.astype(f32) + b_forget.astype(f32)).transpose(0, 2, 1)
    o_a = _forgetting_attention(_heads(fq, FOX_HEADS), _heads(fk, FOX_HEADS), _heads(fv, FOX_HEADS), log_f)
    o_b = _stick_breaking_attention(_heads(sq, SB_HEADS), _heads(sk, SB_HEADS), _heads(sv, SB_HEADS))
    o_c = _gdn_branch(gqkv, gbeta, ga, ggate, conv_w, gdn_a_log, gdn_dt_bias, gdn_norm_g)
    y_a = o_a @ w_branch[:FOX_W]
    y_b = o_b @ w_branch[FOX_W:FOX_W + SB_W]
    y_c = o_c @ w_branch[FOX_W + SB_W:]
    gates = jax.nn.sigmoid(bgates).reshape(B, S, N_BRANCH, D_MODEL)
    merged = gates[:, :, 0] * y_a + gates[:, :, 1] * y_b + gates[:, :, 2] * y_c
    return merged @ w_o

def _swiglu(h, w_up, w_down):
    gate, up = jnp.split(h @ w_up, 2, axis=-1)
    return (jax.nn.silu(gate) * up) @ w_down

def _modulate(x, m):
    return x * (1.0 + m[:, 1]) + m[:, 0]

def setup_inputs(seed: int = 0) -> dict:
    key = jax.random.key(seed)
    ks = jax.random.split(key, 20)
    f32 = jnp.float32

    def nrm(k, shape, s):
        return jax.random.normal(k, shape, f32) * s

    x = nrm(ks[0], (BATCH, SEQ, D_MODEL), 1.0)
    c = nrm(ks[1], (BATCH, D_MODEL), 1.0)
    w_ada = nrm(ks[2], (DEPTH, D_MODEL, N_SUBLAYERS * 3 * D_MODEL), 0.2 * D_MODEL ** -0.5)
    b_ada = nrm(ks[3], (DEPTH, N_SUBLAYERS * 3 * D_MODEL), 0.02)
    ln_g = 1.0 + nrm(ks[4], (DEPTH, N_SUBLAYERS, D_MODEL), 0.02)
    ln_b = nrm(ks[5], (DEPTH, N_SUBLAYERS, D_MODEL), 0.02)
    ffn_w_up = nrm(ks[6], (DEPTH, 2, D_MODEL, 2 * FFN_HIDDEN), D_MODEL ** -0.5)
    ffn_w_down = nrm(ks[7], (DEPTH, 2, FFN_HIDDEN, D_MODEL), DEEPNORM_BETA * FFN_HIDDEN ** -0.5)
    w_in = nrm(ks[8], (DEPTH, D_MODEL, IN_COLS), D_MODEL ** -0.5)
    b_forget = jax.random.uniform(ks[9], (DEPTH, FOX_HEADS), f32, 1.0, 5.0)
    conv_w = nrm(ks[10], (DEPTH, CONV_WIDTH, 2 * GDN_KW + GDN_VW), CONV_WIDTH ** -0.5)
    gdn_a_log = jnp.log(jax.random.uniform(ks[11], (DEPTH, GDN_HEADS), f32, 1.0, 16.0))
    dt = jnp.exp(jax.random.uniform(ks[12], (DEPTH, GDN_HEADS), f32, math.log(1e-3), math.log(1e-1)))
    gdn_dt_bias = dt + jnp.log(-jnp.expm1(-dt))
    gdn_norm_g = 1.0 + nrm(ks[13], (DEPTH, GDN_VAL_DIM), 0.02)
    w_branch = jnp.concatenate([nrm(ks[14], (DEPTH, FOX_W, D_MODEL), FOX_W ** -0.5),
                                nrm(ks[15], (DEPTH, SB_W, D_MODEL), SB_W ** -0.5),
                                nrm(ks[16], (DEPTH, GDN_VW, D_MODEL), GDN_VW ** -0.5)], axis=1)
    w_o = nrm(ks[17], (DEPTH, D_MODEL, D_MODEL), DEEPNORM_BETA * D_MODEL ** -0.5)
    return {'x': x, 'c': c, 'w_ada': w_ada, 'b_ada': b_ada, 'ln_g': ln_g, 'ln_b': ln_b,
            'ffn_w_up': ffn_w_up, 'ffn_w_down': ffn_w_down, 'w_in': w_in, 'b_forget': b_forget,
            'conv_w': conv_w, 'gdn_a_log': gdn_a_log, 'gdn_dt_bias': gdn_dt_bias,
            'gdn_norm_g': gdn_norm_g, 'w_branch': w_branch, 'w_o': w_o}

def reference(x, c, w_ada, b_ada, ln_g, ln_b, ffn_w_up, ffn_w_down, w_in, b_forget, conv_w,
              gdn_a_log, gdn_dt_bias, gdn_norm_g, w_branch, w_o):
    B = x.shape[0]
    sc = jax.nn.silu(c)
    for l in range(DEPTH):
        mod = (sc @ w_ada[l] + b_ada[l]).reshape(B, N_SUBLAYERS, 3, D_MODEL)[:, :, :, None, :]
        m = mod[:, 0]
        y = _swiglu(_modulate(x, m), ffn_w_up[l, 0], ffn_w_down[l, 0])
        x = _layer_norm(DEEPNORM_ALPHA * x + 0.5 * (1.0 + m[:, 2]) * y, ln_g[l, 0], ln_b[l, 0])
        m = mod[:, 1]
        y = _mixer(_modulate(x, m), w_in[l], b_forget[l], conv_w[l], gdn_a_log[l], gdn_dt_bias[l],
                   gdn_norm_g[l], w_branch[l], w_o[l])
        x = _layer_norm(DEEPNORM_ALPHA * x + (1.0 + m[:, 2]) * y, ln_g[l, 1], ln_b[l, 1])
        m = mod[:, 2]
        y = _swiglu(_modulate(x, m), ffn_w_up[l, 1], ffn_w_down[l, 1])
        x = _layer_norm(DEEPNORM_ALPHA * x + 0.5 * (1.0 + m[:, 2]) * y, ln_g[l, 2], ln_b[l, 2])
    return x


_drawn_inputs = setup_inputs


def setup_inputs(seed=0):
    import zlib

    import numpy as np

    out = dict(_drawn_inputs(seed))
    spreads = {}
    factors = {'b_ada': 3.203, 'gdn_norm_g': 8.0}
    for name, (base, spread) in spreads.items():
        noise = np.random.default_rng([zlib.crc32(name.encode()), seed]).standard_normal(out[name].shape)
        drawn = base * np.exp(spread * noise) if base else spread * noise
        out[name] = __import__('jax').numpy.asarray(drawn.astype(out[name].dtype))
    for name, factor in factors.items():
        out[name] = (out[name] * factor).astype(out[name].dtype)
    return out
```

```python
import math
from contextlib import ExitStack

import concourse.bass as bass
from concourse import mybir

F32 = mybir.dt.float32
F32R = mybir.dt.float32r
ALU = mybir.AluOpType
ACT = mybir.ActivationFunctionType
AX = mybir.AxisListType
ds = bass.ds

P = 128
BIG = 1.0e30
LN_EPS = 1e-5
RMS_EPS = 1e-6

PER = {
    "acc_row": 48, "raw_in0": 1632, "raw_in1": 1632, "raw_in2": 1152, "ln_rows": 96, "prm_in": 64,
    "acc_zero": 3, "x_affine": 6, "ln_rstd": 6, "x_gain": 6, "o_rs": 2, "h_f32": 6, "w_hi": 102, "up_silu": 44,
    "act_hi": 22, "mix_ev": 14, "conv_silu": 3, "ssq_ln": 1, "ssq_exp": 1, "sp_exp": 1, "sp_ln": 1, "ea": 1,
    "beta_e": 1, "fox_exp": 2, "fox_pt": 2, "o_ab": 2, "sb_e": 1, "sb_l": 1, "sb_w": 1, "kv": 2, "egc": 1,
    "g_exp": 4, "dec": 1, "at": 2, "m1": 12, "state": 1, "o_hi": 2, "gates": 1, "o_ss": 2, "o_c": 1, "m_hi": 2,
    "mod_mm": 3, "w_used": 102, "ln_xt": 6, "gate_mm": 3, "up_mm": 22, "act_T": 22, "y_mm": 3, "ssq_mm": 1,
    "rows_mm": 1, "fox_mm": 2, "foxp_T": 1, "fox_pv": 1, "sb_mm": 2, "sb_cum": 1, "sb_pv": 1, "kv_T": 1,
    "gram_mm": 2, "at_T": 2, "m1_mm": 12, "m2_mm": 12, "vnew_mm": 2, "state_mm": 1, "o0_mm": 1, "yb_mm": 9,
    "zq_mm": 1, "o1_mm": 1, "o_T": 1, "merged_T": 2, "act_lo": 22, "fold": 252, "ada_done": 36, "w_lo": 102,
    "mod_cols": 3, "h_hi": 6, "h_lo": 6, "gate_bc": 3, "act": 44, "mod_a": 6, "ln_gy": 6, "ln_sum": 6,
    "ln_bn": 12, "ln_mv": 6, "ln_var": 6, "ln_x": 6, "convw": 1, "pad": 1, "conv": 12, "cv_sq": 2, "qk_norm": 2,
    "sp_arg": 4, "sp_abs": 1, "sp": 1, "lg": 4, "beta1": 1, "beta": 1, "lgu1": 4, "lgu": 4, "ccol": 1,
    "dec_arg": 1, "fox_b": 2, "fox_s": 2, "fox_max": 2, "fox_neg": 2, "fox_rec": 2, "fox_p": 2, "sb_z": 2,
    "sb_abs": 1, "sb_sp": 1, "sb_arg": 1, "g_gu": 2, "g_diff": 4, "g_em": 4, "g_a": 2, "g_mats": 2, "x_tmp": 4,
    "x_set": 2, "inv_x": 14, "ats": 12, "inv_m": 10, "bv": 1, "vnew": 3, "o_raw": 2, "o_lo": 2, "z_v": 1,
    "beta_n": 1, "rhs1": 1, "q_s": 1, "y_ev": 12, "o_ms": 2, "o_n": 2, "o_gated": 2, "merged1": 4, "merged": 4,
    "m_lo": 2,
}
OFF = {
    "rows_in": 64, "acc_row": 16, "raw_in0": 128, "raw_in1": 128, "raw_in2": 128, "x_in": 16, "acc_zero": 1,
    "x_affine": 1, "sc_ready": 1, "h_f32": 2, "cols_T": 1, "mod_mm": 1, "w_used": 2, "ln_xt": 2, "cols": 1,
    "act_lo": 1, "fold": 84, "ada_done": 12, "w_lo": 2, "mod_cols": 1, "h_hi": 2, "h_lo": 2,
}


def trunk(nc, x_in, c_in, w_ada, b_ada, ln_g, ln_b, w_up, w_down, w_in, b_forget, conv_w,
          a_log, dt_bias, norm_g, w_branch, w_o, out):
    _, SEQ, D = x_in.shape
    DEPTH = w_in.shape[0]
    HID = w_down.shape[2]
    TAPS = conv_w.shape[1]
    NT = SEQ // P
    KD = D // P
    KH = HID // P
    CW = 256
    NCH = HID // CW
    HEADS = 4
    DH = 64
    FOX_W = SB_W = HEADS * DH
    GW = HEADS * P
    SCALE = DH ** -0.5
    ALPHA = (2.0 * DEPTH) ** 0.25
    assert NT == 2 and KD == 8 and NCH * CW == HID and TAPS == 4

    C_FQ, C_FK, C_FV = 0, FOX_W, 2 * FOX_W
    C_FF = 3 * FOX_W
    C_SQ = C_FF + HEADS
    C_SK, C_SV = C_SQ + SB_W, C_SQ + 2 * SB_W
    C_GQ = C_SQ + 3 * SB_W
    C_GB = C_GQ + 3 * GW
    C_GG = C_GB + 2 * HEADS
    C_BG = C_GG + GW

    UP_U, DOWN_U = 2 * NCH, NCH
    FFN_U = UP_U + DOWN_U
    MIX_CH = 14
    BR0 = 2 * MIX_CH
    MIX_U = BR0 + 8
    U_A, U_M, U_B = 0, FFN_U, FFN_U + MIX_U
    UNITS = 2 * FFN_U + MIX_U
    assert UNITS % 2 == 0
    ADA_N = 12
    ADA_C = 3 * D // ADA_N
    PRO = ADA_N // 3

    ctx = ExitStack()
    with ctx:
        def sb(name, shape, dt=F32, where=None):
            return (where or ctx).enter_context(nc.sbuf_tensor(name, shape, dt))

        raw = sb("raw", [P, 3, 2048])
        whi = sb("whi", [P, 2, 2048], F32R)
        wlo = sb("wlo", [P, 2, 2048], F32R)
        hhi = sb("hhi", [P, KD, SEQ], F32R)
        hlo = sb("hlo", [P, KD, SEQ], F32R)
        x = sb("x", [P, NT, D])
        lnw = sb("lnw", [P, NT, D])
        acc = sb("acc", [P, 3 * D])
        gatebc = sb("gatebc", [P, D])
        lnbc = sb("lnbc", [P, 2, D])
        ident = sb("ident", [P, P])
        tri1 = sb("tri1", [P, 2, P])
        trid = sb("trid", [P, P])
        foxm = sb("foxm", [P, 2, P])
        sbm = sb("sbm", [P, 2, P])
        strict = sb("strict", [P, P])
        incl_t = sb("incl_t", [P, P])
        lev_t = sb("lev_t", [P, 7, P])
        lev1 = sb("lev1", [P, P])
        cols = sb("cols", [P, 192])
        sc = sb("sc", [P, KD])
        modab = sb("modab", [P, 2, KD])
        modt = sb("modt", [P, KD])
        stats = sb("stats", [P, NT, 2, 6])
        mv = sb("mv", [P, NT, 2])
        var = sb("var", [P, NT])
        rstd = sb("rstd", [P, NT])
        mhalf = sb("mhalf", [P, 8])
        epsc = sb("epsc", [P, 1])
        prm = sb("prm", [P, 12])
        nrmg = sb("nrmg", [P, P])

        with ExitStack() as ffn_mem:
            athi = sb("athi", [P, KH, SEQ], F32R, ffn_mem)
            atlo = sb("atlo", [P, KH, SEQ], F32R, ffn_mem)
            sg = sb("sg", [P, NT, CW], F32, ffn_mem)
            act_t = sb("act_t", [P, NT, CW], F32, ffn_mem)
        gates = sb("gates", [P, NT, 3 * D])
        cv = sb("cv", [P, 12, SEQ])
        att = sb("att", [P, 6, 512])
        ggs = sb("ggs", [P, NT, 512])
        kn = sb("kn", [P, HEADS, P])
        vn = sb("vn", [P, NT, HEADS, P])
        ot = sb("ot", [P, KD, SEQ])
        scr = sb("scr", [P, 4096])
        sm = sb("sm", [P, NT, 12])
        sp_a = sb("sp_a", [P, NT, 8])
        sp_b = sb("sp_b", [P, NT, 8])
        sp_c = sb("sp_c", [P, NT, 8])
        lg = sb("lg", [P, NT, 8])
        ea = sb("ea", [P, HEADS])
        beta = sb("beta", [P, NT, HEADS])
        beta_t = sb("beta_t", [P, NT, HEADS])
        ccol = sb("ccol", [P, 4, HEADS])
        fmax = sb("fmax", [P, 8])
        fneg = sb("fneg", [P, 8])
        fsum = sb("fsum", [P, 8])
        frec = sb("frec", [P, 8])
        egc = sb("egc", [P, HEADS])
        dec = sb("dec", [P, HEADS])
        dtmp = sb("dtmp", [P, HEADS])
        oss = sb("oss", [P, 8])
        ors = sb("ors", [P, 8])
        convw = sb("convw", [P, TAPS * 12])

        pg = ctx.enter_context(nc.psum_tensor("pg", [P, 4, 512], F32))
        pt = ctx.enter_context(nc.psum_tensor("pt", [P, 4, 512], F32))

        qkt = att[:, 0:4, :].rearrange("p a (b s) -> p a b s", b=2)
        val = att[:, 4:6, :]
        ones = tri1[:, 1, :]
        tri = tri1[:, 0, :]
        merged = cv[:, 0:8, :].rearrange("p (t a) s -> p t (a s)", t=NT)

        S = {name: ctx.enter_context(nc.semaphore("s_" + name)) for name in
             [*sorted(PER | OFF), "fills", "masks", "masks_done", "out"]}

        def counter(l):
            def at(name, k=1):
                return k if l is None else l * PER.get(name, 0) + (OFF.get(name, 0) + k)
            return at

        def alone(eng, name, value):
            value = eng.snap(eng.to_reg(value))
            eng.wait_ge(S[name], 0)
            return value

        block = ctx.enter_context(nc.Block())

        @block.sync
        def _(sp):

            def pair(dst, src, name):
                for d, s in zip(dst, src):
                    sp.dma_start(d, s).then_inc(S[name], 16)

            sp.dma_start(lnw[0:8, 0, 384:512], c_in.rearrange("b (k p) -> (b k) p", p=P)).then_inc(S["rows_in"], 16)
            sp.dma_start(lnw[0:48, 0, 0:128], ln_g.rearrange("l s (k p) -> (l s k) p", p=P)).then_inc(S["rows_in"], 16)
            sp.dma_start(lnw[0:48, 0, 128:256], ln_b.rearrange("l s (k p) -> (l s k) p", p=P)).then_inc(S["rows_in"], 16)
            sp.dma_start(lnw[0:96, 0, 256:384], conv_w.rearrange("l t (c p) -> (l t c) p", p=P)).then_inc(S["rows_in"], 16)
            sp.wait_ge(S["acc_zero"], 1)
            sp.dma_start(acc[0:1, :], b_ada[0:1, 0:3 * D]).then_inc(S["acc_row"], 16)

            def ada_dst(slot):
                r = raw[:, slot, :].rearrange("p (k c) -> p k c", k=KD)
                return [r[:, 0:4, :], r[:, 4:8, :]]

            for i in range(ADA_N):
                slot, n = i % 3, i // 3
                if n:
                    sp.wait_ge(S["ada_done"], i - 2)
                w = w_ada[0, :, i * ADA_C:(i + 1) * ADA_C].rearrange("(k p) c -> p k c", p=P)
                pair(ada_dst(slot), [w[:, 0:4, :], w[:, 4:8, :]], f"raw_in{slot}")
                if i == 2:
                    sp.dma_start(x[:, :, :], x_in[0].rearrange("(t p) d -> p t d", p=P)).then_inc(S["x_in"], 16)

            sp.wait_ge(S["ada_done"], ADA_N - 1)
            with sp.Fori(0, DEPTH) as l:
                at = counter(l)

                def w_view(slot, k):
                    return raw[:, slot, :].rearrange("p (k c) -> p k c", k=k)

                def free(u):
                    sp.wait_ge(S["w_lo"], alone(sp, "w_lo", at("w_lo", u - 1)))

                def rows(w, u, r0):
                    free(u)
                    d = w_view(u % 2, 2)
                    pair([d[:, 0, :], d[:, 1, :]],
                         [w[ds(l, 1), r0 + k * P:r0 + (k + 1) * P, :].rearrange("a p c -> (a p) c") for k in (0, 1)],
                         f"raw_in{u % 2}")

                def ada(idx, nl, s, j):
                    sp.wait_ge(S["ada_done"], alone(sp, "ada_done", at("ada_done", idx)))
                    w = w_ada[ds(nl, 1), :, ds(s * 3 * D + j * ADA_C, ADA_C)].rearrange("a (k p) c -> p (a k) c", p=P)
                    pair(ada_dst(2), [w[:, 0:4, :], w[:, 4:8, :]], "raw_in2")

                def acc_row(k, nl, s):
                    sp.wait_ge(S["acc_zero"], alone(sp, "acc_zero", at("acc_zero", k)))
                    sp.dma_start(acc[0:1, :], b_ada[ds(nl, 1), s * 3 * D:(s + 1) * 3 * D]).then_inc(S["acc_row"], 16)

                def ln_rows(k, s):
                    sp.wait_ge(S["x_affine"], alone(sp, "x_affine", at("x_affine", 2 * k)))
                    for n, src in enumerate((ln_g, ln_b)):
                        sp.dma_start(lnbc[:, n, :], src[ds(l, 1), s, :].broadcast_to((P, D))).then_inc(S["ln_rows"], 16)

                def up_unit(f, u, j, ui):
                    d = w_view(u % 2, 4)
                    src = []
                    for half in (0, 1):
                        w = w_up[ds(l, 1), f, ui * 512:(ui + 1) * 512, ds(half * HID + j * CW, CW)]
                        src.append(w.rearrange("a (k p) c -> p (a k) c", p=P))
                    pair([d[:, :, 0:CW], d[:, :, CW:2 * CW]], src, f"raw_in{u % 2}")

                def ffn(f, s, u0, a0, nl, ns):
                    for ui in (0, 1):
                        free(u0 + ui)
                        up_unit(f, u0 + ui, 0, ui)
                    acc_row(s + 1, nl, ns)
                    ln_rows(s, s)
                    with sp.Fori(1, NCH) as j:
                        for ui in (0, 1):
                            u = u0 + ui
                            sp.wait_ge(S["w_lo"], alone(sp, "w_lo", l * PER["w_lo"] + j * 2 + (OFF["w_lo"] + u - 1)))
                            up_unit(f, u, j, ui)
                        sp.wait_ge(S["ada_done"], alone(sp, "ada_done", l * PER["ada_done"] + j + (OFF["ada_done"] + a0 - 1)))
                        w = w_ada[ds(nl, 1), :, ds(ns * 3 * D - ADA_C + j * ADA_C, ADA_C)].rearrange(
                            "a (k p) c -> p (a k) c", p=P)
                        pair(ada_dst(2), [w[:, 0:4, :], w[:, 4:8, :]], "raw_in2")
                    for d in range(DOWN_U):
                        rows(w_down[:, f], u0 + UP_U + d, d * 2 * P)
                        if d in (0, 3):
                            k = NCH - 1 + (d == 3)
                            ada(a0 + k, nl, ns, k)

                def two(u, w, c0, c1):
                    free(u)
                    d = w_view(u % 2, 4)
                    r = w.rearrange("a (k p) c -> p (a k) c", p=P)
                    pair([d[:, :, 0:256], d[:, :, 256:512]], [r[:, :, c0:c0 + 256], r[:, :, c1:c1 + 256]],
                         f"raw_in{u % 2}")

                def mixer():
                    sp.dma_start(prm[:, 0:4], b_forget[ds(l, 1), :].broadcast_to((P, HEADS))).then_inc(S["prm_in"], 16)
                    sp.dma_start(prm[:, 4:8], dt_bias[ds(l, 1), :].broadcast_to((P, HEADS))).then_inc(S["prm_in"], 16)
                    sp.dma_start(prm[:, 8:12], a_log[ds(l, 1), :].broadcast_to((P, HEADS))).then_inc(S["prm_in"], 16)
                    sp.dma_start(nrmg[:, :], norm_g[ds(l, 1), :].broadcast_to((P, P))).then_inc(S["prm_in"], 16)
                    starts = [(C_GQ, C_GQ + 256), (C_GQ + GW, C_GQ + GW + 256), (C_GQ + 2 * GW, C_GQ + 2 * GW + 256),
                              (C_GG, C_GG + 256), None, (C_FQ, C_FK), (C_FV, C_SV), (C_SQ, C_SK)]
                    starts += [(C_BG + 512 * g, C_BG + 512 * g + 256) for g in range(6)]
                    n_ada = 0
                    for i in range(MIX_U):
                        u = U_M + i
                        if i < BR0:
                            w = w_in[ds(l, 1), (i % 2) * 512:(i % 2 + 1) * 512, :]
                            if starts[i // 2]:
                                two(u, w, *starts[i // 2])
                            else:
                                free(u)
                                d = raw[:, u % 2, 0:48].rearrange("p (k c) -> p k c", k=4)
                                r = w.rearrange("a (k p) c -> p (a k) c", p=P)
                                pair([d[:, :, 0:4], d[:, :, 4:12]],
                                     [r[:, :, C_FF:C_FF + HEADS], r[:, :, C_GB:C_GB + 2 * HEADS]], f"raw_in{u % 2}")
                        elif i < BR0 + 4:
                            rows(w_branch, u, (i - BR0) * 2 * P)
                        else:
                            rows(w_o, u, (i - BR0 - 4) * 2 * P)
                        if i == 1:
                            acc_row(2, l, 2)
                            ln_rows(1, 1)
                        if i >= 2 and i % 2 == 0 and n_ada < ADA_N:
                            ada(ADA_N + n_ada, l, 2, n_ada)
                            n_ada += 1

                ffn(0, 0, U_A, 0, l, 1)
                mixer()
                ffn(1, 2, U_B, 2 * ADA_N, 1 - l, 0)

            at = counter(None)
            sp.wait_ge(S["x_affine"], OFF["x_affine"] + DEPTH * PER["x_affine"])
            sp.dma_start(out[0].rearrange("(t p) d -> p t d", p=P), x[:, :, :]).then_inc(S["out"], 16)
            sp.wait_ge(S["out"], 16)

        @block.gpsimd
        def _(pool):
            pool.memset(acc[:, :], 0.0).then_inc(S["acc_zero"], 1)
            pool.memset(mhalf[:, :], -0.5).then_inc(S["fills"], 1)
            pool.memset(epsc[:, :], 0.0).then_inc(S["x_affine"], 1)
            pool.wait_ge(S["x_affine"], 1)
            for t, v in ((ident[:, :], 0.0), (tri1[:, :, :], 1.0), (trid[:, :], 1.0), (foxm[:, :, :], 0.0),
                         (sbm[:, :, :], 0.0), (strict[:, :], 1.0), (incl_t[:, :], 1.0), (lev_t[:, :, :], 0.0),
                         (lev1[:, :], 0.0)):
                pool.memset(t, v).then_inc(S["fills"], 1)
            pool.wait_ge(S["fills"], 10)

            def sel(ap, op, fill, base, pattern, cm):
                return pool.affine_select(out=ap, in_=ap, pattern=pattern, compare_op=op, fill=fill, base=base,
                                          channel_multiplier=cm).then_inc(S["masks"], 1)
            sel(ident[:, :], ALU.not_equal, 1.0, 0, [[-1, P]], 1)
            sel(tri, ALU.is_ge, 0.0, 0, [[1, P]], -1)
            sel(trid[:, :], ALU.is_ge, 0.0, 0, [[-1, P]], 1)
            sel(foxm[:, 1, :], ALU.is_ge, BIG, 0, [[-1, P]], 1)
            sel(sbm[:, 0, :], ALU.is_gt, -BIG, 0, [[1, P]], -1)
            sel(strict[:, :], ALU.is_gt, 0.0, 0, [[-1, P]], 1)
            sel(incl_t[:, :], ALU.is_ge, 0.0, 0, [[1, P]], -1)
            n = 7
            for lv in range(7):
                s = 1 << lv
                v = lev_t[:, lv, :].rearrange("p (b u r) -> p b u r", u=2, r=s)[:, :, 1, :]
                pool.memset(v, 1.0).then_inc(S["fills"], 1)
            v1 = lev1[:, :].rearrange("p (b u) -> p b u", u=2)[:, :, 0]
            pool.memset(v1, 1.0).then_inc(S["fills"], 1)
            pool.wait_ge(S["fills"], 18)
            for lv in range(7):
                s = 1 << lv
                nb = P // (2 * s)
                v = lev_t[:, lv, :].rearrange("p (b u r) -> p b u r", u=2, r=s)[:, :, 1, :]
                sel(v, ALU.is_ge, 0.0, 0, [[-2 * s, nb], [0, s]], 1)
                n += 1
                pool.wait_ge(S["masks"], n)
                sel(v, ALU.is_ge, 0.0, s - 1, [[2 * s, nb], [0, s]], -1)
                n += 1
            sel(v1, ALU.is_equal, 0.0, -1, [[-2, P // 2]], 1)
            n += 1
            pool.wait_ge(S["masks"], n)
            pool.memset(epsc[:, :], RMS_EPS).then_inc(S["masks_done"], 1)

            with pool.Fori(0, DEPTH) as l:
                at = counter(l)

                def norm_rest(s):
                    for t in range(NT):
                        pool.wait_ge(S["ln_var"], alone(pool, "ln_var", at("ln_var", NT * s + t + 1)))
                        pool.tensor_tensor(rstd[:, t:t + 1], var[:, t:t + 1], mhalf[:, 0:1], ALU.pow).then_inc(S["ln_rstd"], 1)
                    for t in range(NT):
                        pool.wait_ge(S["ln_xt"], alone(pool, "ln_xt", at("ln_xt", NT * s + t + 1)))
                        pool.wait_ge(S["ln_rows"], alone(pool, "ln_rows", at("ln_rows", 32 * (s + 1))))
                        pool.tensor_tensor(x[:, t, :], x[:, t, :], lnbc[:, 0, :], ALU.mult).then_inc(S["x_gain"], 1)
                        pool.wait_ge(S["x_gain"], alone(pool, "x_gain", at("x_gain", NT * s + t + 1)))
                        pool.tensor_tensor(x[:, t, :], x[:, t, :], lnbc[:, 1, :], ALU.add).then_inc(S["x_affine"], 1)

                def clear(s):
                    pool.wait_ge(S["gate_mm"], alone(pool, "gate_mm", at("gate_mm", s + 1)))
                    pool.memset(acc[:, :], 0.0).then_inc(S["acc_zero"], 1)

                clear(0)
                norm_rest(0)
                clear(1)
                for t in range(NT):
                    pool.wait_ge(S["o_ms"], alone(pool, "o_ms", at("o_ms", t + 1)))
                    pool.tensor_tensor(ors[:, 4 * t:4 * t + 4], oss[:, 4 * t:4 * t + 4], mhalf[:, 0:4], ALU.pow).then_inc(S["o_rs"], 1)
                norm_rest(1)
                clear(2)
                norm_rest(2)

        GD = {"x": 0, "xt": 1, "at": 2, "ats": 3, "m": 4, "it": 5}

        def gd(t, name):
            k = GD[name]
            return att[:, k, :] if t == 0 else scr[:, k * 512:(k + 1) * 512]

        TASKS = {
            (2, 1): ["silu0"], (4, 1): ["silu1"], (6, 1): ["silu2"],
            (8, 0): ["l2norm"], (10, 0): ["params"], (11, 0): ["rows"],
            (12, 1): ["fox_p"], (13, 1): ["fox_T"], (14, 1): ["fox_o"],
            (16, 0): ["sb_z"], (17, 0): ["sb_r"], (18, 0): ["sb_o", "kv"],
            (19, 0): ["dec0"], (19, 1): ["dec1"], (20, 0): ["inv0"],
            (26, 1): ["f1"], (27, 0): ["f2"], (27, 1): ["o_split", "sig"],
            (28, 0): ["f3"], (28, 1): ["f4"], (29, 0): ["f5"], (29, 1): ["oT", "c_split"], (31, 1): ["mrg"],
        }
        slot = (20, 1)
        for lv in range(1, 7):
            for half in ("ma", "mb"):
                TASKS.setdefault(slot, []).append(f"{half}{lv}")
                slot = (slot[0], 1) if slot[1] == 0 else (slot[0] + 1, 0)
        assert slot <= (26, 1), slot

        @block.scalar
        def _(act):
            act.wait_ge(S["cols_T"], 1)
            act.activation(sc[:, :], pt[:, 0, 192:200], ACT.Silu).then_inc(S["sc_ready"], 1)

            def modulate(at, k, t):
                act.wait_ge(S["mod_cols"], at("mod_cols", k + 1))
                act.wait_ge(S["ln_xt"], at("ln_xt", NT * k + t + 1))
                for c in range(KD):
                    ins = act.activation(lnw[:, t, c * P:(c + 1) * P],
                                         pt[:, 2 * t + c // 4, (c % 4) * P:(c % 4 + 1) * P],
                                         ACT.Identity, bias=modab[:, 1, c:c + 1], scale=modab[:, 0, c:c + 1])
                ins.then_inc(S["h_f32"], 1)

            w0 = counter(None)
            for t in range(NT):
                modulate(w0, 0, t)

            with act.Fori(0, DEPTH) as l:
                at = counter(l)

                def split(u, size=2048):
                    s = u % 2
                    act.wait_ge(S[f"raw_in{s}"], at(f"raw_in{s}", 32 * (u // 2 + 1)))
                    act.wait_ge(S["w_used"], at("w_used", u - 1))
                    act.activation(whi[:, s, 0:size], raw[:, s, 0:size], ACT.Copy).then_inc(S["w_hi"], 1)

                def split_j(u, j):
                    s = u % 2
                    act.wait_ge(S[f"raw_in{s}"], l * PER[f"raw_in{s}"] + j * 32
                                + (OFF.get(f"raw_in{s}", 0) + 32 * (u // 2 + 1)))
                    act.wait_ge(S["w_used"], l * PER["w_used"] + j * 2 + (OFF["w_used"] + u - 1))
                    act.activation(whi[:, s, :], raw[:, s, :], ACT.Copy).then_inc(S["w_hi"], 1)

                def silu(f, u0, t, j, dyn=None):
                    name, step, k = (("up_mm", 1, f * NCH + j + 1), ("w_used", 2, u0 + 2 * j + 2))[t]
                    if dyn is None:
                        act.wait_ge(S[name], at(name, k))
                    else:
                        act.wait_ge(S[name], l * PER.get(name, 0) + dyn * step + (OFF.get(name, 0) + k))
                    act.activation(sg[:, t, :], pg[:, t, 0:CW], ACT.Silu).then_inc(S["up_silu"], 1)

                def ffn(f, s, u0, first):
                    if first:
                        split(u0)
                        split(u0 + 1)
                    split(u0 + 2)
                    silu(f, u0, 0, 0)
                    silu(f, u0, 1, 0)
                    with act.Fori(1, NCH - 1) as j:
                        chunk_j(f, u0, j)
                        split_j(u0 + 2, j)
                        silu(f, u0, 0, 0, j)
                        silu(f, u0, 1, 0, j)
                    split(u0 + 2 * NCH - 1)
                    act_hi(f, NCH - 1)
                    split(u0 + 2 * NCH)
                    silu(f, u0, 0, NCH - 1)
                    silu(f, u0, 1, NCH - 1)
                    for d in range(DOWN_U):
                        u = u0 + UP_U + d
                        if d == 1:
                            act_hi(f, NCH)
                        if d < DOWN_U - 1 or s == 0:
                            split(u + 1)
                    norm_stage(s, u0 + FFN_U)

                def chunk_j(f, u0, j):
                    split_j(u0 + 1, j)
                    act.wait_ge(S["act_T"], alone(act, "act_T", l * PER["act_T"] + j + (f * NCH)))
                    act.activation(athi[:, ds(j * 2 - 2, 2), :],
                                   pt[:, 0, :].rearrange("p (k s) -> p k s", k=2), ACT.Copy).then_inc(S["act_hi"], 1)

                def act_hi(f, j):
                    act.wait_ge(S["act_T"], at("act_T", f * NCH + j))
                    act.activation(athi[:, 2 * j - 2:2 * j, :],
                                   pt[:, 0, :].rearrange("p (k s) -> p k s", k=2), ACT.Copy).then_inc(S["act_hi"], 1)

                def norm_stage(s, u_next):
                    if u_next < UNITS:
                        split(u_next + 1)
                    for t in range(NT):
                        modulate(at, s, t)

                def g_row(a):
                    return a.rearrange("p (h s) -> p h s", h=HEADS)

                def evac(k):
                    b = 2 * (k % 2)
                    act.wait_ge(S["w_used"], at("w_used", U_M + 2 * k + 2))
                    two = pg[:, b:b + 2, :]
                    if k < 3:
                        if k:
                            act.wait_ge(S["conv"], at("conv", 4 * k))
                        act.wait_ge(S["pad"], at("pad", 1))
                        pre = scr[:, 0:4 * 260].rearrange("p (c s) -> p c s", c=4)
                        ins = act.activation(pre[:, :, 4:260], two.rearrange("p b (c s) -> p (b c) s", c=2), ACT.Copy)
                    elif k == 3:
                        ins = act.activation(ggs[:, :, :], two, ACT.Silu)
                    elif k == 4:
                        ins = act.activation(sm[:, :, :], pg[:, b:b + 2, 0:12], ACT.Copy)
                    elif k == 6:
                        ins = act.activation(val, two, ACT.Copy)
                    elif k in (5, 7):
                        a = 0 if k == 5 else 2
                        ins = act.activation(att[:, a:a + 2, :], two, ACT.Copy)
                    else:
                        ins = act.activation(gates[:, :, (k - 8) * 512:(k - 7) * 512], two, ACT.Copy)
                    ins.then_inc(S["mix_ev"], 1)

                def conv_silu(k):
                    act.wait_ge(S["conv"], at("conv", 4 * k + 4))
                    act.activation(cv[:, 4 * k:4 * k + 4, :],
                                   scr[:, 1040:2064].rearrange("p (c s) -> p c s", c=4), ACT.Silu).then_inc(S["conv_silu"], 1)

                def l2norm():
                    act.wait_ge(S["ssq_mm"], at("ssq_mm", 1))
                    act.activation(scr[:, 2048:4096], pt[:, :, :].rearrange("p b s -> p (b s)"), ACT.Ln,
                                   bias=epsc[:, 0:1]).then_inc(S["ssq_ln"], 1)
                    act.wait_ge(S["ssq_ln"], at("ssq_ln", 1))
                    act.activation(scr[:, 2048:4096], scr[:, 2048:4096], ACT.Exp, scale=-0.5).then_inc(S["ssq_exp"], 1)

                def params():
                    act.wait_ge(S["sp_abs"], at("sp_abs", 1))
                    act.activation(sp_b[:, :, :], sp_b[:, :, :], ACT.Exp, scale=-1.0).then_inc(S["sp_exp"], 1)
                    act.wait_ge(S["sp_exp"], at("sp_exp", 1))
                    act.activation(sp_b[:, :, :], sp_b[:, :, :], ACT.Ln, bias=1.0).then_inc(S["sp_ln"], 1)
                    act.wait_ge(S["prm_in"], at("prm_in", 64))
                    act.activation(ea[:, :], prm[:, 8:12], ACT.Exp).then_inc(S["ea"], 1)
                    act.activation(beta_t[:, :, :], sm[:, :, 4:8], ACT.Exp, scale=-1.0).then_inc(S["beta_e"], 1)

                def fox_exp():
                    for t in range(NT):
                        n = P * (t + 1)
                        act.wait_ge(S["fox_neg"], at("fox_neg", t + 1))
                        for h in range(HEADS):
                            a = fox_s(t)[:, h, :]
                            ins = act.activation(a, a, ACT.Exp, bias=fneg[:, 4 * t + h:4 * t + h + 1],
                                                 accum_out=fsum[:, 4 * t + h:4 * t + h + 1])
                        ins.then_inc(S["fox_exp"], 1)

                def fox_pt():
                    act.wait_ge(S["foxp_T"], at("foxp_T", 1))
                    act.activation(scr[:, 1536:2560], pt[:, 0:2, :].rearrange("p b s -> p (b s)"), ACT.Copy).then_inc(S["fox_pt"], 1)
                    act.activation(scr[:, 2560:3072], pt[:, 2, :], ACT.Copy).then_inc(S["fox_pt"], 1)

                def fox_o():
                    act.wait_ge(S["fox_pv"], at("fox_pv", 1))
                    act.activation(ot[:, 0:2, :], pt[:, 3, :].rearrange("p (k s) -> p k s", k=2), ACT.Copy).then_inc(S["o_ab"], 1)

                def sb_ln():
                    act.wait_ge(S["sb_abs"], at("sb_abs", 1))
                    act.activation(scr[:, 1536:3072], scr[:, 1536:3072], ACT.Exp, scale=-1.0).then_inc(S["sb_e"], 1)
                    act.wait_ge(S["sb_e"], at("sb_e", 1))
                    act.activation(scr[:, 1536:3072], scr[:, 1536:3072], ACT.Ln, bias=1.0).then_inc(S["sb_l"], 1)

                def sb_w():
                    act.wait_ge(S["sb_arg"], at("sb_arg", 1))
                    act.activation(scr[:, 0:1536], scr[:, 0:1536], ACT.Exp).then_inc(S["sb_w"], 1)

                def sb_o():
                    act.wait_ge(S["sb_pv"], at("sb_pv", 1))
                    act.activation(ot[:, 2:4, :], pt[:, 3, :].rearrange("p (k s) -> p k s", k=2), ACT.Copy).then_inc(S["o_ab"], 1)

                def kv():
                    act.wait_ge(S["kv_T"], at("kv_T", 1))
                    act.activation(kn[:, :, :], g_row(pt[:, 0, :]), ACT.Copy).then_inc(S["kv"], 1)
                    act.activation(vn[:, :, :, :].rearrange("p t h s -> p (t h s)"),
                                   pt[:, 1:3, :].rearrange("p b s -> p (b s)"), ACT.Copy).then_inc(S["kv"], 1)
                    act.wait_ge(S["ccol"], at("ccol", 1))
                    act.activation(egc[:, :], ccol[:, 3, :], ACT.Exp).then_inc(S["egc"], 1)

                def decays(t):
                    act.wait_ge(S["g_diff"], at("g_diff", 2 * t + 1))
                    act.activation(gd(t, "ats"), gd(t, "ats"), ACT.Exp, scale=-1.0).then_inc(S["g_exp"], 1)
                    act.wait_ge(S["g_diff"], at("g_diff", 2 * t + 2))
                    act.activation(gd(t, "it"), gd(t, "it"), ACT.Exp).then_inc(S["g_exp"], 1)
                    if t == 0:
                        act.wait_ge(S["dec_arg"], at("dec_arg", 1))
                        act.activation(dec[:, :], dtmp[:, :], ACT.Exp).then_inc(S["dec"], 1)

                def at_copy(t):
                    act.wait_ge(S["at_T"], at("at_T", t + 1))
                    act.activation(gd(t, "at"), pt[:, 3, :], ACT.Copy).then_inc(S["at"], 1)

                def m1_copy(lv, t):
                    act.wait_ge(S["m1_mm"], at("m1_mm", 2 * (lv - 1) + t + 1))
                    act.activation(gd(t, "m"), pt[:, t, :], ACT.Copy).then_inc(S["m1"], 1)

                def branch_hi(first, n, name_wait, k):
                    act.wait_ge(S[name_wait], at(name_wait, k))
                    act.activation(hhi[:, first:first + n, :], ot[:, first:first + n, :], ACT.Copy).then_inc(S["o_hi"], 1)

                def sigmoids():
                    act.wait_ge(S["mix_ev"], at("mix_ev", MIX_CH))
                    act.activation(gates[:, :, :], gates[:, :, :], ACT.Sigmoid).then_inc(S["gates"], 1)

                def merged_hi(t):
                    act.wait_ge(S["merged_T"], at("merged_T", t + 1))
                    act.activation(hhi[:, :, t * P:(t + 1) * P],
                                   pt[:, 2 * t:2 * t + 2, :].rearrange("p b (k s) -> p (b k) s", k=4), ACT.Copy).then_inc(S["m_hi"], 1)

                def fox_s(t):
                    return (scr[:, 0:512] if t == 0 else scr[:, 512:1536]).rearrange("p (h s) -> p h s", h=HEADS)

                def mixer():
                    for i in range(MIX_U):
                        u = U_M + i
                        small = i + 1 in (8, 9)
                        if i > 0:
                            split(u + 1, 48 if small else 2048)
                        for task in TASKS.get((i, 0), ()):
                            if task in tasks:
                                tasks[task]()
                        if i < BR0 and i % 2:
                            evac(i // 2)
                        for task in TASKS.get((i, 1), ()):
                            if task in tasks:
                                tasks[task]()
                    norm_stage(1, U_B)

                tasks = {
                    "silu0": lambda: conv_silu(0), "silu1": lambda: conv_silu(1), "silu2": lambda: conv_silu(2),
                    "l2norm": l2norm, "params": params, "fox_p": fox_exp, "fox_T": fox_pt, "fox_o": fox_o,
                    "sb_z": sb_ln, "sb_r": sb_w, "sb_o": sb_o, "kv": kv,
                    "dec0": lambda: decays(0), "dec1": lambda: (at_copy(0), decays(1)), "inv0": lambda: at_copy(1),
                    "o_split": lambda: branch_hi(0, 4, "o_ab", 2),
                    "c_split": lambda: (branch_hi(4, 4, "o_c", 1)), "sig": sigmoids,
                    "mrg": lambda: (merged_hi(0), merged_hi(1)),
                    "f2": lambda: state_copy(), "f5": lambda: (o_sq(0), o_sq(1)), "oT": lambda: o_copy(),
                }
                for lv in range(1, 7):
                    tasks[f"ma{lv}"] = lambda lv=lv: (m1_copy(lv, 0), m1_copy(lv, 1))

                def state_copy():
                    act.wait_ge(S["state_mm"], at("state_mm", 1))
                    act.activation(gd(0, "x"), pt[:, 1, :], ACT.Copy).then_inc(S["state"], 1)

                def o_sq(t):
                    act.wait_ge(S["o_raw"], at("o_raw", t + 1))
                    for h in range(HEADS):
                        ins = act.activation(gd(t, "ats")[:, h * P:(h + 1) * P],
                                             lnw[:, t, h * P:(h + 1) * P], ACT.Square,
                                             accum_out=oss[:, 4 * t + h:4 * t + h + 1])
                    ins.then_inc(S["o_ss"], 1)

                def o_copy():
                    act.wait_ge(S["o_T"], at("o_T", 1))
                    act.activation(ot[:, 4:8, :], pt[:, 0:2, :].rearrange("p b (k s) -> p (b k) s", k=2), ACT.Copy).then_inc(S["o_c"], 1)

                ffn(0, 0, U_A, True)
                mixer()
                ffn(1, 2, U_B, False)

        @block.tensor
        def _(pe):
            pe.wait_ge(S["masks_done"], 1)
            pe.wait_ge(S["rows_in"], 64)
            pe.transpose(pt[:, 0, 0:48], lnw[0:48, 0, 0:128], ident[0:48, 0:48])
            pe.transpose(pt[:, 0, 48:96], lnw[0:48, 0, 128:256], ident[0:48, 0:48])
            pe.transpose(pt[:, 0, 96:192], lnw[0:96, 0, 256:384], ident[0:96, 0:96])
            pe.transpose(pt[:, 0, 192:200], lnw[0:8, 0, 384:512], ident[0:8, 0:8]).then_inc(S["cols_T"], 1)

            def mod_columns(at, k):
                pe.wait_ge(S["ada_done"], at("ada_done", ADA_N * (k + 1)))
                for part in (0, 1):
                    for c in range(KD):
                        ins = pe.matmul(pt[:, 3, part * KD + c:part * KD + c + 1],
                                        acc[:, part * D + c * P:part * D + (c + 1) * P], ones[:, 0:1],
                                        start=True, stop=True)
                ins.then_inc(S["mod_mm"], 1)

            def gate_rows(at):
                for n in (0, 1):
                    ins = pe.matmul(pt[:, n, :], ones, acc[:, 2 * D + n * 512:2 * D + (n + 1) * 512],
                                    start=True, stop=True)
                ins.then_inc(S["gate_mm"], 1)

            def x_transposes(t, credit=False):
                for c in range(KD):
                    ins = pe.transpose(pt[:, 2 * t + c // 4, (c % 4) * P:(c % 4 + 1) * P],
                                       x[:, t, c * P:(c + 1) * P], ident[:, :])
                    if credit and c == 0:
                        ins.then_inc(S["w_used"], 2)
                ins.then_inc(S["ln_xt"], 1)

            w0 = counter(None)
            pe.wait_ge(S["cols"], 1)
            mod_columns(w0, 0)
            pe.wait_ge(S["x_in"], 16)
            pe.wait_ge(S["mod_cols"], 1)
            for t in range(NT):
                x_transposes(t, credit=t == 0)

            with pe.Fori(0, DEPTH) as l:
                at = counter(l)

                def mm3(out_ap, a, b, first, last, group=False):
                    for n, (i, j) in enumerate(((0, 0), (0, 1), (1, 0))):
                        ins = pe.matmul(out_ap, a[i], b[j], start=first and n == 0, stop=last and n == 2,
                                        skip_group_check=group)
                    return ins

                def wv(u, k):
                    return [w[:, u % 2, :].rearrange("p (k c) -> p k c", k=k) for w in (whi, wlo)]

                def h_part(kt, t):
                    return [h[:, kt, t * P:(t + 1) * P] for h in (hhi, hlo)]

                def up_half(u, ui, t):
                    w = wv(u, 4)
                    for k in range(4):
                        ins = mm3(pg[:, t, :], h_part(4 * ui + k, t), [v[:, k, :] for v in w],
                                  ui == 0 and k == 0, ui == 1 and k == 3)
                    return ins

                def act_transposes():
                    for t in range(NT):
                        for k in (0, 1):
                            ins = pe.transpose(pt[:, 0, k * SEQ + t * P:k * SEQ + (t + 1) * P],
                                               act_t[:, t, k * P:(k + 1) * P], ident[:, :])
                    ins.then_inc(S["act_T"], 1)

                def ffn(f, s, u0):
                    up0 = f * 2 * NCH
                    pe.wait_ge(S["w_lo"], at("w_lo", u0 + 1))
                    for t in range(NT):
                        pe.wait_ge(S["h_lo"], at("h_lo", NT * (s - 1) + t + 1))
                        ins = up_half(u0, 0, t)
                    ins.then_inc(S["w_used"], 1)
                    gate_rows(at)
                    pe.wait_ge(S["w_lo"], at("w_lo", u0 + 2))
                    for t in range(NT):
                        up_half(u0 + 1, 1, t).then_inc(S[("up_mm", "w_used")[t]], 1)

                    def body(j):
                        if isinstance(j, int):
                            pe.wait_ge(S["w_lo"], at("w_lo", u0 + 2 * j + 1))
                        else:
                            pe.wait_ge(S["w_lo"], l * PER["w_lo"] + j * 2 + (OFF["w_lo"] + u0 + 1))
                        for t in range(NT):
                            if isinstance(j, int):
                                pe.wait_ge(S["act"], at("act", up0 + 2 * (j - 1) + t + 1))
                            else:
                                pe.wait_ge(S["act"], l * PER["act"] + j * 2 + (up0 + t - 1))
                            ins = up_half(u0, 0, t)
                        ins.then_inc(S["w_used"], 1)
                        if isinstance(j, int):
                            pe.wait_ge(S["act_lo"], at("act_lo", f * NCH + j - 1))
                        else:
                            pe.wait_ge(S["act_lo"], l * PER["act_lo"] + j + (OFF["act_lo"] + f * NCH - 1))
                        pe.wait_ge(S["gate_bc"], at("gate_bc", s + 1))
                        act_transposes()
                        if isinstance(j, int):
                            pe.wait_ge(S["w_lo"], at("w_lo", u0 + 2 * j + 2))
                        else:
                            pe.wait_ge(S["w_lo"], l * PER["w_lo"] + j * 2 + (OFF["w_lo"] + u0 + 2))
                        for t in range(NT):
                            up_half(u0 + 1, 1, t).then_inc(S[("up_mm", "w_used")[t]], 1)

                    with pe.Fori(1, NCH - 1) as j:
                        body(j)
                    body(NCH - 1)
                    for d in range(DOWN_U):
                        u = u0 + UP_U + d
                        pe.wait_ge(S["w_lo"], at("w_lo", u + 1))
                        if d == 0:
                            pe.wait_ge(S["act_lo"], at("act_lo", f * NCH + 1))
                        if d == DOWN_U - 1:
                            pe.wait_ge(S["act_lo"], at("act_lo", f * NCH + NCH))
                        w = wv(u, 2)
                        for t in ((1, 0) if d == 0 else (0, 1)):
                            if d == 0 and t == 0:
                                pe.wait_ge(S["act"], at("act", up0 + 2 * NCH))
                            for n in (0, 1):
                                for k in (0, 1):
                                    a = [v[:, 2 * d + k, t * P:(t + 1) * P] for v in (athi, atlo)]
                                    ins = mm3(pg[:, 2 * t + n, :], a, [v[:, k, n * 512:(n + 1) * 512] for v in w],
                                              d == 0 and k == 0, d == DOWN_U - 1 and k == 1)
                            if d == DOWN_U - 1 and t == 0:
                                ins.then_inc(S["y_mm"], 1)
                        ins.then_inc(S["w_used"], 1)
                        if d == 0:
                            pe.wait_ge(S["act_lo"], at("act_lo", f * NCH + NCH - 1))
                            act_transposes()
                        if d == 6:
                            mod_columns(at, s)
                    norm_stage(s)

                def norm_stage(s):
                    pe.wait_ge(S["mod_cols"], at("mod_cols", s + 1))
                    for t in range(NT):
                        pe.wait_ge(S["ln_x"], at("ln_x", NT * s + t + 1))
                        x_transposes(t)

                def chunk_half(i, half):
                    k, ui, u = i // 2, i % 2, U_M + i
                    b = 2 * (k % 2)
                    if half == 0:
                        pe.wait_ge(S["w_lo"], at("w_lo", u + 1))
                        if ui == 0:
                            if k == 0:
                                pe.wait_ge(S["h_lo"], at("h_lo", 2))
                            if k >= 2:
                                pe.wait_ge(S["mix_ev"], at("mix_ev", k - 1))
                    kts = (2 * half, 2 * half + 1)
                    last = ui == 1 and half == 1
                    if k in (0, 1, 2, 5, 7):
                        w = wv(u, 4)
                        for c in range(4):
                            for kt in kts:
                                first = ui == 0 and kt == 0 and c % 2 == 0
                                ins = mm3(pg[:, b + c // 2, (c % 2) * SEQ:(c % 2 + 1) * SEQ],
                                          [v[:, kt, c * P:(c + 1) * P] for v in w],
                                          [v[:, 4 * ui + kt, :] for v in (hhi, hlo)],
                                          first, last and kt == 3, group=True)
                    else:
                        n = 12 if k == 4 else 512
                        w = ([v[:, u % 2, 0:48].rearrange("p (k c) -> p k c", k=4) for v in (whi, wlo)]
                             if k == 4 else wv(u, 4))
                        for t in range(NT):
                            for kt in kts:
                                ins = mm3(pg[:, b + t, 0:n], h_part(4 * ui + kt, t), [v[:, kt, :] for v in w],
                                          ui == 0 and kt == 0, last and kt == 3)
                    if half == 1:
                        ins.then_inc(S["w_used"], 1)

                def ssq():
                    pe.wait_ge(S["cv_sq"], at("cv_sq", 2))
                    pe.wait_ge(S["gate_bc"], at("gate_bc", 2))
                    for b in range(4):
                        ins = pe.matmul(pt[:, b, :], ones, scr[:, b * 512:(b + 1) * 512], start=True, stop=True)
                    ins.then_inc(S["ssq_mm"], 1)

                def rows():
                    pe.wait_ge(S["lgu"], at("lgu", 4))
                    for hp in (0, 1):
                        r0 = scr[:, 512 * hp:512 * hp + 512]
                        pe.matmul(pt[:, hp, :], ones, r0, start=True, stop=False, skip_group_check=True)
                        r1 = scr[:, 1024 + 256 * hp:1024 + 256 * hp + 256].rearrange("p (h s) -> p h s", h=2)
                        ins = pe.matmul(pt[:, hp, :].rearrange("p (h s) -> p h s", h=2)[:, :, P:2 * P], ones, r1,
                                        start=False, stop=True, skip_group_check=True)
                    c = pt[:, 2, 0:16].rearrange("p (a h) -> p a h", a=4)
                    pe.matmul(c[:, 0, :], tri, lg[:, 0, 0:4], start=True, stop=True)
                    pe.matmul(c[:, 1, :], ones, lg[:, 0, 0:4], start=True, stop=False)
                    pe.matmul(c[:, 1, :], tri, lg[:, 1, 0:4], start=False, stop=True)
                    pe.matmul(c[:, 2, :], tri, lg[:, 0, 4:8], start=True, stop=True)
                    pe.matmul(c[:, 3, :], tri, lg[:, 1, 4:8], start=True, stop=True)
                    ins = pe.matmul(pt[:, 2, 16:20], ones, lg[:, 0, 4:8], start=True, stop=True)
                    ins.then_inc(S["rows_mm"], 1)

                def heads(a, h, lo, hi):
                    return qkt[(h % 2) * DH:(h % 2 + 1) * DH, a, h // 2, lo:hi]

                def fox_scores():
                    pe.wait_ge(S["mix_ev"], at("mix_ev", 6))
                    pe.wait_ge(S["fox_b"], at("fox_b", 2))
                    for odd in (0, 1):
                        for h in (odd, odd + 2):
                            pe.matmul(pt[:, 0, h * P:(h + 1) * P], heads(0, h, 0, P), heads(1, h, 0, P),
                                      start=True, stop=True)
                            ins = pe.matmul(pt[:, 1 + h // 2, (h % 2) * SEQ:(h % 2 + 1) * SEQ],
                                            heads(0, h, P, SEQ), heads(1, h, 0, SEQ), start=True, stop=True)
                        ins.then_inc(S["fox_mm"], 1)
                        pe.wait_ge(S["fox_mm"], at("fox_mm", odd + 1))

                def fox_T():
                    pe.wait_ge(S["fox_p"], at("fox_p", 2))
                    for h in range(HEADS):
                        o0 = pt[:, h // 2, (h % 2) * SEQ:(h % 2 + 1) * SEQ]
                        p1 = scr[:, 512 + h * SEQ:512 + (h + 1) * SEQ]
                        pe.transpose(o0[:, 0:P], scr[:, h * P:(h + 1) * P], ident[:, :])
                        pe.transpose(o0[:, P:SEQ], p1[:, 0:P], ident[:, :])
                        ins = pe.transpose(pt[:, 2, h * P:(h + 1) * P], p1[:, P:SEQ], ident[:, :])
                    ins.then_inc(S["foxp_T"], 1)

                def pv(name, v0, w0_, w1_):
                    for h in range(HEADS):
                        r = (h % 2) * DH
                        o = pt[r:r + DH, 3, (h // 2) * SEQ:(h // 2 + 1) * SEQ]
                        pe.matmul(o, val[:, 0, v0 + h * DH:v0 + (h + 1) * DH], w0_[:, h * SEQ:(h + 1) * SEQ],
                                  start=True, stop=False, skip_group_check=True)
                        ins = pe.matmul(o[:, P:SEQ], val[:, 1, v0 + h * DH:v0 + (h + 1) * DH],
                                        w1_[:, h * P:(h + 1) * P], start=False, stop=True, skip_group_check=True)
                    ins.then_inc(S[name], 1)

                def fox_pv():
                    pe.wait_ge(S["fox_pt"], at("fox_pt", 2))
                    pe.wait_ge(S["mix_ev"], at("mix_ev", 7))
                    pv("fox_pv", 0, scr[:, 1536:2560], scr[:, 2560:3072])

                def sb_scores():
                    pe.wait_ge(S["mix_ev"], at("mix_ev", 8))
                    pe.wait_ge(S["fox_pt"], at("fox_pt", 2))
                    pe.wait_ge(S["fox_b"], at("fox_b", 2))
                    for odd in (0, 1):
                        for h in (odd, odd + 2):
                            pe.matmul(pt[:, h // 2, (h % 2) * SEQ:(h % 2 + 1) * SEQ], heads(3, h, 0, P),
                                      heads(2, h, 0, SEQ), start=True, stop=True)
                            ins = pe.matmul(pt[:, 2, h * P:(h + 1) * P], heads(3, h, P, SEQ), heads(2, h, P, SEQ),
                                            start=True, stop=True)
                        ins.then_inc(S["sb_mm"], 1)
                        pe.wait_ge(S["sb_mm"], at("sb_mm", odd + 1))

                def sb_cum():
                    pe.wait_ge(S["sb_sp"], at("sb_sp", 1))
                    for hp in (0, 1):
                        pe.matmul(pt[:, hp, :], trid[:, :], scr[:, 1536 + 512 * hp:1536 + 512 * (hp + 1)],
                                  start=True, stop=False, skip_group_check=True)
                        pe.matmul(pt[:, hp, :].rearrange("p (h s) -> p h s", h=2)[:, :, P:2 * P], ones,
                                  scr[:, 2560 + 256 * hp:2560 + 256 * (hp + 1)].rearrange("p (h s) -> p h s", h=2),
                                  start=False, stop=True, skip_group_check=True)
                    ins = pe.matmul(pt[:, 2, :], trid[:, :], scr[:, 2560:3072], start=True, stop=True)
                    ins.then_inc(S["sb_cum"], 1)

                def sb_pv():
                    pe.wait_ge(S["sb_w"], at("sb_w", 1))
                    pe.wait_ge(S["o_ab"], at("o_ab", 1))
                    pv("sb_pv", 256, scr[:, 0:1024], scr[:, 1024:1536])

                def hs(a, h):
                    return a[:, h * P:(h + 1) * P]

                def qh(h, t):
                    return cv[:, h, t * P:(t + 1) * P]

                def kh(h, t):
                    return cv[:, HEADS + h, t * P:(t + 1) * P]

                def kv():
                    pe.wait_ge(S["conv_silu"], at("conv_silu", 3))
                    pe.wait_ge(S["qk_norm"], at("qk_norm", 2))
                    pe.wait_ge(S["sb_arg"], at("sb_arg", 1))
                    for h in range(HEADS):
                        pe.transpose(hs(pt[:, 0, :], h), kh(h, 0), ident[:, :])
                        for t in range(NT):
                            ins = pe.transpose(hs(pt[:, 1 + t, :], h), cv[:, 2 * HEADS + h, t * P:(t + 1) * P], ident[:, :])
                    ins.then_inc(S["kv_T"], 1)

                def grams(t):
                    if t == 0:
                        pe.wait_ge(S["kv"], at("kv", 2))
                    else:
                        pe.wait_ge(S["g_mats"], at("g_mats", 1))
                    pe.wait_ge(S["g_gu"], at("g_gu", t + 1))
                    for h in range(HEADS):
                        pe.matmul(hs(pt[:, 0, :], h), kh(h, t), kh(h, t), start=True, stop=True)
                    for h in range(HEADS):
                        pe.matmul(hs(pt[:, 1, :], h), kh(h, t), qh(h, t), start=True, stop=True)
                    ins = pe.matmul(pt[:, 2, :], ones, gd(t, "m"), start=True, stop=True)
                    ins.then_inc(S["gram_mm"], 1)

                def a_T(t):
                    pe.wait_ge(S["g_a"], at("g_a", t + 1))
                    if t:
                        pe.wait_ge(S["at"], at("at", 1))
                    else:
                        pe.wait_ge(S["o_ab"], at("o_ab", 2))
                    for h in range(HEADS):
                        ins = pe.transpose(hs(pt[:, 3, :], h), hs(gd(t, "m"), h), ident[:, :])
                    ins.then_inc(S["at_T"], 1)

                def m1(lv):
                    for t in range(NT):
                        pe.wait_ge(S["inv_x"], at("inv_x", 2 * (lv - 1) + 2))
                        pe.wait_ge(S["ats"], at("ats", 2 * (lv - 1) + t + 1))
                        for h in range(HEADS):
                            ins = pe.matmul(hs(pt[:, t, :], h), hs(gd(t, "ats"), h), hs(gd(t, "x"), h),
                                            start=True, stop=True)
                        ins.then_inc(S["m1_mm"], 1)

                def m2(lv):
                    for t in range(NT):
                        pe.wait_ge(S["m1"], at("m1", 2 * (lv - 1) + t + 1))
                        b = 2 - 2 * t
                        for h in range(HEADS):
                            if lv < 6:
                                pe.matmul(hs(pt[:, b, :], h), hs(gd(t, "xt"), h), hs(gd(t, "m"), h), start=True, stop=True)
                        for h in range(HEADS):
                            ins = pe.matmul(hs(pt[:, b + 1, :], h), hs(gd(t, "m"), h), hs(gd(t, "xt"), h),
                                            start=True, stop=True)
                        ins.then_inc(S["m2_mm"], 1)

                def f1():
                    pe.wait_ge(S["bv"], at("bv", 1))
                    pe.wait_ge(S["inv_x"], at("inv_x", 13))
                    for h in range(HEADS):
                        ins = pe.matmul(hs(pt[:, 0, :], h), hs(gd(0, "xt"), h), hs(gd(0, "ats"), h), start=True, stop=True)
                    ins.then_inc(S["vnew_mm"], 1)

                def f2():
                    pe.wait_ge(S["vnew"], at("vnew", 2))
                    pe.wait_ge(S["inv_x"], at("inv_x", 14))
                    for h in range(HEADS):
                        ins = pe.matmul(hs(pt[:, 1, :], h), kn[:, h, :], hs(scr[:, 3584:4096], h), start=True, stop=True)
                    ins.then_inc(S["state_mm"], 1)
                    for h in range(HEADS):
                        ins = pe.matmul(hs(pt[:, 2, :], h), hs(gd(0, "it"), h), hs(scr[:, 3072:3584], h),
                                        start=True, stop=True)
                    ins.then_inc(S["o0_mm"], 1)

                def f3():
                    pe.wait_ge(S["state"], at("state", 1))
                    for h in range(HEADS):
                        pe.matmul(hs(pt[:, 0, :], h), kh(h, 1), hs(gd(0, "x"), h), start=True, stop=True)
                    for h in range(HEADS):
                        ins = pe.matmul(hs(pt[:, 3, :], h), qh(h, 1), hs(gd(0, "x"), h), start=True, stop=True)
                    ins.then_inc(S["zq_mm"], 1)

                def f4():
                    pe.wait_ge(S["rhs1"], at("rhs1", 1))
                    pe.wait_ge(S["inv_x"], at("inv_x", 14))
                    for h in range(HEADS):
                        ins = pe.matmul(hs(pt[:, 1, :], h), hs(gd(1, "xt"), h), hs(gd(1, "ats"), h), start=True, stop=True)
                    ins.then_inc(S["vnew_mm"], 1)

                def f5():
                    pe.wait_ge(S["vnew"], at("vnew", 3))
                    for h in range(HEADS):
                        ins = pe.matmul(hs(pt[:, 2, :], h), hs(gd(1, "it"), h), hs(scr[:, 3072:3584], h),
                                        start=True, stop=True)
                    ins.then_inc(S["o1_mm"], 1)

                def o_T():
                    for t in range(NT):
                        pe.wait_ge(S["o_gated"], at("o_gated", t + 1))
                        for h in range(HEADS):
                            ins = pe.transpose(pt[:, h // 2, (h % 2) * SEQ + t * P:(h % 2) * SEQ + (t + 1) * P],
                                               hs(lnw[:, t, 512:1024], h), ident[:, :])
                    ins.then_inc(S["o_T"], 1)

                def merged_T():
                    for t in range(NT):
                        pe.wait_ge(S["merged"], at("merged", 2 * t + 2))
                        for c in range(KD):
                            ins = pe.transpose(pt[:, 2 * t + c // 4, (c % 4) * P:(c % 4 + 1) * P],
                                               merged[:, t, c * P:(c + 1) * P], ident[:, :])
                        ins.then_inc(S["merged_T"], 1)

                tasks = {"l2norm": ssq, "rows": rows, "fox_p": fox_scores, "fox_T": fox_T, "fox_o": fox_pv,
                         "sb_z": sb_scores, "sb_r": sb_cum, "sb_o": sb_pv, "kv": kv,
                         "dec0": lambda: grams(0), "dec1": lambda: (a_T(0), grams(1)), "inv0": lambda: a_T(1),
                         "f1": f1, "f2": f2, "f3": f3, "f4": f4, "f5": f5, "oT": o_T, "mrg": merged_T}
                for lv in range(1, 7):
                    tasks[f"ma{lv}"] = lambda lv=lv: m1(lv)
                    tasks[f"mb{lv}"] = lambda lv=lv: m2(lv)

                def rows_unit(i, half):
                    u = U_M + i
                    b = i - BR0
                    w = wv(u, 2)
                    if half == 0:
                        pe.wait_ge(S["w_lo"], at("w_lo", u + 1))
                    if b < 4:
                        first, last = b < 3, b != 2
                    else:
                        first, last = b == 4, b == 7
                    for t in (half,):
                        for n in (0, 1):
                            if b == 0:
                                pe.wait_ge(S["mix_ev"], at("mix_ev", MIX_CH - 1 if t == 0 else MIX_CH))
                                pe.wait_ge(S["o_lo"], at("o_lo", 1))
                            if b in (1, 2):
                                pe.wait_ge(S["y_ev"], at("y_ev", 4 * (b - 1) + 2 * t + n + 1))
                            if b == 2 and t == 0 and n == 0:
                                pe.wait_ge(S["o_lo"], at("o_lo", 2))
                            if b == 4:
                                pe.wait_ge(S["y_ev"], at("y_ev", 8 + 2 * t + n + 1))
                                pe.wait_ge(S["m_lo"], at("m_lo", t + 1))
                            for k in (0, 1):
                                kt = (2 * b if b < 4 else 2 * (b - 4)) + k
                                ins = mm3(pg[:, 2 * t + n, :], h_part(kt, t), [v[:, k, n * 512:(n + 1) * 512] for v in w],
                                          first and k == 0, last and k == 1)
                            if b < 4 and last and (half, n) != (1, 1):
                                ins.then_inc(S["yb_mm"], 1)
                    if (b, half) == (7, 0):
                        ins.then_inc(S["y_mm"], 1)
                    if half == 1:
                        ins.then_inc(S["w_used"], 1)

                def mixer():
                    for i in range(MIX_U):
                        for half in (0, 1):
                            if i < BR0:
                                chunk_half(i, half)
                            else:
                                rows_unit(i, half)
                            if (i, half) == (0, 1):
                                gate_rows(at)
                            if (i, half) == (33, 0):
                                pe.wait_ge(S["m_lo"], at("m_lo", 2))
                                mod_columns(at, 1)
                            for task in TASKS.get((i, half), ()):
                                if task in tasks:
                                    tasks[task]()
                    norm_stage(1)

                ffn(0, 0, U_A)
                mixer()
                ffn(1, 2, U_B)

        @block.vector
        def _(dve):
            dve.wait_ge(S["cols_T"], 1)
            dve.wait_ge(S["sc_ready"], 1)
            dve.tensor_copy(cols[:, :], pt[:, 0, 0:192]).then_inc(S["cols"], 1)
            dve.memset(modt[:, :], 0.0).then_inc(S["act_lo"], 1)

            def fold(slot, col0, base, dyn=None):
                a = acc[:, col0:col0 + ADA_C] if dyn is None else acc[:, ds(col0 + dyn * ADA_C, ADA_C)]
                r = raw[:, slot, :].rearrange("p (k c) -> p k c", k=KD)
                for k in range(KD):
                    ins = dve.scalar_tensor_tensor(out=a, in0=r[:, k, :], scalar=sc[:, k:k + 1], in1=a,
                                                   op0=ALU.mult, op1=ALU.add)
                    if k < KD - 1:
                        ins.then_inc(S["fold"], 1)
                        base(k + 1)
                return ins

            dve.wait_ge(S["acc_row"], 16)
            for i in range(ADA_N):
                slot = i % 3
                dve.wait_ge(S[f"raw_in{slot}"], 32 * (i // 3 + 1))
                ins = fold(slot, i * ADA_C, lambda k, i=i: dve.wait_ge(S["fold"], 7 * i + k))
                ins.then_inc(S["ada_done"], 1)

            def mod_cols(first, at, k, lncol):
                dve.wait_ge(S["mod_mm"], at("mod_mm", k + 1))
                if first:
                    dve.tensor_scalar(modab[:, 0, :], pt[:, 3, KD:2 * KD], 1.0, None, ALU.add).then_inc(S["w_lo"], 2)
                    dve.tensor_copy(modab[:, 1, :], pt[:, 3, 0:KD]).then_inc(S["mod_cols"], 1)
                    return
                dve.wait_ge(S["ada_done"], at("ada_done", ADA_N * (k + 1)))
                g = cols[:, ds(lncol, KD)]
                b = cols[:, ds(lncol + 48, KD)]
                dve.scalar_tensor_tensor(out=modab[:, 0, :], in0=pt[:, 3, KD:2 * KD], scalar=1.0, in1=g,
                                         op0=ALU.add, op1=ALU.mult).then_inc(S["mod_a"], 1)
                dve.scalar_tensor_tensor(out=modt[:, :], in0=pt[:, 3, KD:2 * KD], scalar=1.0, in1=b,
                                         op0=ALU.add, op1=ALU.mult).then_inc(S["mod_a"], 1)
                dve.wait_ge(S["mod_a"], at("mod_a", 2 * k + 2))
                dve.tensor_tensor(modab[:, 1, :], modt[:, :], pt[:, 3, 0:KD], ALU.add).then_inc(S["mod_cols"], 1)

            def h_split(at, k, t):
                dve.wait_ge(S["h_f32"], at("h_f32", NT * k + t + 1))
                src = lnw[:, t, :].rearrange("p (k s) -> p k s", k=KD)
                hi = hhi[:, :, t * P:(t + 1) * P]
                dve.tensor_copy(hi, src).then_inc(S["h_hi"], 1)
                dve.wait_ge(S["h_hi"], at("h_hi", NT * k + t + 1))
                dve.tensor_tensor(hlo[:, :, t * P:(t + 1) * P], src, hi.bitcast(F32), ALU.subtract).then_inc(S["h_lo"], 1)

            w0 = counter(None)
            mod_cols(True, w0, 0, 0)
            for t in range(NT):
                h_split(w0, 0, t)

            with dve.Fori(0, DEPTH) as l:
                at = counter(l)

                def split(u, size=2048):
                    s = u % 2
                    dve.wait_ge(S["w_hi"], at("w_hi", u + 1))
                    ins = dve.tensor_tensor(wlo[:, s, 0:size], raw[:, s, 0:size], whi[:, s, 0:size].bitcast(F32),
                                            ALU.subtract)
                    ins.then_inc(S["w_lo"], 1)

                def split_j(u, j):
                    s = u % 2
                    dve.wait_ge(S["w_hi"], l * PER["w_hi"] + j * 2 + (u + 1))
                    dve.tensor_tensor(wlo[:, s, :], raw[:, s, :], whi[:, s, :].bitcast(F32), ALU.subtract).then_inc(S["w_lo"], 1)

                def ada(idx, j):
                    dve.wait_ge(S["raw_in2"], at("raw_in2", 32 * (idx + 1)))
                    dve.wait_ge(S["acc_row"], at("acc_row", 16 * (idx // ADA_N + 1)))
                    ins = fold(2, j * ADA_C, lambda k: dve.wait_ge(S["fold"], at("fold", 7 * idx + k)))
                    ins.then_inc(S["ada_done"], 1)

                def gate_bc(s, coef):
                    dve.wait_ge(S["gate_mm"], at("gate_mm", s + 1))
                    dve.tensor_scalar(gatebc[:, :], pt[:, 0:2, :].rearrange("p b c -> p (b c)"), coef, coef,
                                      ALU.mult, ALU.add).then_inc(S["gate_bc"], 1)

                def act_lo(f, j):
                    dve.wait_ge(S["act_hi"], at("act_hi", f * NCH + j))
                    dve.tensor_tensor(atlo[:, 2 * j - 2:2 * j, :], pt[:, 0, :].rearrange("p (k s) -> p k s", k=2),
                                      athi[:, 2 * j - 2:2 * j, :].bitcast(F32), ALU.subtract).then_inc(S["act_lo"], 1)

                def act_mul(base, t, j=None):
                    if j is None:
                        dve.wait_ge(S["up_silu"], at("up_silu", base + t + 1))
                    else:
                        dve.wait_ge(S["up_silu"], l * PER["up_silu"] + j * 2 + (base + t + 1))
                    dve.tensor_tensor(act_t[:, t, :], sg[:, t, :], pg[:, t, CW:2 * CW], ALU.mult).then_inc(S["act"], 1)

                def ffn(f, s, u0, a0, first):
                    up0 = f * 2 * NCH
                    if first:
                        split(u0)
                        split(u0 + 1)
                    gate_bc(s, 0.5)
                    split(u0 + 2)
                    act_mul(up0, 0)
                    act_mul(up0, 1)
                    with dve.Fori(1, NCH - 1) as j:
                        split_j(u0 + 1, j)
                        dve.wait_ge(S["act_hi"], l * PER["act_hi"] + j + (f * NCH))
                        dve.tensor_tensor(atlo[:, ds(j * 2 - 2, 2), :], pt[:, 0, :].rearrange("p (k s) -> p k s", k=2),
                                          athi[:, ds(j * 2 - 2, 2), :].bitcast(F32), ALU.subtract).then_inc(S["act_lo"], 1)
                        split_j(u0 + 2, j)
                        dve.wait_ge(S["raw_in2"], l * PER["raw_in2"] + j * 32 + (OFF["raw_in2"] + 32 * a0))
                        dve.wait_ge(S["acc_row"], at("acc_row", 16 * (s + 1)))

                        def step(k):
                            dve.wait_ge(S["fold"], l * PER["fold"] + j * 7 + (OFF["fold"] + 7 * (a0 - 1) + k))
                        ins = fold(2, -ADA_C, step, dyn=j)
                        ins.then_inc(S["ada_done"], 1)
                        act_mul(up0, 0, j)
                        act_mul(up0, 1, j)
                    split(u0 + 2 * NCH - 1)
                    act_lo(f, NCH - 1)
                    split(u0 + 2 * NCH)
                    ada(a0 + NCH - 2, NCH - 2)
                    act_mul(up0 + 2 * (NCH - 1), 0)
                    act_mul(up0 + 2 * (NCH - 1), 1)
                    for d in range(DOWN_U):
                        u = u0 + UP_U + d
                        if d == 1:
                            act_lo(f, NCH)
                        if d < DOWN_U - 1 or s == 0:
                            split(u + 1)
                        if d in (1, 4):
                            k = NCH - 1 + (d == 4)
                            ada(a0 + k, k)
                    mod_cols(False, at, s, l * 24 + s * 8)
                    norm_stage(s, u0 + FFN_U)

                def norm_stage(s, u_next):
                    def residual(t):
                        if t == 0:
                            dve.wait_ge(S["y_mm"], at("y_mm", s + 1))
                        else:
                            dve.wait_ge(S["w_used"], at("w_used", u_next))
                        dve.wait_ge(S["x_affine"], at("x_affine", NT * s))
                        dve.tensor_tensor(lnw[:, t, :], pg[:, 2 * t:2 * t + 2, :].rearrange("p b c -> p (b c)"),
                                          gatebc[:, :], ALU.mult).then_inc(S["ln_gy"], 1)
                        dve.wait_ge(S["ln_gy"], at("ln_gy", NT * s + t + 1))
                        dve.scalar_tensor_tensor(out=x[:, t, :], in0=x[:, t, :], scalar=ALPHA, in1=lnw[:, t, :],
                                                 op0=ALU.mult, op1=ALU.add).then_inc(S["ln_sum"], 1)

                    def moments(t):
                        dve.wait_ge(S["ln_sum"], at("ln_sum", NT * s + t + 1))
                        for n in (0, 1):
                            dve.bn_stats(stats[:, t, n, :], x[:, t, n * 512:(n + 1) * 512]).then_inc(S["ln_bn"], 1)
                        dve.wait_ge(S["ln_bn"], alone(dve, "ln_bn", l * PER["ln_bn"] + (2 * NT * s + 2 * t + 2)))
                        dve.bn_aggr(mv[:, t, :], stats[:, t, :, :]).then_inc(S["ln_mv"], 1)
                        dve.wait_ge(S["ln_mv"], at("ln_mv", NT * s + t + 1))
                        dve.tensor_scalar(var[:, t:t + 1], mv[:, t, 1:2], LN_EPS, None, ALU.add).then_inc(S["ln_var"], 1)

                    def normed(t):
                        dve.wait_ge(S["ln_rstd"], at("ln_rstd", NT * s + t + 1))
                        dve.tensor_scalar(x[:, t, :], x[:, t, :], mv[:, t, 0:1], rstd[:, t:t + 1],
                                          ALU.subtract, ALU.mult).then_inc(S["ln_x"], 1)
                    residual(0)
                    moments(0)
                    residual(1)
                    normed(0)
                    moments(1)
                    normed(1)
                    if u_next < UNITS:
                        split(u_next + 1)
                    for t in range(NT):
                        h_split(at, s, t)

                def conv(k):
                    dve.wait_ge(S["mix_ev"], at("mix_ev", k + 1))
                    dve.wait_ge(S["convw"], at("convw", 1))
                    if k:
                        dve.wait_ge(S["conv_silu"], at("conv_silu", k))
                    pre = scr[:, 0:1040].rearrange("p (c s) -> p c s", c=4)
                    res = scr[:, 1040:2064].rearrange("p (c s) -> p c s", c=4)
                    for tap in range(TAPS):
                        for c in range(4):
                            n = tap * 12 + 4 * k + c
                            w = convw[:, n:n + 1]
                            src = pre[:, c, 1 + tap:1 + tap + SEQ]
                            if tap == 0:
                                ins = dve.tensor_scalar(res[:, c, :], src, w, None, ALU.mult)
                            else:
                                ins = dve.scalar_tensor_tensor(out=res[:, c, :], in0=src, scalar=w, in1=res[:, c, :],
                                                               op0=ALU.mult, op1=ALU.add)
                        ins.then_inc(S["conv"], 1)
                        if tap < TAPS - 1:
                            dve.wait_ge(S["conv"], at("conv", 4 * k + tap + 1))

                def pad():
                    dve.tensor_copy(convw[:, :], cols[:, ds(l * 48 + 96, 48)]).then_inc(S["convw"], 1)
                    dve.wait_ge(S["w_used"], at("w_used", U_M))
                    dve.memset(scr[:, 0:1040].rearrange("p (c s) -> p c s", c=4)[:, :, 0:4], 0.0).then_inc(S["pad"], 1)

                def squares():
                    dve.wait_ge(S["conv_silu"], at("conv_silu", 3))
                    src = cv[:, 0:8, :].rearrange("p c s -> p (c s)")
                    for n in (0, 1):
                        a = src[:, n * 1024:(n + 1) * 1024]
                        dve.tensor_tensor(scr[:, n * 1024:(n + 1) * 1024], a, a, ALU.mult).then_inc(S["cv_sq"], 1)

                def qk_norm():
                    dve.wait_ge(S["ssq_exp"], at("ssq_exp", 1))
                    src = cv[:, 0:8, :].rearrange("p c s -> p (c s)")
                    dve.scalar_tensor_tensor(out=src[:, 0:1024], in0=src[:, 0:1024], scalar=P ** -0.5,
                                             in1=scr[:, 2048:3072], op0=ALU.mult, op1=ALU.mult).then_inc(S["qk_norm"], 1)
                    dve.tensor_tensor(src[:, 1024:2048], src[:, 1024:2048], scr[:, 3072:4096], ALU.mult).then_inc(S["qk_norm"], 1)

                def params():
                    dve.wait_ge(S["mix_ev"], at("mix_ev", 5))
                    dve.wait_ge(S["prm_in"], at("prm_in", 64))
                    for t in range(NT):
                        dve.scalar_tensor_tensor(out=sp_a[:, t, 0:4], in0=sm[:, t, 0:4], scalar=-1.0,
                                                 in1=prm[:, 0:4], op0=ALU.mult, op1=ALU.subtract).then_inc(S["sp_arg"], 1)
                        dve.tensor_tensor(sp_a[:, t, 4:8], sm[:, t, 8:12], prm[:, 4:8], ALU.add).then_inc(S["sp_arg"], 1)
                    dve.wait_ge(S["sp_arg"], at("sp_arg", 4))
                    dve.scalar_tensor_tensor(out=sp_b[:, :, :], in0=sp_a[:, :, :], scalar=-1.0, in1=sp_a[:, :, :],
                                             op0=ALU.mult, op1=ALU.max).then_inc(S["sp_abs"], 1)
                    dve.wait_ge(S["sp_ln"], at("sp_ln", 1))
                    dve.scalar_tensor_tensor(out=sp_c[:, :, :], in0=sp_a[:, :, :], scalar=0.0, in1=sp_b[:, :, :],
                                             op0=ALU.max, op1=ALU.add).then_inc(S["sp"], 1)
                    dve.wait_ge(S["sp"], at("sp", 1))
                    dve.wait_ge(S["ea"], at("ea", 1))
                    for t in range(NT):
                        dve.tensor_scalar(lg[:, t, 0:4], sp_c[:, t, 0:4], -1.0, None, ALU.mult).then_inc(S["lg"], 1)
                        dve.scalar_tensor_tensor(out=lg[:, t, 4:8], in0=sp_c[:, t, 4:8], scalar=-1.0, in1=ea[:, :],
                                                 op0=ALU.mult, op1=ALU.mult).then_inc(S["lg"], 1)
                    dve.wait_ge(S["beta_e"], at("beta_e", 1))
                    dve.tensor_scalar(beta_t[:, :, :], beta_t[:, :, :], 1.0, None, ALU.add).then_inc(S["beta1"], 1)
                    dve.wait_ge(S["beta1"], at("beta1", 1))
                    dve.reciprocal(beta[:, :, :], beta_t[:, :, :]).then_inc(S["beta"], 1)
                    dve.wait_ge(S["lg"], at("lg", 4))
                    dve.wait_ge(S["qk_norm"], at("qk_norm", 2))
                    for h in range(HEADS):
                        ins = dve.tensor_scalar(scr[:, h * SEQ:(h + 1) * SEQ], tri1[:, :, :].rearrange("p a s -> p (a s)"),
                                                lg[:, 0, h:h + 1], None, ALU.mult)
                        ins.then_inc(S["lgu1"], 1)
                    dve.wait_ge(S["lgu1"], at("lgu1", 4))
                    for h in range(HEADS):
                        ins = dve.tensor_scalar(scr[:, 1024 + h * P:1024 + (h + 1) * P], tri, lg[:, 1, h:h + 1], None, ALU.mult)
                        ins.then_inc(S["lgu"], 1)

                def fox_bias():
                    dve.wait_ge(S["rows_mm"], at("rows_mm", 1))
                    dve.tensor_copy(ccol[:, :, :].rearrange("p a h -> p (a h)"), pt[:, 2, 0:16]).then_inc(S["ccol"], 1)
                    dve.wait_ge(S["ccol"], at("ccol", 1))
                    dve.tensor_tensor(dtmp[:, :], pt[:, 2, 16:20], ccol[:, 2, :], ALU.subtract).then_inc(S["dec_arg"], 1)
                    r = pt[:, 0:2, :].rearrange("p b (h s) -> p (b h) s", h=2)
                    for h in range(HEADS):
                        ins = dve.scalar_tensor_tensor(out=scr[:, h * P:(h + 1) * P], in0=r[:, h, 0:P],
                                                       scalar=ccol[:, 0, h:h + 1], in1=foxm[:, 1, :],
                                                       op0=ALU.subtract, op1=ALU.add)
                    ins.then_inc(S["fox_b"], 1)
                    for h in range(HEADS):
                        ins = dve.scalar_tensor_tensor(out=scr[:, 512 + h * SEQ:512 + (h + 1) * SEQ], in0=r[:, h, :],
                                                       scalar=ccol[:, 1, h:h + 1],
                                                       in1=foxm[:, :, :].rearrange("p a s -> p (a s)"),
                                                       op0=ALU.subtract, op1=ALU.add)
                    ins.then_inc(S["fox_b"], 1)

                def fox_softmax():
                    dve.wait_ge(S["fox_mm"], at("fox_mm", 2))
                    dve.wait_ge(S["fox_b"], at("fox_b", 2))
                    dve.scalar_tensor_tensor(out=scr[:, 0:512], in0=pt[:, 0, :], scalar=SCALE, in1=scr[:, 0:512],
                                             op0=ALU.mult, op1=ALU.subtract).then_inc(S["fox_s"], 1)
                    dve.scalar_tensor_tensor(out=scr[:, 512:1536], in0=pt[:, 1:3, :].rearrange("p b s -> p (b s)"),
                                             scalar=SCALE, in1=scr[:, 512:1536], op0=ALU.mult, op1=ALU.subtract).then_inc(S["fox_s"], 1)
                    for t in range(NT):
                        dve.wait_ge(S["fox_s"], at("fox_s", t + 1))
                        s = (scr[:, 0:512] if t == 0 else scr[:, 512:1536]).rearrange("p (h s) -> p h s", h=HEADS)
                        dve.tensor_reduce(fmax[:, 4 * t:4 * t + 4], s, AX.X, ALU.max).then_inc(S["fox_max"], 1)
                        dve.wait_ge(S["fox_max"], at("fox_max", t + 1))
                        dve.tensor_scalar(fneg[:, 4 * t:4 * t + 4], fmax[:, 4 * t:4 * t + 4], -1.0, None, ALU.mult).then_inc(S["fox_neg"], 1)
                    for t in range(NT):
                        dve.wait_ge(S["fox_exp"], at("fox_exp", t + 1))
                        dve.reciprocal(frec[:, 4 * t:4 * t + 4], fsum[:, 4 * t:4 * t + 4]).then_inc(S["fox_rec"], 1)
                        dve.wait_ge(S["fox_rec"], at("fox_rec", t + 1))
                        n = P * (t + 1)
                        for h in range(HEADS):
                            a = scr[:, h * n + 512 * t:(h + 1) * n + 512 * t]
                            ins = dve.tensor_scalar(a, a, frec[:, 4 * t + h:4 * t + h + 1], None, ALU.mult)
                        ins.then_inc(S["fox_p"], 1)

                def sb_z():
                    dve.wait_ge(S["sb_mm"], at("sb_mm", 2))
                    dve.wait_ge(S["fox_pv"], at("fox_pv", 1))
                    z0 = scr[:, 0:1024].rearrange("p (h s) -> p h s", h=HEADS)
                    z1 = scr[:, 1024:1536].rearrange("p (h s) -> p h s", h=HEADS)
                    p0 = pt[:, 0:2, :].rearrange("p b (h s) -> p (b h) s", h=2)
                    m0 = sbm[:, :, :].rearrange("p a s -> p (a s)").unsqueeze(1).broadcast_to((P, HEADS, SEQ))
                    dve.scalar_tensor_tensor(out=z0, in0=p0, scalar=SCALE, in1=m0, op0=ALU.mult, op1=ALU.add).then_inc(S["sb_z"], 1)
                    m1_ = sbm[:, 0, :].unsqueeze(1).broadcast_to((P, HEADS, P))
                    dve.scalar_tensor_tensor(out=z1, in0=pt[:, 2, :].rearrange("p (h s) -> p h s", h=HEADS),
                                             scalar=SCALE, in1=m1_, op0=ALU.mult, op1=ALU.add).then_inc(S["sb_z"], 1)
                    dve.wait_ge(S["sb_z"], at("sb_z", 2))
                    dve.scalar_tensor_tensor(out=scr[:, 1536:3072], in0=scr[:, 0:1536], scalar=-1.0, in1=scr[:, 0:1536],
                                             op0=ALU.mult, op1=ALU.max).then_inc(S["sb_abs"], 1)
                    dve.wait_ge(S["sb_l"], at("sb_l", 1))
                    dve.scalar_tensor_tensor(out=scr[:, 1536:3072], in0=scr[:, 0:1536], scalar=0.0,
                                             in1=scr[:, 1536:3072], op0=ALU.max, op1=ALU.add).then_inc(S["sb_sp"], 1)

                def sb_arg():
                    dve.wait_ge(S["sb_cum"], at("sb_cum", 1))
                    dve.tensor_tensor(scr[:, 0:1536], scr[:, 0:1536], pt[:, 0:3, :].rearrange("p b s -> p (b s)"),
                                      ALU.subtract).then_inc(S["sb_arg"], 1)

                def hv(a):
                    return a.rearrange("p (h s) -> p h s", h=HEADS)

                def bc(m):
                    return m.unsqueeze(1).broadcast_to((P, HEADS, P))

                def g_rows(t):
                    if t == 0:
                        dve.wait_ge(S["sb_pv"], at("sb_pv", 1))
                    for h in range(HEADS):
                        ins = dve.tensor_scalar(gd(t, "m")[:, h * P:(h + 1) * P], tri, lg[:, t, 4 + h:5 + h], None, ALU.mult)
                    ins.then_inc(S["g_gu"], 1)

                def g_mats(t):
                    dve.wait_ge(S["gram_mm"], at("gram_mm", t + 1))
                    for h in range(HEADS):
                        row = pt[:, 2, h * P:(h + 1) * P]
                        ins = dve.tensor_scalar(gd(t, "ats")[:, h * P:(h + 1) * P], row, ccol[:, 2 + t, h:h + 1], 0.0,
                                                ALU.subtract, ALU.max)
                    ins.then_inc(S["g_diff"], 1)
                    for h in range(HEADS):
                        row = pt[:, 2, h * P:(h + 1) * P]
                        ins = dve.tensor_scalar(gd(t, "it")[:, h * P:(h + 1) * P], row, ccol[:, 2 + t, h:h + 1], 0.0,
                                                ALU.subtract, ALU.min)
                    ins.then_inc(S["g_diff"], 1)
                    dve.wait_ge(S["g_exp"], at("g_exp", 2 * t + 1))
                    dve.tensor_tensor(hv(gd(t, "ats")), hv(gd(t, "ats")), bc(strict[:, :]), ALU.mult).then_inc(S["g_em"], 1)
                    dve.wait_ge(S["g_em"], at("g_em", 2 * t + 1))
                    dve.wait_ge(S["beta"], at("beta", 1))
                    for h in range(HEADS):
                        sl = slice(h * P, (h + 1) * P)
                        ins = dve.scalar_tensor_tensor(out=gd(t, "m")[:, sl], in0=pt[:, 0, sl],
                                                       scalar=beta[:, t, h:h + 1], in1=gd(t, "ats")[:, sl],
                                                       op0=ALU.mult, op1=ALU.mult)
                    ins.then_inc(S["g_a"], 1)
                    dve.wait_ge(S["g_exp"], at("g_exp", 2 * t + 2))
                    dve.tensor_tensor(hv(gd(t, "it")), hv(gd(t, "it")), bc(incl_t[:, :]), ALU.mult).then_inc(S["g_em"], 1)
                    dve.wait_ge(S["g_em"], at("g_em", 2 * t + 2))
                    dve.tensor_tensor(gd(t, "it"), gd(t, "it"), pt[:, 1, :], ALU.mult).then_inc(S["g_mats"], 1)

                def inv_start(t):
                    dve.wait_ge(S["g_a"], at("g_a", t + 1))
                    dve.tensor_tensor(hv(gd(t, "ats")), hv(gd(t, "m")), bc(lev1[:, :]), ALU.mult).then_inc(S["x_tmp"], 1)
                    dve.wait_ge(S["x_tmp"], at("x_tmp", 2 * t + 1))
                    dve.tensor_tensor(hv(gd(t, "x")), bc(ident[:, :]), hv(gd(t, "ats")), ALU.subtract).then_inc(S["x_set"], 1)
                    dve.wait_ge(S["at"], at("at", t + 1))
                    dve.wait_ge(S["x_set"], at("x_set", t + 1))
                    dve.tensor_tensor(hv(gd(t, "ats")), hv(gd(t, "at")), bc(lev_t[:, 0, :]), ALU.mult).then_inc(S["x_tmp"], 1)
                    dve.wait_ge(S["x_tmp"], at("x_tmp", 2 * t + 2))
                    dve.tensor_tensor(hv(gd(t, "xt")), bc(ident[:, :]), hv(gd(t, "ats")), ALU.subtract).then_inc(S["inv_x"], 1)
                    dve.wait_ge(S["inv_x"], at("inv_x", t + 1))
                    dve.tensor_tensor(hv(gd(t, "ats")), hv(gd(t, "at")), bc(lev_t[:, 1, :]), ALU.mult).then_inc(S["ats"], 1)

                def inv_step(lv):
                    for t in range(NT):
                        dve.wait_ge(S["m2_mm"], at("m2_mm", 2 * (lv - 1) + t + 1))
                        b = 2 - 2 * t
                        if lv < 6:
                            dve.tensor_tensor(gd(t, "x"), gd(t, "x"), pt[:, b, :], ALU.subtract).then_inc(S["inv_m"], 1)
                        dve.tensor_tensor(gd(t, "xt"), gd(t, "xt"), pt[:, b + 1, :], ALU.subtract).then_inc(S["inv_x"], 1)
                        if lv < 6:
                            dve.tensor_tensor(hv(gd(t, "ats")), hv(gd(t, "at")), bc(lev_t[:, lv + 1, :]), ALU.mult).then_inc(S["ats"], 1)

                def bv():
                    dve.wait_ge(S["m2_mm"], at("m2_mm", 12))
                    for h in range(HEADS):
                        ins = dve.tensor_scalar(gd(0, "ats")[:, h * P:(h + 1) * P], vn[:, 0, h, :], beta[:, 0, h:h + 1],
                                                None, ALU.mult)
                    ins.then_inc(S["bv"], 1)

                def f1():
                    dve.wait_ge(S["vnew_mm"], at("vnew_mm", 1))
                    dve.wait_ge(S["dec"], at("dec", 1))
                    dve.tensor_copy(scr[:, 3072:3584], pt[:, 0, :]).then_inc(S["vnew"], 1)
                    for h in range(HEADS):
                        sl = slice(h * P, (h + 1) * P)
                        ins = dve.tensor_scalar(scr[:, 3584:4096][:, sl], pt[:, 0, sl], dec[:, h:h + 1], None, ALU.mult)
                    ins.then_inc(S["vnew"], 1)

                def f2():
                    dve.wait_ge(S["o0_mm"], at("o0_mm", 1))
                    dve.tensor_copy(lnw[:, 0, 0:512], pt[:, 2, :]).then_inc(S["o_raw"], 1)

                def f3():
                    dve.wait_ge(S["zq_mm"], at("zq_mm", 1))
                    dve.wait_ge(S["egc"], at("egc", 1))
                    for h in range(HEADS):
                        sl = slice(h * P, (h + 1) * P)
                        ins = dve.scalar_tensor_tensor(out=gd(0, "m")[:, sl], in0=pt[:, 0, sl], scalar=egc[:, h:h + 1],
                                                       in1=vn[:, 1, h, :], op0=ALU.mult, op1=ALU.subtract)
                    ins.then_inc(S["z_v"], 1)
                    dve.wait_ge(S["z_v"], at("z_v", 1))
                    dve.tensor_scalar(beta_t[:, 1, :], beta[:, 1, :], -1.0, None, ALU.mult).then_inc(S["beta_n"], 1)
                    dve.wait_ge(S["beta_n"], at("beta_n", 1))
                    for h in range(HEADS):
                        sl = slice(h * P, (h + 1) * P)
                        ins = dve.tensor_scalar(gd(1, "ats")[:, sl], gd(0, "m")[:, sl], beta_t[:, 1, h:h + 1], None, ALU.mult)
                    ins.then_inc(S["rhs1"], 1)
                    for h in range(HEADS):
                        sl = slice(h * P, (h + 1) * P)
                        ins = dve.tensor_scalar(gd(0, "at")[:, sl], pt[:, 3, sl], egc[:, h:h + 1], None, ALU.mult)
                    ins.then_inc(S["q_s"], 1)

                def f4():
                    dve.wait_ge(S["vnew_mm"], at("vnew_mm", 2))
                    dve.wait_ge(S["o0_mm"], at("o0_mm", 1))
                    dve.tensor_copy(scr[:, 3072:3584], pt[:, 1, :]).then_inc(S["vnew"], 1)

                def o_gate(t):
                    dve.wait_ge(S["o_ss"], at("o_ss", t + 1))
                    dve.tensor_scalar(oss[:, 4 * t:4 * t + 4], oss[:, 4 * t:4 * t + 4], 1.0 / P, RMS_EPS,
                                      ALU.mult, ALU.add).then_inc(S["o_ms"], 1)
                    dve.wait_ge(S["o_rs"], at("o_rs", t + 1))
                    for h in range(HEADS):
                        sl = slice(h * P, (h + 1) * P)
                        ins = dve.scalar_tensor_tensor(out=lnw[:, t, 512:1024][:, sl], in0=lnw[:, t, 0:512][:, sl],
                                                       scalar=ors[:, 4 * t + h:4 * t + h + 1], in1=nrmg[:, :],
                                                       op0=ALU.mult, op1=ALU.mult)
                    ins.then_inc(S["o_n"], 1)
                    dve.wait_ge(S["o_n"], at("o_n", t + 1))
                    dve.tensor_tensor(lnw[:, t, 512:1024], lnw[:, t, 512:1024], ggs[:, t, :], ALU.mult).then_inc(S["o_gated"], 1)

                def f5():
                    dve.wait_ge(S["o1_mm"], at("o1_mm", 1))
                    dve.wait_ge(S["q_s"], at("q_s", 1))
                    dve.tensor_tensor(lnw[:, 1, 0:512], gd(0, "at"), pt[:, 2, :], ALU.add).then_inc(S["o_raw"], 1)
                    o_gate(0)
                    o_gate(1)

                def branch_lo(first, n, k):
                    dve.wait_ge(S["o_hi"], at("o_hi", k))
                    dve.tensor_tensor(hlo[:, first:first + n, :], ot[:, first:first + n, :],
                                      hhi[:, first:first + n, :].bitcast(F32), ALU.subtract).then_inc(S["o_lo"], 1)

                def merge(b):
                    for t in range(NT):
                        for n in (0, 1):
                            q = 4 * b + 2 * t + n
                            if (t, n) == (1, 1):
                                dve.wait_ge(S["w_used"], at("w_used", U_M + BR0 + (1, 2, 4)[b]))
                            else:
                                dve.wait_ge(S["yb_mm"], at("yb_mm", 3 * b + 2 * t + n + 1))
                            g = gates[:, t, b * D + n * 512:b * D + (n + 1) * 512]
                            m = merged[:, t, n * 512:(n + 1) * 512]
                            if b == 0:
                                dve.wait_ge(S["gates"], at("gates", 1))
                                dve.wait_ge(S["zq_mm"], at("zq_mm", 1))
                                dve.tensor_tensor(m, pg[:, 2 * t + n, :], g, ALU.mult).then_inc(S["y_ev"], 1)
                            else:
                                dve.tensor_tensor(g, pg[:, 2 * t + n, :], g, ALU.mult).then_inc(S["y_ev"], 1)
                                dve.wait_ge(S["y_ev"], at("y_ev", q + 1))
                                ins = dve.tensor_tensor(m, m, g, ALU.add)
                                ins.then_inc(S["merged" if b == 2 else "merged1"], 1)

                def merged_lo(t):
                    dve.wait_ge(S["m_hi"], at("m_hi", t + 1))
                    dve.tensor_tensor(hlo[:, :, t * P:(t + 1) * P],
                                      pt[:, 2 * t:2 * t + 2, :].rearrange("p b (k s) -> p (b k) s", k=4),
                                      hhi[:, :, t * P:(t + 1) * P].bitcast(F32), ALU.subtract).then_inc(S["m_lo"], 1)

                tasks = {
                    "l2norm": qk_norm, "params": params, "rows": fox_bias, "fox_p": fox_softmax,
                    "sb_z": sb_z, "sb_r": sb_arg, "kv": lambda: (g_rows(0), g_rows(1)),
                    "dec0": lambda: g_mats(0), "dec1": lambda: (inv_start(0), g_mats(1)), "inv0": lambda: inv_start(1),
                    "f1": f1, "f2": f2, "f3": f3, "f4": f4, "f5": f5,
                    "o_split": lambda: branch_lo(0, 4, 1), "c_split": lambda: branch_lo(4, 4, 2),
                    "mrg": lambda: (merged_lo(0), merged_lo(1)),
                }
                for lv in range(1, 7):
                    tasks[f"mb{lv}"] = lambda lv=lv: (inv_step(lv), bv() if lv == 6 else None)

                def mixer():
                    n_ada = 0
                    pad()
                    for i in range(MIX_U):
                        u = U_M + i
                        if i > 0:
                            split(u + 1, 48 if i + 1 in (8, 9) else 2048)
                        if i == 1:
                            gate_bc(1, 1.0)
                        for task in TASKS.get((i, 0), ()):
                            if task in tasks:
                                tasks[task]()
                        if i in (1, 3, 5):
                            conv(i // 2)
                        if i == 7:
                            squares()
                        if i in (BR0, BR0 + 1, BR0 + 3):
                            merge({0: 0, 1: 1, 3: 2}[i - BR0])
                        for task in TASKS.get((i, 1), ()):
                            if task in tasks:
                                tasks[task]()
                        if i >= 2 and i % 2 == 0 and n_ada < ADA_N:
                            ada(ADA_N + n_ada, n_ada)
                            n_ada += 1
                        if i == 34:
                            mod_cols(False, at, 1, l * 24 + 8)
                    norm_stage(1, U_B)

                ffn(0, 0, U_A, 0, True)
                mixer()
                ffn(1, 2, U_B, 2 * ADA_N, False)


_INS = ["x", "c", "w_ada", "b_ada", "ln_g", "ln_b", "ffn_w_up", "ffn_w_down", "w_in", "b_forget", "conv_w",
        "gdn_a_log", "gdn_dt_bias", "gdn_norm_g", "w_branch", "w_o"]


def kernel(**inputs):
    import numpy as _np
    import concourse.bacc as _bacc
    from concourse import mybir as _mybir
    from concourse.bass_utils import run_bass_kernel_spmd as _run

    nc = _bacc.Bacc("TRN2", target_bir_lowering=False, num_devices=1)
    arrays, args = {}, []
    for name in _INS:
        a = _np.ascontiguousarray(inputs[name])
        arrays[f"in_{name}_dram"] = a
        args.append(nc.dram_tensor(f"in_{name}_dram", a.shape, _mybir.dt.from_np(a.dtype), kind="ExternalInput").ap())
    args.append(nc.dram_tensor("out_0_dram", inputs["x"].shape, _mybir.dt.float32, kind="ExternalOutput").ap())
    trunk(nc, *args)
    r = _run(nc, [arrays], core_ids=[0])
    return r.results[0]["out_0_dram"]
```

```python
import math
from contextlib import ExitStack

import concourse.bass as bass
from concourse import mybir

F32 = mybir.dt.float32
F32R = mybir.dt.float32r
ALU = mybir.AluOpType
ACT = mybir.ActivationFunctionType
AX = mybir.AxisListType
ds = bass.ds

P = 128
BIG = 1.0e30
LN_EPS = 1e-5
RMS_EPS = 1e-6

PER = {
    "raw_in0": 832, "raw_in1": 832, "raw_in2": 800, "raw_in3": 800, "x_affine": 6, "fold": 104, "ada_done": 36,
    "prm_in": 64, "ln_rows": 96, "acc_zero": 3, "acc_row": 48, "ada_in": 576, "ada_half": 20, "ln_rstd": 6,
    "x_gain": 6, "o_rs": 2, "h_f32a": 6, "h_hia": 6, "w_hi": 204, "up_silu": 44, "act_hi": 22, "mix_ev": 14,
    "conv": 12, "conv_silu": 3, "cv_sq": 2, "sp_exp": 1, "ea": 1, "beta_e": 1, "sp_ln": 1, "ssq_ln": 1,
    "ssq_exp": 1, "fox_exp": 2, "fox_pt": 2, "o_ab": 2, "sb_e": 1, "sb_l": 1, "sb_w": 1, "kv": 2, "egc": 1,
    "g_exp": 4, "dec": 1, "at": 2, "m1": 12, "gates": 1, "state": 1, "o_hi": 2, "o_ss": 2, "o_c": 1, "m_hi": 2,
    "w_used": 204, "ln_xt": 6, "mod_mm": 3, "gate_mm": 3, "up_mm": 22, "act_T": 22, "y_mm": 3, "ssq_mm": 1,
    "rows_mm": 1, "fox_mm": 2, "foxp_T": 1, "fox_pv": 1, "sb_mm": 2, "sb_cum": 1, "sb_pv": 1, "kv_T": 1,
    "gram_mm": 2, "at_T": 2, "m1_mm": 12, "m2_mm": 12, "vnew_mm": 2, "state_mm": 1, "o0_mm": 1, "zq_mm": 1,
    "yb_mm": 9, "o1_mm": 1, "o_T": 1, "merged_T": 2, "act_lo": 22, "act": 44, "mod_a": 6, "mod_cols": 3,
    "h_f32": 6, "h_hi": 6, "h_lo": 6, "w_lo": 204, "gate_bc": 3, "fold_dve": 80, "ln_gy": 6, "ln_sum": 6,
    "ln_bn": 12, "ln_mv": 6, "ln_var": 6, "ln_x": 6, "convw": 1, "pad": 1, "sp_arg": 4, "sp_abs": 1, "sp": 1,
    "lg": 4, "beta1": 1, "beta": 1, "lgu1": 4, "lgu": 4, "ccol": 1, "dec_arg": 1, "fox_b": 2, "qk_norm": 2,
    "fox_s": 2, "fox_max": 2, "fox_neg": 2, "fox_rec": 2, "fox_p": 2, "sb_z": 2, "sb_abs": 1, "sb_sp": 1,
    "sb_arg": 1, "g_gu": 2, "g_diff": 4, "g_em": 4, "g_a": 2, "g_mats": 2, "x_tmp": 4, "x_set": 2, "inv_x": 14,
    "ats": 12, "inv_m": 10, "bv": 1, "vnew": 3, "o_raw": 2, "o_lo": 2, "z_v": 1, "beta_n": 1, "rhs1": 1,
    "q_s": 1, "y_ev": 12, "o_ms": 2, "o_n": 2, "o_gated": 2, "merged1": 4, "merged": 4, "m_lo": 2,
}
OFF = {
    "rows_in": 64, "first_row": 16, "raw_in0": 64, "raw_in1": 64, "raw_in2": 96, "x_in": 16, "raw_in3": 96,
    "first_in": 64, "x_affine": 1, "fold": 16, "ada_done": 4, "acc_zero": 1, "sc_ready": 1, "h_f32a": 2,
    "h_hia": 2, "w_used": 4, "cols_T": 1, "ln_xt": 2, "mod_mm": 1, "cols": 1, "act_lo": 2, "act": 2,
    "fold_first": 56, "ada_first": 8, "mod_a": 1, "mod_cols": 1, "h_f32": 2, "h_hi": 2, "h_lo": 2,
}


def trunk(nc, x_in, c_in, w_ada, b_ada, ln_g, ln_b, w_up, w_down, w_in, b_forget, conv_w,
          a_log, dt_bias, norm_g, w_branch, w_o, out):
    _, SEQ, D = x_in.shape
    DEPTH = w_in.shape[0]
    HID = w_down.shape[2]
    TAPS = conv_w.shape[1]
    NT = SEQ // P
    KD = D // P
    KH = HID // P
    CW = 256
    NCH = HID // CW
    HEADS = 4
    DH = 64
    FOX_W = SB_W = HEADS * DH
    GW = HEADS * P
    SCALE = DH ** -0.5
    ALPHA = (2.0 * DEPTH) ** 0.25
    assert NT == 2 and KD == 8 and NCH * CW == HID and TAPS == 4

    C_FQ, C_FK, C_FV = 0, FOX_W, 2 * FOX_W
    C_FF = 3 * FOX_W
    C_SQ = C_FF + HEADS
    C_SK, C_SV = C_SQ + SB_W, C_SQ + 2 * SB_W
    C_GQ = C_SQ + 3 * SB_W
    C_GB = C_GQ + 3 * GW
    C_GG = C_GB + 2 * HEADS
    C_BG = C_GG + GW

    UP_U, DOWN_U = 2 * NCH, NCH
    FFN_U = UP_U + DOWN_U
    MIX_CH = 14
    BR0 = 2 * MIX_CH
    MIX_U = BR0 + 8
    U_A, U_M, U_B = 0, FFN_U, FFN_U + MIX_U
    UNITS = 2 * FFN_U + MIX_U
    assert UNITS % 2 == 0
    PAIRS = (NCH - 1) // 2
    assert 2 * PAIRS + 1 == NCH
    ADA_N = 12
    ADA_C = 3 * D // ADA_N
    POOL_FIRST = [3, 6, 9, 11]
    FIRST_SLOT = [0, 1, 2, 3, 4, 0, 1, 2, 3, 4, 2, 3]
    FIRST_SEM = ["raw_in0", "raw_in1", "raw_in2", "raw_in3", "first_in"]
    FIRST_USE = [FIRST_SLOT[:i + 1].count(FIRST_SLOT[i]) for i in range(ADA_N)]
    DVE_FIRST = [i for i in range(ADA_N) if i not in POOL_FIRST]

    ctx = ExitStack()
    with ctx:
        def sb(name, shape, dt=F32, where=None):
            return (where or ctx).enter_context(nc.sbuf_tensor(name, shape, dt))

        with ExitStack() as landing:
            wraw = sb("wraw", [P, 4, 2048], F32, landing)
        wlo = sb("wlo", [P, 4, 2048], F32R)
        whi = sb("whi", [P, 4, 1024], F32R)
        aw = sb("aw", [P, 2048])
        hhi = sb("hhi", [P, KD, SEQ], F32R)
        hlo = sb("hlo", [P, KD, SEQ], F32R)
        x = sb("x", [P, NT, D])
        lnw = sb("lnw", [P, NT, D])
        acc = sb("acc", [P, 3 * D])
        gatebc = sb("gatebc", [P, D])
        lnbc = sb("lnbc", [P, 2, D])
        ident = sb("ident", [P, P])
        tri1 = sb("tri1", [P, 2, P])
        trid = sb("trid", [P, P])
        foxm = sb("foxm", [P, 2, P])
        sbm = sb("sbm", [P, 2, P])
        strict = sb("strict", [P, P])
        incl_t = sb("incl_t", [P, P])
        lev_t = sb("lev_t", [P, 7, P])
        lev1 = sb("lev1", [P, P])
        cols = sb("cols", [P, 192])
        sc = sb("sc", [P, KD])
        modab = sb("modab", [P, 2, KD])
        modt = sb("modt", [P, KD])
        stats = sb("stats", [P, NT, 2, 6])
        mv = sb("mv", [P, NT, 2])
        var = sb("var", [P, NT])
        rstd = sb("rstd", [P, NT])
        mhalf = sb("mhalf", [P, 8])
        epsc = sb("epsc", [P, 1])
        prm = sb("prm", [P, 12])
        nrmg = sb("nrmg", [P, P])

        with ExitStack() as ffn_mem:
            athi = sb("athi", [P, KH, SEQ], F32R, ffn_mem)
            atlo = sb("atlo", [P, KH, SEQ], F32R, ffn_mem)
            sg = sb("sg", [P, NT, CW], F32, ffn_mem)
            act_t = sb("act_t", [P, NT, CW], F32, ffn_mem)
        gates = sb("gates", [P, NT, 3 * D])
        cv = sb("cv", [P, 12, SEQ])
        att = sb("att", [P, 6, 512])
        ggs = sb("ggs", [P, NT, 512])
        kn = sb("kn", [P, HEADS, P])
        vn = sb("vn", [P, NT, HEADS, P])
        ot = sb("ot", [P, KD, SEQ])
        scr = sb("scr", [P, 4096])
        sm = sb("sm", [P, NT, 12])
        sp_a = sb("sp_a", [P, NT, 8])
        sp_b = sb("sp_b", [P, NT, 8])
        sp_c = sb("sp_c", [P, NT, 8])
        lg = sb("lg", [P, NT, 8])
        ea = sb("ea", [P, HEADS])
        beta = sb("beta", [P, NT, HEADS])
        beta_t = sb("beta_t", [P, NT, HEADS])
        ccol = sb("ccol", [P, 4, HEADS])
        fmax = sb("fmax", [P, 8])
        fneg = sb("fneg", [P, 8])
        fsum = sb("fsum", [P, 8])
        frec = sb("frec", [P, 8])
        egc = sb("egc", [P, HEADS])
        dec = sb("dec", [P, HEADS])
        dtmp = sb("dtmp", [P, HEADS])
        oss = sb("oss", [P, 8])
        ors = sb("ors", [P, 8])
        convw = sb("convw", [P, TAPS * 12])

        pg = ctx.enter_context(nc.psum_tensor("pg", [P, 4, 512], F32))
        pt = ctx.enter_context(nc.psum_tensor("pt", [P, 4, 512], F32))

        qkt = att[:, 0:4, :].rearrange("p a (b s) -> p a b s", b=2)
        val = att[:, 4:6, :]
        ones = tri1[:, 1, :]
        tri = tri1[:, 0, :]
        merged = cv[:, 0:8, :].rearrange("p (t a) s -> p t (a s)", t=NT)

        def pro_slot(slot):
            return wraw[:, slot, :] if slot < 4 else aw[:, :]

        S = {name: ctx.enter_context(nc.semaphore("s_" + name)) for name in
             [*sorted(PER | OFF), "fills", "masks", "masks_done", "out"]}

        def counter(l):
            def at(name, k=1):
                return k if l is None else l * PER.get(name, 0) + (OFF.get(name, 0) + k)
            return at

        def alone(eng, name, value):
            value = eng.snap(eng.to_reg(value))
            eng.wait_ge(S[name], 0)
            return value

        block = ctx.enter_context(nc.Block())

        @block.sync
        def _(sp):

            def pair(dst, src, name):
                for d, s in zip(dst, src):
                    sp.dma_start(d, s).then_inc(S[name], 16)

            sp.dma_start(lnw[0:8, 0, 384:512], c_in.rearrange("b (k p) -> (b k) p", p=P)).then_inc(S["rows_in"], 16)
            sp.dma_start(lnw[0:48, 0, 0:128], ln_g.rearrange("l s (k p) -> (l s k) p", p=P)).then_inc(S["rows_in"], 16)
            sp.dma_start(lnw[0:48, 0, 128:256], ln_b.rearrange("l s (k p) -> (l s k) p", p=P)).then_inc(S["rows_in"], 16)
            sp.dma_start(lnw[0:96, 0, 256:384], conv_w.rearrange("l t (c p) -> (l t c) p", p=P)).then_inc(S["rows_in"], 16)
            sp.wait_ge(S["acc_zero"], 1)
            sp.dma_start(acc[0:1, :], b_ada[0:1, 0:3 * D]).then_inc(S["first_row"], 16)

            def ada_dst(slot):
                r = pro_slot(slot).rearrange("p (k c) -> p k c", k=KD)
                return [r[:, 0:4, :], r[:, 4:8, :]]

            for i in range(ADA_N):
                before = [k for k in range(i) if FIRST_SLOT[k] == FIRST_SLOT[i]][-1:]
                if before and before[0] in POOL_FIRST:
                    sp.wait_ge(S["ada_done"], POOL_FIRST.index(before[0]) + 1)
                elif before:
                    sp.wait_ge(S["ada_first"], DVE_FIRST.index(before[0]) + 1)
                w = w_ada[0, :, i * ADA_C:(i + 1) * ADA_C].rearrange("(k p) c -> p k c", p=P)
                pair(ada_dst(FIRST_SLOT[i]), [w[:, 0:4, :], w[:, 4:8, :]], FIRST_SEM[FIRST_SLOT[i]])
                if i == 2:
                    sp.dma_start(x[:, :, :], x_in[0].rearrange("(t p) d -> p t d", p=P)).then_inc(S["x_in"], 16)

            with sp.Fori(0, DEPTH) as l:
                at = counter(l)

                def w_view(slot, k):
                    return wraw[:, slot, :].rearrange("p (k c) -> p k c", k=k)

                def free(u):
                    before = u - 4 if u >= UNITS % 4 else u - UNITS % 4
                    sp.wait_ge(S["w_used"], alone(sp, "w_used", at("w_used", 2 * before + 2)))

                def rows(w, u, r0):
                    free(u)
                    d = w_view(u % 4, 2)
                    pair([d[:, 0, :], d[:, 1, :]],
                         [w[ds(l, 1), r0 + k * P:r0 + (k + 1) * P, :].rearrange("a p c -> (a p) c")
                          for k in (0, 1)], f"raw_in{u % 4}")

                def up_unit(f, u, j, ui):
                    d = w_view(u % 4, 4)
                    src = []
                    for half in (0, 1):
                        w = w_up[ds(l, 1), f, ui * 512:(ui + 1) * 512, ds(half * HID + j * CW, CW)]
                        src.append(w.rearrange("a (k p) c -> p (a k) c", p=P))
                    pair([d[:, :, 0:CW], d[:, :, CW:2 * CW]], src, f"raw_in{u % 4}")

                def ffn(f, u0):
                    sp.wait_ge(S["ada_first"], DVE_FIRST.index(5) + 1)
                    sp.wait_ge(S["ada_done"], POOL_FIRST.index(6) + 1)
                    for ui in (0, 1):
                        free(u0 + ui)
                        up_unit(f, u0 + ui, 0, ui)
                    sp.wait_ge(S["ada_done"], len(POOL_FIRST))
                    sp.wait_ge(S["ada_first"], len(DVE_FIRST))
                    with sp.Fori(0, PAIRS) as j:
                        for c in (1, 2):
                            for ui in (0, 1):
                                u = u0 + 2 * c + ui
                                sp.wait_ge(S["w_used"], alone(sp, "w_used", l * PER["w_used"] + j * 8 + (OFF["w_used"] + 2 * u - 6)))
                                up_unit(f, u, j * 2 + c, ui)
                    for d in range(DOWN_U):
                        rows(w_down[:, f], u0 + UP_U + d, d * 2 * P)

                def two(u, w, c0, c1):
                    free(u)
                    d = w_view(u % 4, 4)
                    r = w.rearrange("a (k p) c -> p (a k) c", p=P)
                    pair([d[:, :, 0:256], d[:, :, 256:512]], [r[:, :, c0:c0 + 256], r[:, :, c1:c1 + 256]],
                         f"raw_in{u % 4}")

                def mixer():
                    starts = [(C_GG, C_GG + 256), (C_GQ, C_GQ + 256), (C_GQ + GW, C_GQ + GW + 256),
                              (C_GQ + 2 * GW, C_GQ + 2 * GW + 256), None, (C_FQ, C_FK), (C_FV, C_SV), (C_SQ, C_SK)]
                    starts += [(C_BG + 512 * g, C_BG + 512 * g + 256) for g in range(6)]
                    for i in range(MIX_U):
                        u = U_M + i
                        if i < BR0:
                            w = w_in[ds(l, 1), (i % 2) * 512:(i % 2 + 1) * 512, :]
                            if starts[i // 2]:
                                two(u, w, *starts[i // 2])
                            else:
                                free(u)
                                d = wraw[:, u % 4, 0:48].rearrange("p (k c) -> p k c", k=4)
                                r = w.rearrange("a (k p) c -> p (a k) c", p=P)
                                pair([d[:, :, 0:4], d[:, :, 4:12]],
                                     [r[:, :, C_FF:C_FF + HEADS], r[:, :, C_GB:C_GB + 2 * HEADS]], f"raw_in{u % 4}")
                        elif i < BR0 + 4:
                            rows(w_branch, u, (i - BR0) * 2 * P)
                        else:
                            rows(w_o, u, (i - BR0 - 4) * 2 * P)

                ffn(0, U_A)
                mixer()
                ffn(1, U_B)

            at = counter(None)
            sp.wait_ge(S["x_affine"], OFF["x_affine"] + DEPTH * PER["x_affine"])
            sp.dma_start(out[0].rearrange("(t p) d -> p t d", p=P), x[:, :, :]).then_inc(S["out"], 16)
            sp.wait_ge(S["out"], 16)

        @block.gpsimd
        def _(pool):
            pool.memset(ident[:, :], 0.0).then_inc(S["fills"], 1)
            pool.wait_ge(S["fills"], 1)
            pool.affine_select(out=ident[:, :], in_=ident[:, :], pattern=[[-1, P]], compare_op=ALU.not_equal, fill=1.0,
                               base=0, channel_multiplier=1).then_inc(S["masks"], 1)
            pool.memset(mhalf[:, :], -0.5).then_inc(S["fills"], 1)
            pool.memset(epsc[:, :], 0.0).then_inc(S["x_affine"], 1)
            pool.wait_ge(S["x_affine"], 1)
            for t, v in ((tri1[:, :, :], 1.0), (trid[:, :], 1.0), (foxm[:, :, :], 0.0),
                         (sbm[:, :, :], 0.0), (strict[:, :], 1.0), (incl_t[:, :], 1.0), (lev_t[:, :, :], 0.0),
                         (lev1[:, :], 0.0)):
                pool.memset(t, v).then_inc(S["fills"], 1)
            pool.wait_ge(S["fills"], 10)

            def sel(ap, op, fill, base, pattern, cm):
                return pool.affine_select(out=ap, in_=ap, pattern=pattern, compare_op=op, fill=fill, base=base,
                                          channel_multiplier=cm).then_inc(S["masks"], 1)
            sel(tri, ALU.is_ge, 0.0, 0, [[1, P]], -1)
            sel(trid[:, :], ALU.is_ge, 0.0, 0, [[-1, P]], 1)
            sel(foxm[:, 1, :], ALU.is_ge, BIG, 0, [[-1, P]], 1)
            sel(sbm[:, 0, :], ALU.is_gt, -BIG, 0, [[1, P]], -1)
            sel(strict[:, :], ALU.is_gt, 0.0, 0, [[-1, P]], 1)
            sel(incl_t[:, :], ALU.is_ge, 0.0, 0, [[1, P]], -1)
            n = 7
            for lv in range(7):
                s = 1 << lv
                v = lev_t[:, lv, :].rearrange("p (b u r) -> p b u r", u=2, r=s)[:, :, 1, :]
                pool.memset(v, 1.0).then_inc(S["fills"], 1)
            v1 = lev1[:, :].rearrange("p (b u) -> p b u", u=2)[:, :, 0]
            pool.memset(v1, 1.0).then_inc(S["fills"], 1)
            pool.wait_ge(S["fills"], 18)
            for lv in range(7):
                s = 1 << lv
                nb = P // (2 * s)
                v = lev_t[:, lv, :].rearrange("p (b u r) -> p b u r", u=2, r=s)[:, :, 1, :]
                sel(v, ALU.is_ge, 0.0, 0, [[-2 * s, nb], [0, s]], 1)
                n += 1
                pool.wait_ge(S["masks"], n)
                sel(v, ALU.is_ge, 0.0, s - 1, [[2 * s, nb], [0, s]], -1)
                n += 1
            sel(v1, ALU.is_equal, 0.0, -1, [[-2, P // 2]], 1)
            n += 1
            pool.wait_ge(S["masks"], n)
            pool.memset(epsc[:, :], RMS_EPS).then_inc(S["masks_done"], 1)

            def fold(src, a, at, n):
                r = src.rearrange("p (k c) -> p k c", k=KD)
                pool.tensor_tensor(r, r, sc[:, :].unsqueeze(2).broadcast_to((P, KD, ADA_C)), ALU.mult).then_inc(S["fold"], 1)
                for m, k in enumerate((4, 2, 1)):
                    pool.wait_ge(S["fold"], alone(pool, "fold", at("fold", n + m + 1)))
                    pool.tensor_tensor(r[:, 0:k, :], r[:, 0:k, :], r[:, k:2 * k, :], ALU.add).then_inc(S["fold"], 1)
                pool.wait_ge(S["fold"], alone(pool, "fold", at("fold", n + 4)))
                pool.tensor_tensor(a, a, r[:, 0, :], ALU.add).then_inc(S["ada_done"], 1)
                return n + 4

            def half_fold(at, n):
                r = aw[:, :].rearrange("p (k c) -> p k c", k=KD)[:, 4:8, :]
                pool.tensor_tensor(r, r, sc[:, 4:8].unsqueeze(2).broadcast_to((P, 4, ADA_C)), ALU.mult).then_inc(S["fold"], 1)
                pool.wait_ge(S["fold"], alone(pool, "fold", at("fold", n + 1)))
                pool.tensor_tensor(r[:, 0:2, :], r[:, 0:2, :], r[:, 2:4, :], ALU.add).then_inc(S["fold"], 1)
                pool.wait_ge(S["fold"], alone(pool, "fold", at("fold", n + 2)))
                pool.tensor_tensor(r[:, 0, :], r[:, 0, :], r[:, 1, :], ALU.add).then_inc(S["ada_half"], 1)
                return n + 2

            w0 = counter(None)
            pool.wait_ge(S["sc_ready"], 1)
            pool.wait_ge(S["first_row"], 16)
            for n, i in enumerate(POOL_FIRST):
                pool.wait_ge(S[FIRST_SEM[FIRST_SLOT[i]]], 32 * FIRST_USE[i])
                fold(pro_slot(FIRST_SLOT[i]), acc[:, i * ADA_C:(i + 1) * ADA_C], w0, 4 * n)

            with pool.Fori(0, DEPTH) as l:
                at = counter(l)

                def ada(s, n):
                    nl, ns = (1 - l, 0) if s == 2 else (l, s + 1)
                    pool.wait_ge(S["acc_zero"], alone(pool, "acc_zero", at("acc_zero", s + 1)))
                    pool.dma_start(acc[0:1, :], b_ada[ds(nl, 1), ns * 3 * D:(ns + 1) * 3 * D]).then_inc(S["acc_row"], 16)
                    for j in range(ADA_N):
                        idx = s * ADA_N + j
                        pool.wait_ge(S["ada_done"], alone(pool, "ada_done", at("ada_done", idx)))
                        c0 = ns * 3 * D + j * ADA_C
                        w = w_ada[ds(nl, 1), :, c0:c0 + ADA_C].rearrange("a (k p) c -> p (a k) c", p=P)
                        r = aw[:, :].rearrange("p (k c) -> p k c", k=KD)
                        pool.dma_start(r, w).then_inc(S["ada_in"], 16)
                        if j == 0:
                            pool.wait_ge(S["acc_row"], alone(pool, "acc_row", at("acc_row", 16 * (s + 1))))
                        pool.wait_ge(S["ada_in"], alone(pool, "ada_in", at("ada_in", 16 * (idx + 1))))
                        if s != 1 and j < 2 * PAIRS:
                            n = half_fold(at, n)
                        else:
                            n = fold(aw[:, :], acc[:, j * ADA_C:(j + 1) * ADA_C], at, n)
                    return n

                def ln_rows(s):
                    pool.wait_ge(S["x_affine"], alone(pool, "x_affine", at("x_affine", NT * s)))
                    for n, src in enumerate((ln_g, ln_b)):
                        pool.dma_start(lnbc[:, n, :], src[ds(l, 1), s, :].broadcast_to((P, D))).then_inc(S["ln_rows"], 16)

                def norm_rest(s):
                    for t in range(NT):
                        pool.wait_ge(S["ln_var"], alone(pool, "ln_var", at("ln_var", NT * s + t + 1)))
                        pool.tensor_tensor(rstd[:, t:t + 1], var[:, t:t + 1], mhalf[:, 0:1], ALU.pow).then_inc(S["ln_rstd"], 1)
                    for t in range(NT):
                        pool.wait_ge(S["ln_xt"], alone(pool, "ln_xt", at("ln_xt", NT * s + t + 1)))
                        pool.wait_ge(S["ln_rows"], alone(pool, "ln_rows", at("ln_rows", 32 * (s + 1))))
                        pool.tensor_tensor(x[:, t, :], x[:, t, :], lnbc[:, 0, :], ALU.mult).then_inc(S["x_gain"], 1)
                        pool.wait_ge(S["x_gain"], alone(pool, "x_gain", at("x_gain", NT * s + t + 1)))
                        pool.tensor_tensor(x[:, t, :], x[:, t, :], lnbc[:, 1, :], ALU.add).then_inc(S["x_affine"], 1)

                def clear(s):
                    pool.wait_ge(S["gate_mm"], alone(pool, "gate_mm", at("gate_mm", s + 1)))
                    pool.memset(acc[:, :], 0.0).then_inc(S["acc_zero"], 1)

                pool.dma_start(prm[:, 0:4], b_forget[ds(l, 1), :].broadcast_to((P, HEADS))).then_inc(S["prm_in"], 16)
                pool.dma_start(prm[:, 4:8], dt_bias[ds(l, 1), :].broadcast_to((P, HEADS))).then_inc(S["prm_in"], 16)
                pool.dma_start(prm[:, 8:12], a_log[ds(l, 1), :].broadcast_to((P, HEADS))).then_inc(S["prm_in"], 16)
                pool.dma_start(nrmg[:, :], norm_g[ds(l, 1), :].broadcast_to((P, P))).then_inc(S["prm_in"], 16)
                ln_rows(0)
                clear(0)
                steps = ada(0, 0)
                norm_rest(0)
                ln_rows(1)
                clear(1)
                steps = ada(1, steps)
                for t in range(NT):
                    pool.wait_ge(S["o_ms"], alone(pool, "o_ms", at("o_ms", t + 1)))
                    pool.tensor_tensor(ors[:, 4 * t:4 * t + 4], oss[:, 4 * t:4 * t + 4], mhalf[:, 0:4], ALU.pow).then_inc(S["o_rs"], 1)
                norm_rest(1)
                ln_rows(2)
                clear(2)
                ada(2, steps)
                norm_rest(2)

        GD = {"x": 0, "xt": 1, "at": 2, "ats": 3, "m": 4, "it": 5}

        def gd(t, name):
            k = GD[name]
            return att[:, k, :] if t == 0 else scr[:, k * 512:(k + 1) * 512]

        TASKS = {
            (4, 0): ["tap00"], (4, 1): ["tap01"], (5, 0): ["tap02"], (5, 1): ["tap03", "silu0"],
            (6, 0): ["tap10"], (6, 1): ["tap11"], (7, 0): ["tap12"], (7, 1): ["tap13", "silu1"],
            (8, 0): ["tap20"], (8, 1): ["tap21"], (9, 0): ["tap22"], (9, 1): ["tap23", "silu2"],
            (10, 0): ["squares"], (10, 1): ["l2norm", "params"], (11, 1): ["l2_ln", "params2"],
            (12, 0): ["rows", "l2_exp"], (12, 1): ["qk_norm"],
            (13, 0): ["fox_p"], (14, 0): ["fox_T"], (15, 0): ["fox_o"],
            (22, 0): ["sig"], (16, 0): ["sb_z", "sb_l"], (16, 1): ["sb_sp"], (17, 1): ["sb_r"], (18, 1): ["sb_o", "kv"],
            (19, 0): ["dec0"], (19, 1): ["dec1"], (20, 0): ["inv0"],
            (26, 1): ["f1"], (27, 0): ["f2"], (27, 1): ["o_split"],
            (28, 0): ["f3"], (28, 1): ["f4"], (29, 0): ["f5"], (29, 1): ["oT", "c_split"], (31, 1): ["mrg"],
        }
        slot = (20, 1)
        for lv in range(1, 7):
            for half in ("ma", "mb"):
                TASKS.setdefault(slot, []).append(f"{half}{lv}")
                slot = (slot[0], 1) if slot[1] == 0 else (slot[0] + 1, 0)
        assert slot <= (26, 1), slot

        @block.scalar
        def _(act):
            act.wait_ge(S["cols_T"], 1)
            act.activation(sc[:, :], pt[:, 0, 192:200], ACT.Silu).then_inc(S["sc_ready"], 1)

            def modulate(at, k, t):
                act.wait_ge(S["mod_cols"], at("mod_cols", k + 1))
                act.wait_ge(S["ln_xt"], at("ln_xt", NT * k + t + 1))
                for c in range(KD // 2):
                    ins = act.activation(lnw[:, t, c * P:(c + 1) * P], pt[:, 2 * t, c * P:(c + 1) * P],
                                         ACT.Identity, bias=modab[:, 1, c:c + 1], scale=modab[:, 0, c:c + 1])
                ins.then_inc(S["h_f32a"], 1)
                act.wait_ge(S["h_f32a"], at("h_f32a", NT * k + t + 1))
                act.activation(hhi[:, 0:KD // 2, t * P:(t + 1) * P],
                               lnw[:, t, 0:512].rearrange("p (k s) -> p k s", k=KD // 2), ACT.Copy).then_inc(S["h_hia"], 1)

            w0 = counter(None)
            for t in range(NT):
                modulate(w0, 0, t)

            with act.Fori(0, DEPTH) as l:
                at = counter(l)

                def split(h, size=1024):
                    s, o = h // 2 % 4, h % 2 * size
                    act.wait_ge(S[f"raw_in{s}"], at(f"raw_in{s}", 32 * (h // 8 + 1)))
                    act.wait_ge(S["w_used"], at("w_used", h - 3))
                    act.activation(whi[:, h % 4, 0:size], wraw[:, s, o:o + size], ACT.Copy).then_inc(S["w_hi"], 1)

                def split_j(h, j):
                    s, o = h // 2 % 4, h % 2 * 1024
                    act.wait_ge(S[f"raw_in{s}"], l * PER[f"raw_in{s}"] + j * 32
                                + (OFF[f"raw_in{s}"] + 32 * (h // 8 + 1)))
                    act.wait_ge(S["w_used"], l * PER["w_used"] + j * 8 + (OFF["w_used"] + h - 3))
                    act.activation(whi[:, h % 4, :], wraw[:, s, o:o + 1024], ACT.Copy).then_inc(S["w_hi"], 1)

                def silu(f, u0, t, c, j=None):
                    name, step, k = (("up_mm", 2, f * NCH + c + 1), ("w_used", 8, 2 * u0 + 4 * c + 4))[t]
                    if j is None:
                        act.wait_ge(S[name], at(name, k))
                    else:
                        act.wait_ge(S[name], l * PER.get(name, 0) + j * step + (OFF.get(name, 0) + k))
                    act.activation(sg[:, t, :], pg[:, 2 * (c % 2) + t, 0:CW], ACT.Silu).then_inc(S["up_silu"], 1)

                def act_hi(f, c, j=None):
                    src = pt[:, c % 2, :].rearrange("p (k s) -> p k s", k=2)
                    if j is None:
                        act.wait_ge(S["act_T"], at("act_T", f * NCH + c + 1))
                        act.activation(athi[:, 2 * c:2 * c + 2, :], src, ACT.Copy).then_inc(S["act_hi"], 1)
                    else:
                        act.wait_ge(S["act_T"], alone(act, "act_T", l * PER["act_T"] + j * 2 + (f * NCH + c + 1)))
                        act.activation(athi[:, ds(j * 4 + 2 * c, 2), :], src, ACT.Copy).then_inc(S["act_hi"], 1)

                def ffn(f, s, u0, first):
                    h0 = 2 * u0
                    for h in range(0 if first else 3, 7):
                        split(h0 + h)
                    with act.Fori(0, PAIRS) as j:
                        for c in (1, 2):
                            silu(f, u0, 0, c - 1, j)
                            silu(f, u0, 1, c - 1, j)
                            split_j(h0 + 4 * c + 3, j)
                            split_j(h0 + 4 * c + 4, j)
                            split_j(h0 + 4 * c + 5, j)
                            act_hi(f, c - 1, j)
                            split_j(h0 + 4 * c + 6, j)
                    silu(f, u0, 0, NCH - 1)
                    silu(f, u0, 1, NCH - 1)
                    for h in range(4 * NCH + 3, 2 * FFN_U + (3 if s == 0 else 0)):
                        split(h0 + h)
                        if h == 4 * NCH + 5:
                            act_hi(f, NCH - 1)
                    norm_stage(s)

                def norm_stage(s):
                    for t in range(NT):
                        modulate(at, s, t)

                def g_row(a):
                    return a.rearrange("p (h s) -> p h s", h=HEADS)

                def evac(k):
                    b = 2 * (k % 2)
                    act.wait_ge(S["w_used"], at("w_used", 2 * (U_M + 2 * k + 2)))
                    two = pg[:, b:b + 2, :]
                    if k in (1, 2, 3):
                        if k > 1:
                            act.wait_ge(S["conv"], at("conv", 4 * (k - 1)))
                        act.wait_ge(S["pad"], at("pad", 1))
                        pre = scr[:, 0:4 * 260].rearrange("p (c s) -> p c s", c=4)
                        ins = act.activation(pre[:, :, 4:260], two.rearrange("p b (c s) -> p (b c) s", c=2), ACT.Copy)
                    elif k == 0:
                        ins = act.activation(ggs[:, :, :], two, ACT.Silu)
                    elif k == 4:
                        ins = act.activation(sm[:, :, :], pg[:, b:b + 2, 0:12], ACT.Copy)
                    elif k == 6:
                        ins = act.activation(val, two, ACT.Copy)
                    elif k in (5, 7):
                        a = 0 if k == 5 else 2
                        ins = act.activation(att[:, a:a + 2, :], two, ACT.Copy)
                    else:
                        ins = act.activation(gates[:, :, (k - 8) * 512:(k - 7) * 512], two,
                                             ACT.Copy if k < 10 else ACT.Sigmoid)
                    ins.then_inc(S["mix_ev"], 1)

                def conv_silu(k):
                    act.wait_ge(S["conv"], at("conv", 4 * k + 4))
                    act.activation(cv[:, 4 * k:4 * k + 4, :],
                                   scr[:, 1040:2064].rearrange("p (c s) -> p c s", c=4), ACT.Silu).then_inc(S["conv_silu"], 1)

                def conv_first(k):
                    act.wait_ge(S["mix_ev"], at("mix_ev", k + 2))
                    act.wait_ge(S["convw"], at("convw", 1))
                    if k:
                        act.wait_ge(S["conv_silu"], at("conv_silu", k))
                    pre = scr[:, 0:1040].rearrange("p (c s) -> p c s", c=4)
                    res = scr[:, 1040:2064].rearrange("p (c s) -> p c s", c=4)
                    for c in range(4):
                        ins = act.activation(res[:, c, :], pre[:, c, 1:1 + SEQ], ACT.Copy,
                                             scale=convw[:, 4 * k + c:4 * k + c + 1])
                    ins.then_inc(S["conv"], 1)

                def squares():
                    act.wait_ge(S["conv_silu"], at("conv_silu", 3))
                    src = cv[:, 0:8, :].rearrange("p c s -> p (c s)")
                    for n in (0, 1):
                        act.activation(scr[:, n * 1024:(n + 1) * 1024], src[:, n * 1024:(n + 1) * 1024], ACT.Square).then_inc(S["cv_sq"], 1)

                def l2_ln():
                    act.wait_ge(S["ssq_mm"], at("ssq_mm", 1))
                    act.activation(scr[:, 2048:4096], pt[:, :, :].rearrange("p b s -> p (b s)"), ACT.Ln,
                                   bias=epsc[:, 0:1]).then_inc(S["ssq_ln"], 1)

                def l2_exp():
                    act.wait_ge(S["ssq_ln"], at("ssq_ln", 1))
                    act.activation(scr[:, 2048:4096], scr[:, 2048:4096], ACT.Exp, scale=-0.5).then_inc(S["ssq_exp"], 1)

                def params():
                    act.wait_ge(S["sp_abs"], at("sp_abs", 1))
                    act.activation(sp_b[:, :, :], sp_b[:, :, :], ACT.Exp, scale=-1.0).then_inc(S["sp_exp"], 1)
                    act.wait_ge(S["prm_in"], at("prm_in", 64))
                    act.activation(ea[:, :], prm[:, 8:12], ACT.Exp).then_inc(S["ea"], 1)
                    act.activation(beta_t[:, :, :], sm[:, :, 4:8], ACT.Exp, scale=-1.0).then_inc(S["beta_e"], 1)
                    act.wait_ge(S["sp_exp"], at("sp_exp", 1))
                    act.activation(sp_b[:, :, :], sp_b[:, :, :], ACT.Ln, bias=1.0).then_inc(S["sp_ln"], 1)

                def fox_exp():
                    for t in range(NT):
                        n = P * (t + 1)
                        act.wait_ge(S["fox_neg"], at("fox_neg", t + 1))
                        for h in range(HEADS):
                            a = fox_s(t)[:, h, :]
                            ins = act.activation(a, a, ACT.Exp, bias=fneg[:, 4 * t + h:4 * t + h + 1],
                                                 accum_out=fsum[:, 4 * t + h:4 * t + h + 1])
                        ins.then_inc(S["fox_exp"], 1)

                def fox_pt():
                    act.wait_ge(S["foxp_T"], at("foxp_T", 1))
                    act.activation(scr[:, 1536:2560], pt[:, 0:2, :].rearrange("p b s -> p (b s)"), ACT.Copy).then_inc(S["fox_pt"], 1)
                    act.activation(scr[:, 2560:3072], pt[:, 2, :], ACT.Copy).then_inc(S["fox_pt"], 1)

                def fox_o():
                    act.wait_ge(S["fox_pv"], at("fox_pv", 1))
                    act.activation(ot[:, 0:2, :], pt[:, 3, :].rearrange("p (k s) -> p k s", k=2), ACT.Copy).then_inc(S["o_ab"], 1)

                def sb_exp():
                    act.wait_ge(S["sb_abs"], at("sb_abs", 1))
                    act.activation(scr[:, 1536:3072], scr[:, 1536:3072], ACT.Exp, scale=-1.0).then_inc(S["sb_e"], 1)

                def sb_ln():
                    act.wait_ge(S["sb_e"], at("sb_e", 1))
                    act.activation(scr[:, 1536:3072], scr[:, 1536:3072], ACT.Ln, bias=1.0).then_inc(S["sb_l"], 1)

                def sb_w():
                    act.wait_ge(S["sb_arg"], at("sb_arg", 1))
                    act.activation(scr[:, 0:1536], scr[:, 0:1536], ACT.Exp).then_inc(S["sb_w"], 1)

                def sb_o():
                    act.wait_ge(S["sb_pv"], at("sb_pv", 1))
                    act.activation(ot[:, 2:4, :], pt[:, 3, :].rearrange("p (k s) -> p k s", k=2), ACT.Copy).then_inc(S["o_ab"], 1)

                def kv():
                    act.wait_ge(S["kv_T"], at("kv_T", 1))
                    act.activation(kn[:, :, :], g_row(pt[:, 0, :]), ACT.Copy).then_inc(S["kv"], 1)
                    act.activation(vn[:, :, :, :].rearrange("p t h s -> p (t h s)"),
                                   pt[:, 1:3, :].rearrange("p b s -> p (b s)"), ACT.Copy).then_inc(S["kv"], 1)
                    act.wait_ge(S["ccol"], at("ccol", 1))
                    act.activation(egc[:, :], ccol[:, 3, :], ACT.Exp).then_inc(S["egc"], 1)

                def decays(t):
                    act.wait_ge(S["g_diff"], at("g_diff", 2 * t + 1))
                    act.activation(gd(t, "ats"), gd(t, "ats"), ACT.Exp, scale=-1.0).then_inc(S["g_exp"], 1)
                    act.wait_ge(S["g_diff"], at("g_diff", 2 * t + 2))
                    act.activation(gd(t, "it"), gd(t, "it"), ACT.Exp).then_inc(S["g_exp"], 1)
                    if t == 0:
                        act.wait_ge(S["dec_arg"], at("dec_arg", 1))
                        act.activation(dec[:, :], dtmp[:, :], ACT.Exp).then_inc(S["dec"], 1)

                def at_copy(t):
                    act.wait_ge(S["at_T"], at("at_T", t + 1))
                    act.activation(gd(t, "at"), pt[:, 3, :], ACT.Copy).then_inc(S["at"], 1)

                def m1_copy(lv, t):
                    act.wait_ge(S["m1_mm"], at("m1_mm", 2 * (lv - 1) + t + 1))
                    act.activation(gd(t, "m"), pt[:, t, :], ACT.Copy).then_inc(S["m1"], 1)

                def branch_hi(first, n, name_wait, k):
                    act.wait_ge(S[name_wait], at(name_wait, k))
                    act.activation(hhi[:, first:first + n, :], ot[:, first:first + n, :], ACT.Copy).then_inc(S["o_hi"], 1)

                def sigmoids():
                    act.wait_ge(S["mix_ev"], at("mix_ev", 10))
                    act.activation(gates[:, :, 0:D], gates[:, :, 0:D], ACT.Sigmoid).then_inc(S["gates"], 1)

                def merged_hi(t):
                    act.wait_ge(S["merged_T"], at("merged_T", t + 1))
                    act.activation(hhi[:, :, t * P:(t + 1) * P],
                                   pt[:, 2 * t:2 * t + 2, :].rearrange("p b (k s) -> p (b k) s", k=4), ACT.Copy).then_inc(S["m_hi"], 1)

                def fox_s(t):
                    return (scr[:, 0:512] if t == 0 else scr[:, 512:1536]).rearrange("p (h s) -> p h s", h=HEADS)

                def mixer():
                    for i in range(MIX_U):
                        for half in (0, 1):
                            h = 2 * i + half + 3
                            split(2 * U_M + h, 24 if h // 2 in (8, 9) else 1024)
                            if half == 1 and i < BR0 and i % 2:
                                evac(i // 2)
                            for task in TASKS.get((i, half), ()):
                                if task in tasks:
                                    tasks[task]()
                    norm_stage(1)

                tasks = {
                    "silu0": lambda: conv_silu(0), "silu1": lambda: conv_silu(1), "silu2": lambda: conv_silu(2),
                    "tap00": lambda: conv_first(0), "tap10": lambda: conv_first(1), "tap20": lambda: conv_first(2),
                    "squares": squares,
                    "l2_ln": l2_ln, "l2_exp": l2_exp, "params": params, "fox_p": fox_exp, "fox_T": fox_pt, "fox_o": fox_o,
                    "sb_z": sb_exp, "sb_l": sb_ln, "sb_r": sb_w, "sb_o": sb_o, "kv": kv,
                    "dec0": lambda: decays(0), "dec1": lambda: (at_copy(0), decays(1)), "inv0": lambda: at_copy(1),
                    "o_split": lambda: branch_hi(0, 4, "o_ab", 2),
                    "c_split": lambda: (branch_hi(4, 4, "o_c", 1)), "sig": sigmoids,
                    "mrg": lambda: (merged_hi(0), merged_hi(1)),
                    "f2": lambda: state_copy(), "f5": lambda: (o_sq(0), o_sq(1)), "oT": lambda: o_copy(),
                }
                for lv in range(1, 7):
                    tasks[f"ma{lv}"] = lambda lv=lv: (m1_copy(lv, 0), m1_copy(lv, 1))

                def state_copy():
                    act.wait_ge(S["state_mm"], at("state_mm", 1))
                    act.activation(gd(0, "x"), pt[:, 1, :], ACT.Copy).then_inc(S["state"], 1)

                def o_sq(t):
                    act.wait_ge(S["o_raw"], at("o_raw", t + 1))
                    for h in range(HEADS):
                        ins = act.activation(gd(t, "ats")[:, h * P:(h + 1) * P],
                                             lnw[:, t, h * P:(h + 1) * P], ACT.Square,
                                             accum_out=oss[:, 4 * t + h:4 * t + h + 1])
                    ins.then_inc(S["o_ss"], 1)

                def o_copy():
                    act.wait_ge(S["o_T"], at("o_T", 1))
                    act.activation(ot[:, 4:8, :], pt[:, 0:2, :].rearrange("p b (k s) -> p (b k) s", k=2), ACT.Copy).then_inc(S["o_c"], 1)

                ffn(0, 0, U_A, True)
                mixer()
                ffn(1, 2, U_B, False)

        @block.tensor
        def _(pe):
            pe.wait_ge(S["masks"], 1)
            pe.wait_ge(S["rows_in"], 64)
            pe.transpose(pt[:, 0, 0:48], lnw[0:48, 0, 0:128], ident[0:48, 0:48]).then_inc(S["w_used"], 4)
            pe.transpose(pt[:, 0, 48:96], lnw[0:48, 0, 128:256], ident[0:48, 0:48])
            pe.transpose(pt[:, 0, 96:192], lnw[0:96, 0, 256:384], ident[0:96, 0:96])
            pe.transpose(pt[:, 0, 192:200], lnw[0:8, 0, 384:512], ident[0:8, 0:8]).then_inc(S["cols_T"], 1)

            def mod_columns(dst):
                for part in (0, 1):
                    for c in range(KD):
                        ins = pe.matmul(dst[:, part * KD + c:part * KD + c + 1],
                                        acc[:, part * D + c * P:part * D + (c + 1) * P], ones[:, 0:1],
                                        start=True, stop=True)
                ins.then_inc(S["mod_mm"], 1)

            def gate_rows(at, s):
                pe.wait_ge(S["ada_first"], len(DVE_FIRST))
                pe.wait_ge(S["ada_done"], at("ada_done", ADA_N * s))
                for n in (0, 1):
                    ins = pe.matmul(pt[:, n, :], ones, acc[:, 2 * D + n * 512:2 * D + (n + 1) * 512],
                                    start=True, stop=True)
                ins.then_inc(S["gate_mm"], 1)

            def x_transposes(t):
                for c in range(KD):
                    ins = pe.transpose(pt[:, 2 * t + c // 4, (c % 4) * P:(c % 4 + 1) * P],
                                       x[:, t, c * P:(c + 1) * P], ident[:, :])
                ins.then_inc(S["ln_xt"], 1)

            pe.wait_ge(S["cols"], 1)
            pe.wait_ge(S["sc_ready"], 1)
            pe.wait_ge(S["x_in"], 16)
            for t in range(NT):
                x_transposes(t)
            pe.wait_ge(S["masks_done"], 1)
            pe.wait_ge(S["ada_first"], 6)
            pe.wait_ge(S["ada_done"], 2)
            mod_columns(pg[:, 0, :])

            with pe.Fori(0, DEPTH) as l:
                at = counter(l)

                def mm3(out_ap, a, b, first, last, group=False):
                    for n, (i, j) in enumerate(((0, 0), (0, 1), (1, 0))):
                        ins = pe.matmul(out_ap, a[i], b[j], start=first and n == 0, stop=last and n == 2,
                                        skip_group_check=group)
                    return ins

                def wv(h, size=512):
                    n = 1024 if size > 12 else 24
                    lo = wlo[:, h // 2 % 4, h % 2 * n:h % 2 * n + n]
                    return [w.rearrange("p (k c) -> p k c", c=size) for w in (whi[:, h % 4, 0:n], lo)]

                def h_part(kt, t):
                    return [h[:, kt, t * P:(t + 1) * P] for h in (hhi, hlo)]

                def up_half(h0, c, q, t):
                    w = wv(h0 + 4 * c + q)
                    for k in range(2):
                        ins = mm3(pg[:, 2 * (c % 2) + t, :], h_part(2 * q + k, t), [v[:, k, :] for v in w],
                                  q == 0 and k == 0, q == 3 and k == 1)
                    return ins

                def act_transposes(c):
                    for t in range(NT):
                        for k in (0, 1):
                            ins = pe.transpose(pt[:, c % 2, k * SEQ + t * P:k * SEQ + (t + 1) * P],
                                               act_t[:, t, k * P:(k + 1) * P], ident[:, :])
                    ins.then_inc(S["act_T"], 1)

                def ffn(f, s, u0):
                    up0 = f * 2 * NCH
                    h0 = 2 * u0
                    for t in range(NT):
                        pe.wait_ge(S["h_lo"], at("h_lo", NT * (s - 1) + t + 1))
                        for q in range(3):
                            pe.wait_ge(S["w_lo"], at("w_lo", h0 + q + 1))
                            ins = up_half(h0, 0, q, t)
                            if t == 1:
                                ins.then_inc(S["w_used"], 1)
                    gate_rows(at, s)
                    pe.wait_ge(S["w_lo"], at("w_lo", h0 + 4))
                    for t in range(NT):
                        up_half(h0, 0, 3, t).then_inc(S[("up_mm", "w_used")[t]], 1)

                    with pe.Fori(0, PAIRS) as j:
                        for c in (1, 2):
                            for q in range(4):
                                pe.wait_ge(S["w_lo"], l * PER["w_lo"] + j * 8 + (h0 + 4 * c + q + 1))
                                if q == 0:
                                    pe.wait_ge(S["act"], l * PER["act"] + j * 4 + (OFF["act"] + up0 + 2 * (c - 1)))
                                for t in range(NT):
                                    ins = up_half(h0, c, q, t)
                                    if q == 3 and t == 0:
                                        ins.then_inc(S["up_mm"], 1)
                                ins.then_inc(S["w_used"], 1)
                                if q == 1:
                                    pe.wait_ge(S["act"], l * PER["act"] + j * 4 + (OFF["act"] + up0 + 2 * c))
                                    pe.wait_ge(S["act_lo"], l * PER["act_lo"] + j * 2 + (OFF["act_lo"] + f * NCH + c - 2))
                                    pe.wait_ge(S["gate_bc"], at("gate_bc", s + 1))
                                    act_transposes(c - 1)
                    d0 = 4 * NCH
                    d1 = 2 * FFN_U

                    def down(h, t):
                        w = wv(h0 + h, 1024)
                        pe.wait_ge(S["w_lo"], at("w_lo", h0 + h + 1))
                        a = [v[:, h - d0, t * P:(t + 1) * P] for v in (athi, atlo)]
                        for n in (0, 1):
                            ins = mm3(pg[:, 2 * t + n, :], a, [v[:, 0, n * 512:(n + 1) * 512] for v in w],
                                      h == d0, h == d1 - 1)
                        return ins

                    pe.wait_ge(S["act_lo"], at("act_lo", f * NCH + 1))
                    pe.wait_ge(S["act"], at("act", up0 + 2 * (NCH - 1)))
                    for t in (1, 0):
                        if t == 0:
                            pe.wait_ge(S["act"], at("act", up0 + 2 * NCH))
                        for h in (d0, d0 + 1):
                            ins = down(h, t)
                            if t == 0:
                                ins.then_inc(S["w_used"], 1)
                    pe.wait_ge(S["act_lo"], at("act_lo", f * NCH + NCH - 2))
                    act_transposes(NCH - 1)
                    for h in range(d0 + 2, d1 - 3):
                        if h % 2 == 0:
                            pe.wait_ge(S["act_lo"], at("act_lo", f * NCH + (h - d0) // 2 + 1))
                        for t in range(NT):
                            ins = down(h, t)
                        ins.then_inc(S["w_used"], 1)
                        if h == d0 + 15:
                            pe.wait_ge(S["ada_done"], at("ada_done", ADA_N * (s + 1)))
                            mod_columns(pt[:, 3, :])
                    pe.wait_ge(S["act_lo"], at("act_lo", f * NCH + NCH))
                    for t in range(NT):
                        for h in range(d1 - 3, d1):
                            ins = down(h, t)
                            if t == 1:
                                ins.then_inc(S["w_used"], 1)
                        if t == 0:
                            ins.then_inc(S["y_mm"], 1)
                    norm_stage(s)

                def norm_stage(s):
                    pe.wait_ge(S["mod_cols"], at("mod_cols", s + 1))
                    for t in range(NT):
                        pe.wait_ge(S["ln_x"], at("ln_x", NT * s + t + 1))
                        x_transposes(t)

                def chunk_half(i, half, ts=(0, 1)):
                    k, ui = i // 2, i % 2
                    h = 2 * (U_M + i) + half
                    b = 2 * (k % 2)
                    pe.wait_ge(S["w_lo"], at("w_lo", h + 1))
                    if (ui, half) == (0, 0) and k >= 2:
                        pe.wait_ge(S["mix_ev"], at("mix_ev", k - 1))
                    first, last = (ui, half) == (0, 0), (ui, half) == (1, 1)
                    kt0 = 4 * ui + 2 * half
                    w = wv(h, 12 if k == 4 else 512)
                    if k in (1, 2, 3, 5, 7):
                        for c in range(4):
                            for kt in (0, 1):
                                ins = mm3(pg[:, b + c // 2, (c % 2) * SEQ:(c % 2 + 1) * SEQ],
                                          [v[:, kt, c * P:(c + 1) * P] for v in w],
                                          [v[:, kt0 + kt, :] for v in (hhi, hlo)],
                                          first and kt == 0 and c % 2 == 0, last and kt == 1, group=True)
                    else:
                        n = 12 if k == 4 else 512
                        for t in ts:
                            for kt in (0, 1):
                                ins = mm3(pg[:, b + t, 0:n], h_part(kt0 + kt, t), [v[:, kt, :] for v in w],
                                          first and kt == 0, last and kt == 1)
                    if 1 in ts:
                        ins.then_inc(S["w_used"], 1)

                def ssq():
                    pe.wait_ge(S["cv_sq"], at("cv_sq", 2))
                    pe.wait_ge(S["gate_bc"], at("gate_bc", 2))
                    for b in range(4):
                        ins = pe.matmul(pt[:, b, :], ones, scr[:, b * 512:(b + 1) * 512], start=True, stop=True)
                    ins.then_inc(S["ssq_mm"], 1)

                def rows():
                    pe.wait_ge(S["lgu"], at("lgu", 4))
                    pe.wait_ge(S["ssq_ln"], at("ssq_ln", 1))
                    for hp in (0, 1):
                        r0 = scr[:, 512 * hp:512 * hp + 512]
                        pe.matmul(pt[:, hp, :], ones, r0, start=True, stop=False, skip_group_check=True)
                        r1 = scr[:, 1024 + 256 * hp:1024 + 256 * hp + 256].rearrange("p (h s) -> p h s", h=2)
                        ins = pe.matmul(pt[:, hp, :].rearrange("p (h s) -> p h s", h=2)[:, :, P:2 * P], ones, r1,
                                        start=False, stop=True, skip_group_check=True)
                    c = pt[:, 2, 0:16].rearrange("p (a h) -> p a h", a=4)
                    pe.matmul(c[:, 0, :], tri, lg[:, 0, 0:4], start=True, stop=True)
                    pe.matmul(c[:, 1, :], ones, lg[:, 0, 0:4], start=True, stop=False)
                    pe.matmul(c[:, 1, :], tri, lg[:, 1, 0:4], start=False, stop=True)
                    pe.matmul(c[:, 2, :], tri, lg[:, 0, 4:8], start=True, stop=True)
                    pe.matmul(c[:, 3, :], tri, lg[:, 1, 4:8], start=True, stop=True)
                    ins = pe.matmul(pt[:, 2, 16:20], ones, lg[:, 0, 4:8], start=True, stop=True)
                    ins.then_inc(S["rows_mm"], 1)

                def heads(a, h, lo, hi):
                    return qkt[(h % 2) * DH:(h % 2 + 1) * DH, a, h // 2, lo:hi]

                def fox_scores():
                    pe.wait_ge(S["mix_ev"], at("mix_ev", 6))
                    pe.wait_ge(S["fox_b"], at("fox_b", 2))
                    for odd in (0, 1):
                        for h in (odd, odd + 2):
                            pe.matmul(pt[:, 0, h * P:(h + 1) * P], heads(0, h, 0, P), heads(1, h, 0, P),
                                      start=True, stop=True)
                            ins = pe.matmul(pt[:, 1 + h // 2, (h % 2) * SEQ:(h % 2 + 1) * SEQ],
                                            heads(0, h, P, SEQ), heads(1, h, 0, SEQ), start=True, stop=True)
                        ins.then_inc(S["fox_mm"], 1)
                        pe.wait_ge(S["fox_mm"], at("fox_mm", odd + 1))

                def fox_T():
                    pe.wait_ge(S["fox_p"], at("fox_p", 2))
                    for h in range(HEADS):
                        o0 = pt[:, h // 2, (h % 2) * SEQ:(h % 2 + 1) * SEQ]
                        p1 = scr[:, 512 + h * SEQ:512 + (h + 1) * SEQ]
                        pe.transpose(o0[:, 0:P], scr[:, h * P:(h + 1) * P], ident[:, :])
                        pe.transpose(o0[:, P:SEQ], p1[:, 0:P], ident[:, :])
                        ins = pe.transpose(pt[:, 2, h * P:(h + 1) * P], p1[:, P:SEQ], ident[:, :])
                    ins.then_inc(S["foxp_T"], 1)

                def pv(name, v0, w0_, w1_):
                    for h in range(HEADS):
                        r = (h % 2) * DH
                        o = pt[r:r + DH, 3, (h // 2) * SEQ:(h // 2 + 1) * SEQ]
                        pe.matmul(o, val[:, 0, v0 + h * DH:v0 + (h + 1) * DH], w0_[:, h * SEQ:(h + 1) * SEQ],
                                  start=True, stop=False, skip_group_check=True)
                        ins = pe.matmul(o[:, P:SEQ], val[:, 1, v0 + h * DH:v0 + (h + 1) * DH],
                                        w1_[:, h * P:(h + 1) * P], start=False, stop=True, skip_group_check=True)
                    ins.then_inc(S[name], 1)

                def fox_pv():
                    pe.wait_ge(S["fox_pt"], at("fox_pt", 2))
                    pe.wait_ge(S["mix_ev"], at("mix_ev", 7))
                    pv("fox_pv", 0, scr[:, 1536:2560], scr[:, 2560:3072])

                def sb_scores():
                    pe.wait_ge(S["mix_ev"], at("mix_ev", 8))
                    pe.wait_ge(S["fox_pt"], at("fox_pt", 2))
                    pe.wait_ge(S["fox_b"], at("fox_b", 2))
                    for odd in (0, 1):
                        for h in (odd, odd + 2):
                            pe.matmul(pt[:, h // 2, (h % 2) * SEQ:(h % 2 + 1) * SEQ], heads(3, h, 0, P),
                                      heads(2, h, 0, SEQ), start=True, stop=True)
                            ins = pe.matmul(pt[:, 2, h * P:(h + 1) * P], heads(3, h, P, SEQ), heads(2, h, P, SEQ),
                                            start=True, stop=True)
                        ins.then_inc(S["sb_mm"], 1)
                        pe.wait_ge(S["sb_mm"], at("sb_mm", odd + 1))

                def sb_cum():
                    pe.wait_ge(S["sb_sp"], at("sb_sp", 1))
                    for hp in (0, 1):
                        pe.matmul(pt[:, hp, :], trid[:, :], scr[:, 1536 + 512 * hp:1536 + 512 * (hp + 1)],
                                  start=True, stop=False, skip_group_check=True)
                        pe.matmul(pt[:, hp, :].rearrange("p (h s) -> p h s", h=2)[:, :, P:2 * P], ones,
                                  scr[:, 2560 + 256 * hp:2560 + 256 * (hp + 1)].rearrange("p (h s) -> p h s", h=2),
                                  start=False, stop=True, skip_group_check=True)
                    ins = pe.matmul(pt[:, 2, :], trid[:, :], scr[:, 2560:3072], start=True, stop=True)
                    ins.then_inc(S["sb_cum"], 1)

                def sb_pv():
                    pe.wait_ge(S["sb_w"], at("sb_w", 1))
                    pe.wait_ge(S["o_ab"], at("o_ab", 1))
                    pv("sb_pv", 256, scr[:, 0:1024], scr[:, 1024:1536])

                def hs(a, h):
                    return a[:, h * P:(h + 1) * P]

                def qh(h, t):
                    return cv[:, h, t * P:(t + 1) * P]

                def kh(h, t):
                    return cv[:, HEADS + h, t * P:(t + 1) * P]

                def kv():
                    pe.wait_ge(S["conv_silu"], at("conv_silu", 3))
                    pe.wait_ge(S["qk_norm"], at("qk_norm", 2))
                    pe.wait_ge(S["sb_arg"], at("sb_arg", 1))
                    for h in range(HEADS):
                        pe.transpose(hs(pt[:, 0, :], h), kh(h, 0), ident[:, :])
                        for t in range(NT):
                            ins = pe.transpose(hs(pt[:, 1 + t, :], h), cv[:, 2 * HEADS + h, t * P:(t + 1) * P], ident[:, :])
                    ins.then_inc(S["kv_T"], 1)

                def grams(t):
                    if t == 0:
                        pe.wait_ge(S["kv"], at("kv", 2))
                    else:
                        pe.wait_ge(S["g_mats"], at("g_mats", 1))
                    pe.wait_ge(S["g_gu"], at("g_gu", t + 1))
                    for h in range(HEADS):
                        pe.matmul(hs(pt[:, 0, :], h), kh(h, t), kh(h, t), start=True, stop=True)
                    for h in range(HEADS):
                        pe.matmul(hs(pt[:, 1, :], h), kh(h, t), qh(h, t), start=True, stop=True)
                    ins = pe.matmul(pt[:, 2, :], ones, gd(t, "m"), start=True, stop=True)
                    ins.then_inc(S["gram_mm"], 1)

                def a_T(t):
                    pe.wait_ge(S["g_a"], at("g_a", t + 1))
                    if t:
                        pe.wait_ge(S["at"], at("at", 1))
                    else:
                        pe.wait_ge(S["o_ab"], at("o_ab", 2))
                    for h in range(HEADS):
                        ins = pe.transpose(hs(pt[:, 3, :], h), hs(gd(t, "m"), h), ident[:, :])
                    ins.then_inc(S["at_T"], 1)

                def m1(lv):
                    for t in range(NT):
                        pe.wait_ge(S["inv_x"], at("inv_x", 2 * (lv - 1) + 2))
                        pe.wait_ge(S["ats"], at("ats", 2 * (lv - 1) + t + 1))
                        for h in range(HEADS):
                            ins = pe.matmul(hs(pt[:, t, :], h), hs(gd(t, "ats"), h), hs(gd(t, "x"), h),
                                            start=True, stop=True)
                        ins.then_inc(S["m1_mm"], 1)

                def m2(lv):
                    for t in range(NT):
                        pe.wait_ge(S["m1"], at("m1", 2 * (lv - 1) + t + 1))
                        b = 2 - 2 * t
                        for h in range(HEADS):
                            if lv < 6:
                                pe.matmul(hs(pt[:, b, :], h), hs(gd(t, "xt"), h), hs(gd(t, "m"), h), start=True, stop=True)
                        for h in range(HEADS):
                            ins = pe.matmul(hs(pt[:, b + 1, :], h), hs(gd(t, "m"), h), hs(gd(t, "xt"), h),
                                            start=True, stop=True)
                        ins.then_inc(S["m2_mm"], 1)

                def f1():
                    pe.wait_ge(S["bv"], at("bv", 1))
                    pe.wait_ge(S["inv_x"], at("inv_x", 13))
                    for h in range(HEADS):
                        ins = pe.matmul(hs(pt[:, 0, :], h), hs(gd(0, "xt"), h), hs(gd(0, "ats"), h), start=True, stop=True)
                    ins.then_inc(S["vnew_mm"], 1)

                def f2():
                    pe.wait_ge(S["vnew"], at("vnew", 2))
                    pe.wait_ge(S["inv_x"], at("inv_x", 14))
                    for h in range(HEADS):
                        ins = pe.matmul(hs(pt[:, 1, :], h), kn[:, h, :], hs(scr[:, 3584:4096], h), start=True, stop=True)
                    ins.then_inc(S["state_mm"], 1)
                    for h in range(HEADS):
                        ins = pe.matmul(hs(pt[:, 2, :], h), hs(gd(0, "it"), h), hs(scr[:, 3072:3584], h),
                                        start=True, stop=True)
                    ins.then_inc(S["o0_mm"], 1)

                def f3():
                    pe.wait_ge(S["state"], at("state", 1))
                    for h in range(HEADS):
                        pe.matmul(hs(pt[:, 0, :], h), kh(h, 1), hs(gd(0, "x"), h), start=True, stop=True)
                    for h in range(HEADS):
                        ins = pe.matmul(hs(pt[:, 3, :], h), qh(h, 1), hs(gd(0, "x"), h), start=True, stop=True)
                    ins.then_inc(S["zq_mm"], 1)

                def f4():
                    pe.wait_ge(S["rhs1"], at("rhs1", 1))
                    pe.wait_ge(S["inv_x"], at("inv_x", 14))
                    for h in range(HEADS):
                        ins = pe.matmul(hs(pt[:, 1, :], h), hs(gd(1, "xt"), h), hs(gd(1, "ats"), h), start=True, stop=True)
                    ins.then_inc(S["vnew_mm"], 1)

                def f5():
                    pe.wait_ge(S["vnew"], at("vnew", 3))
                    for h in range(HEADS):
                        ins = pe.matmul(hs(pt[:, 2, :], h), hs(gd(1, "it"), h), hs(scr[:, 3072:3584], h),
                                        start=True, stop=True)
                    ins.then_inc(S["o1_mm"], 1)

                def o_T():
                    for t in range(NT):
                        pe.wait_ge(S["o_gated"], at("o_gated", t + 1))
                        for h in range(HEADS):
                            ins = pe.transpose(pt[:, h // 2, (h % 2) * SEQ + t * P:(h % 2) * SEQ + (t + 1) * P],
                                               hs(lnw[:, t, 512:1024], h), ident[:, :])
                    ins.then_inc(S["o_T"], 1)

                def merged_T():
                    for t in range(NT):
                        pe.wait_ge(S["merged"], at("merged", 2 * t + 2))
                        for c in range(KD):
                            ins = pe.transpose(pt[:, 2 * t + c // 4, (c % 4) * P:(c % 4 + 1) * P],
                                               merged[:, t, c * P:(c + 1) * P], ident[:, :])
                        ins.then_inc(S["merged_T"], 1)

                tasks = {"l2norm": ssq, "rows": rows, "fox_p": fox_scores, "fox_T": fox_T, "fox_o": fox_pv,
                         "sb_z": sb_scores, "sb_r": sb_cum, "sb_o": sb_pv, "kv": kv,
                         "dec0": lambda: grams(0), "dec1": lambda: (a_T(0), grams(1)), "inv0": lambda: a_T(1),
                         "f1": f1, "f2": f2, "f3": f3, "f4": f4, "f5": f5, "oT": o_T, "mrg": merged_T}
                for lv in range(1, 7):
                    tasks[f"ma{lv}"] = lambda lv=lv: m1(lv)
                    tasks[f"mb{lv}"] = lambda lv=lv: m2(lv)

                def rows_half(i, half, ts=(0, 1)):
                    h = 2 * (U_M + i) + half
                    b = i - BR0
                    w = wv(h, 1024)
                    pe.wait_ge(S["w_lo"], at("w_lo", h + 1))
                    kt = 2 * (b if b < 4 else b - 4) + half
                    first = half == 0 and (b < 3 or b == 4)
                    last = half == 1 and b in (0, 1, 3, 7)
                    for t in ts:
                        for n in (0, 1):
                            if (b, half) == (0, 0):
                                pe.wait_ge(S["mix_ev"], at("mix_ev", MIX_CH - 1 if t == 0 else MIX_CH))
                                pe.wait_ge(S["o_lo"], at("o_lo", 1))
                            if b in (1, 2) and half == 0:
                                pe.wait_ge(S["y_ev"], at("y_ev", 4 * (b - 1) + 2 * t + n + 1))
                                pe.wait_ge(S["o_lo"], at("o_lo", b))
                            if (b, half) == (4, 0):
                                pe.wait_ge(S["y_ev"], at("y_ev", 8 + 2 * t + n + 1))
                                pe.wait_ge(S["m_lo"], at("m_lo", t + 1))
                            ins = mm3(pg[:, 2 * t + n, :], h_part(kt, t), [v[:, 0, n * 512:(n + 1) * 512] for v in w],
                                      first, last)
                            if b < 4 and last and (t, n) != (1, 1):
                                ins.then_inc(S["yb_mm"], 1)
                    if i == MIX_U - 1 and half == 1 and ts == (0,):
                        ins.then_inc(S["y_mm"], 1)
                    if 1 in ts:
                        ins.then_inc(S["w_used"], 1)

                def mixer():
                    for t in range(NT):
                        pe.wait_ge(S["h_lo"], at("h_lo", t + 1))
                        for q in range(3):
                            chunk_half(q // 2, q % 2, (t,))
                    gate_rows(at, 1)
                    for i in range(MIX_U):
                        for half in (0, 1):
                            q = 2 * i + half
                            if not 3 <= q < 2 * MIX_U - 3:
                                continue
                            if i < BR0:
                                chunk_half(i, half)
                            else:
                                rows_half(i, half)
                            if (i, half) == (33, 0):
                                pe.wait_ge(S["m_lo"], at("m_lo", 2))
                                pe.wait_ge(S["ada_done"], at("ada_done", 2 * ADA_N))
                                mod_columns(pt[:, 3, :])
                            for task in TASKS.get((i, half), ()):
                                if task in tasks:
                                    tasks[task]()
                    for t in range(NT):
                        for q in range(2 * MIX_U - 3, 2 * MIX_U):
                            rows_half(q // 2, q % 2, (t,))
                    norm_stage(1)

                ffn(0, 0, U_A)
                mixer()
                ffn(1, 2, U_B)

        @block.vector
        def _(dve):
            dve.memset(acc[:, :], 0.0).then_inc(S["acc_zero"], 1)
            dve.wait_ge(S["cols_T"], 1)
            dve.wait_ge(S["sc_ready"], 1)
            dve.tensor_copy(cols[:, :], pt[:, 0, 0:192]).then_inc(S["cols"], 1)
            dve.memset(modt[:, :], 0.0).then_inc(S["act_lo"], 2)
            dve.memset(modab[:, :, :], 0.0).then_inc(S["act"], 2)
            dve.wait_ge(S["act"], 2)

            dve.wait_ge(S["first_row"], 16)
            def first_fold(i, n):
                a = acc[:, i * ADA_C:(i + 1) * ADA_C]
                r = pro_slot(FIRST_SLOT[i]).rearrange("p (k c) -> p k c", k=KD)
                dve.wait_ge(S[FIRST_SEM[FIRST_SLOT[i]]], 32 * FIRST_USE[i])
                for k in range(KD):
                    ins = dve.scalar_tensor_tensor(out=a, in0=r[:, k, :], scalar=sc[:, k:k + 1], in1=a,
                                                   op0=ALU.mult, op1=ALU.add)
                    if k < KD - 1:
                        ins.then_inc(S["fold_first"], 1)
                        dve.wait_ge(S["fold_first"], 7 * n + k + 1)
                ins.then_inc(S["ada_first"], 1)

            for n, i in enumerate(DVE_FIRST):
                first_fold(i, n)

            def mod_cols(first, at, k, lncol):
                dve.wait_ge(S["mod_mm"], at("mod_mm", k + 1))
                if first:
                    dve.tensor_scalar(modab[:, 0, :], pg[:, 0, KD:2 * KD], 1.0, None, ALU.add).then_inc(S["mod_a"], 1)
                    dve.tensor_copy(modab[:, 1, :], pg[:, 0, 0:KD]).then_inc(S["mod_cols"], 1)
                    return
                dve.wait_ge(S["ada_done"], at("ada_done", ADA_N * (k + 1)))
                g = cols[:, ds(lncol, KD)]
                b = cols[:, ds(lncol + 48, KD)]
                dve.scalar_tensor_tensor(out=modab[:, 0, :], in0=pt[:, 3, KD:2 * KD], scalar=1.0, in1=g,
                                         op0=ALU.add, op1=ALU.mult).then_inc(S["mod_a"], 1)
                dve.scalar_tensor_tensor(out=modt[:, :], in0=pt[:, 3, KD:2 * KD], scalar=1.0, in1=b,
                                         op0=ALU.add, op1=ALU.mult).then_inc(S["mod_a"], 1)
                dve.wait_ge(S["mod_a"], at("mod_a", 2 * k + 2))
                dve.tensor_tensor(modab[:, 1, :], modt[:, :], pt[:, 3, 0:KD], ALU.add).then_inc(S["mod_cols"], 1)

            def h_split(at, k, t):
                half = KD // 2
                dve.wait_ge(S["ln_xt"], at("ln_xt", NT * k + t + 1))
                dve.wait_ge(S["mod_cols"], at("mod_cols", k + 1))
                for c in range(half, KD):
                    ins = dve.tensor_scalar(lnw[:, t, c * P:(c + 1) * P], pt[:, 2 * t + 1, (c - half) * P:(c - half + 1) * P],
                                            modab[:, 0, c:c + 1], modab[:, 1, c:c + 1], ALU.mult, ALU.add)
                ins.then_inc(S["h_f32"], 1)
                dve.wait_ge(S["h_f32"], at("h_f32", NT * k + t + 1))
                src = lnw[:, t, :].rearrange("p (k s) -> p k s", k=KD)
                hi = hhi[:, :, t * P:(t + 1) * P]
                dve.tensor_copy(hi[:, half:KD, :], src[:, half:KD, :]).then_inc(S["h_hi"], 1)
                dve.wait_ge(S["h_hi"], at("h_hi", NT * k + t + 1))
                dve.wait_ge(S["h_hia"], at("h_hia", NT * k + t + 1))
                dve.tensor_tensor(hlo[:, :, t * P:(t + 1) * P], src, hi.bitcast(F32), ALU.subtract).then_inc(S["h_lo"], 1)

            w0 = counter(None)
            mod_cols(True, w0, 0, 0)
            for t in range(NT):
                h_split(w0, 0, t)

            with dve.Fori(0, DEPTH) as l:
                at = counter(l)

                def split(h, size=1024):
                    a, lo = [w[:, h // 2 % 4, h % 2 * size:h % 2 * size + size] for w in (wraw, wlo)]
                    dve.wait_ge(S["w_hi"], at("w_hi", h + 1))
                    dve.tensor_tensor(lo, a, whi[:, h % 4, 0:size].bitcast(F32), ALU.subtract).then_inc(S["w_lo"], 1)

                def split_j(h, j):
                    a, lo = [w[:, h // 2 % 4, h % 2 * 1024:h % 2 * 1024 + 1024] for w in (wraw, wlo)]
                    dve.wait_ge(S["w_hi"], l * PER["w_hi"] + j * 8 + (h + 1))
                    dve.tensor_tensor(lo, a, whi[:, h % 4, :].bitcast(F32), ALU.subtract).then_inc(S["w_lo"], 1)

                def gate_bc(s, coef):
                    dve.wait_ge(S["gate_mm"], at("gate_mm", s + 1))
                    dve.tensor_scalar(gatebc[:, :], pt[:, 0:2, :].rearrange("p b c -> p (b c)"), coef, coef,
                                      ALU.mult, ALU.add).then_inc(S["gate_bc"], 1)

                def act_lo(f, c, j=None):
                    src = pt[:, c % 2, :].rearrange("p (k s) -> p k s", k=2)
                    if j is None:
                        dve.wait_ge(S["act_hi"], at("act_hi", f * NCH + c + 1))
                        rows = slice(2 * c, 2 * c + 2)
                    else:
                        dve.wait_ge(S["act_hi"], l * PER["act_hi"] + j * 2 + (f * NCH + c + 1))
                        rows = ds(j * 4 + 2 * c, 2)
                    dve.tensor_tensor(atlo[:, rows, :], src, athi[:, rows, :].bitcast(F32), ALU.subtract).then_inc(S["act_lo"], 1)

                def act_mul(f, t, c, j=None):
                    k = 2 * (f * NCH + c) + t + 1
                    if j is None:
                        dve.wait_ge(S["up_silu"], at("up_silu", k))
                    else:
                        dve.wait_ge(S["up_silu"], l * PER["up_silu"] + j * 4 + (k))
                    dve.tensor_tensor(act_t[:, t, :], sg[:, t, :], pg[:, 2 * (c % 2) + t, CW:2 * CW], ALU.mult).then_inc(S["act"], 1)

                def ada_j(s, k, j):
                    idx = s * ADA_N + k
                    a = acc[:, ds(j * (2 * ADA_C) + k * ADA_C, ADA_C)]
                    r = aw[:, :].rearrange("p (k c) -> p k c", k=KD)
                    dve.wait_ge(S["ada_in"], l * PER["ada_in"] + j * 32 + (16 * (idx + 1)))
                    dve.wait_ge(S["acc_row"], at("acc_row", 16 * (s + 1)))
                    fold0 = f_index(s) * 8 * PAIRS + 4 * k
                    for m in range(4):
                        dve.scalar_tensor_tensor(out=a, in0=r[:, m, :], scalar=sc[:, m:m + 1], in1=a,
                                                 op0=ALU.mult, op1=ALU.add).then_inc(S["fold_dve"], 1)
                        dve.wait_ge(S["fold_dve"], l * PER["fold_dve"] + j * 8 + (fold0 + m + 1))
                    dve.wait_ge(S["ada_half"], l * PER["ada_half"] + j * 2 + (f_index(s) * 2 * PAIRS + k + 1))
                    dve.tensor_tensor(a, a, r[:, 4, :], ALU.add).then_inc(S["ada_done"], 1)

                def f_index(s):
                    return s // 2

                def ffn(f, s, u0, first):
                    h0 = 2 * u0
                    for h in range(0 if first else 3, 3 if first else 5):
                        split(h0 + h)
                    gate_bc(s, 0.5)
                    for h in range(3 if first else 5, 7):
                        split(h0 + h)
                    with dve.Fori(0, PAIRS) as j:
                        for c in (1, 2):
                            act_mul(f, 0, c - 1, j)
                            act_mul(f, 1, c - 1, j)
                            split_j(h0 + 4 * c + 3, j)
                            split_j(h0 + 4 * c + 4, j)
                            split_j(h0 + 4 * c + 5, j)
                            act_lo(f, c - 1, j)
                            split_j(h0 + 4 * c + 6, j)
                            ada_j(s, c - 1, j)
                    act_mul(f, 0, NCH - 1)
                    act_mul(f, 1, NCH - 1)
                    for h in range(4 * NCH + 3, 2 * FFN_U + (1 if s == 0 else 0)):
                        split(h0 + h)
                        if h == 4 * NCH + 5:
                            act_lo(f, NCH - 1)
                        if h == 2 * FFN_U - 4:
                            mod_cols(False, at, s, l * 24 + s * 8)
                    norm_stage(s, u0 + FFN_U)

                def norm_stage(s, u_next):
                    def residual(t):
                        if t == 0:
                            dve.wait_ge(S["y_mm"], at("y_mm", s + 1))
                        else:
                            dve.wait_ge(S["w_used"], at("w_used", 2 * u_next))
                        dve.wait_ge(S["x_affine"], at("x_affine", NT * s))
                        dve.tensor_tensor(lnw[:, t, :], pg[:, 2 * t:2 * t + 2, :].rearrange("p b c -> p (b c)"),
                                          gatebc[:, :], ALU.mult).then_inc(S["ln_gy"], 1)
                        dve.wait_ge(S["ln_gy"], at("ln_gy", NT * s + t + 1))
                        dve.scalar_tensor_tensor(out=x[:, t, :], in0=x[:, t, :], scalar=ALPHA, in1=lnw[:, t, :],
                                                 op0=ALU.mult, op1=ALU.add).then_inc(S["ln_sum"], 1)

                    def moments(t):
                        dve.wait_ge(S["ln_sum"], at("ln_sum", NT * s + t + 1))
                        for n in (0, 1):
                            dve.bn_stats(stats[:, t, n, :], x[:, t, n * 512:(n + 1) * 512]).then_inc(S["ln_bn"], 1)
                        dve.wait_ge(S["ln_bn"], alone(dve, "ln_bn", l * PER["ln_bn"] + (2 * NT * s + 2 * t + 2)))
                        dve.bn_aggr(mv[:, t, :], stats[:, t, :, :]).then_inc(S["ln_mv"], 1)
                        dve.wait_ge(S["ln_mv"], at("ln_mv", NT * s + t + 1))
                        dve.tensor_scalar(var[:, t:t + 1], mv[:, t, 1:2], LN_EPS, None, ALU.add).then_inc(S["ln_var"], 1)

                    def normed(t):
                        dve.wait_ge(S["ln_rstd"], at("ln_rstd", NT * s + t + 1))
                        dve.tensor_scalar(x[:, t, :], x[:, t, :], mv[:, t, 0:1], rstd[:, t:t + 1],
                                          ALU.subtract, ALU.mult).then_inc(S["ln_x"], 1)
                    residual(0)
                    moments(0)
                    if u_next < UNITS:
                        split(2 * u_next + 1)
                    normed(0)
                    residual(1)
                    moments(1)
                    normed(1)
                    h_split(at, s, 0)
                    if u_next < UNITS:
                        split(2 * u_next + 2)
                    h_split(at, s, 1)

                def conv(k, tap):
                    dve.wait_ge(S["mix_ev"], at("mix_ev", k + 2))
                    dve.wait_ge(S["convw"], at("convw", 1))
                    dve.wait_ge(S["conv"], at("conv", 4 * k + tap))
                    pre = scr[:, 0:1040].rearrange("p (c s) -> p c s", c=4)
                    res = scr[:, 1040:2064].rearrange("p (c s) -> p c s", c=4)
                    for c in range(4):
                        n = tap * 12 + 4 * k + c
                        w = convw[:, n:n + 1]
                        src = pre[:, c, 1 + tap:1 + tap + SEQ]
                        ins = dve.scalar_tensor_tensor(out=res[:, c, :], in0=src, scalar=w, in1=res[:, c, :],
                                                       op0=ALU.mult, op1=ALU.add)
                    ins.then_inc(S["conv"], 1)

                def pad():
                    dve.tensor_copy(convw[:, :], cols[:, ds(l * 48 + 96, 48)]).then_inc(S["convw"], 1)
                    dve.wait_ge(S["w_used"], at("w_used", 2 * U_M))
                    dve.memset(scr[:, 0:1040].rearrange("p (c s) -> p c s", c=4)[:, :, 0:4], 0.0).then_inc(S["pad"], 1)

                def qk_norm():
                    dve.wait_ge(S["ssq_exp"], at("ssq_exp", 1))
                    src = cv[:, 0:8, :].rearrange("p c s -> p (c s)")
                    dve.scalar_tensor_tensor(out=src[:, 0:1024], in0=src[:, 0:1024], scalar=P ** -0.5,
                                             in1=scr[:, 2048:3072], op0=ALU.mult, op1=ALU.mult).then_inc(S["qk_norm"], 1)
                    dve.tensor_tensor(src[:, 1024:2048], src[:, 1024:2048], scr[:, 3072:4096], ALU.mult).then_inc(S["qk_norm"], 1)

                def params():
                    dve.wait_ge(S["mix_ev"], at("mix_ev", 5))
                    dve.wait_ge(S["prm_in"], at("prm_in", 64))
                    for t in range(NT):
                        dve.scalar_tensor_tensor(out=sp_a[:, t, 0:4], in0=sm[:, t, 0:4], scalar=-1.0,
                                                 in1=prm[:, 0:4], op0=ALU.mult, op1=ALU.subtract).then_inc(S["sp_arg"], 1)
                        dve.tensor_tensor(sp_a[:, t, 4:8], sm[:, t, 8:12], prm[:, 4:8], ALU.add).then_inc(S["sp_arg"], 1)
                    dve.wait_ge(S["sp_arg"], at("sp_arg", 4))
                    dve.scalar_tensor_tensor(out=sp_b[:, :, :], in0=sp_a[:, :, :], scalar=-1.0, in1=sp_a[:, :, :],
                                             op0=ALU.mult, op1=ALU.max).then_inc(S["sp_abs"], 1)

                def params2():
                    dve.wait_ge(S["sp_ln"], at("sp_ln", 1))
                    dve.scalar_tensor_tensor(out=sp_c[:, :, :], in0=sp_a[:, :, :], scalar=0.0, in1=sp_b[:, :, :],
                                             op0=ALU.max, op1=ALU.add).then_inc(S["sp"], 1)
                    dve.wait_ge(S["sp"], at("sp", 1))
                    dve.wait_ge(S["ea"], at("ea", 1))
                    for t in range(NT):
                        dve.tensor_scalar(lg[:, t, 0:4], sp_c[:, t, 0:4], -1.0, None, ALU.mult).then_inc(S["lg"], 1)
                        dve.scalar_tensor_tensor(out=lg[:, t, 4:8], in0=sp_c[:, t, 4:8], scalar=-1.0, in1=ea[:, :],
                                                 op0=ALU.mult, op1=ALU.mult).then_inc(S["lg"], 1)
                    dve.wait_ge(S["beta_e"], at("beta_e", 1))
                    dve.tensor_scalar(beta_t[:, :, :], beta_t[:, :, :], 1.0, None, ALU.add).then_inc(S["beta1"], 1)
                    dve.wait_ge(S["beta1"], at("beta1", 1))
                    dve.reciprocal(beta[:, :, :], beta_t[:, :, :]).then_inc(S["beta"], 1)
                    dve.wait_ge(S["lg"], at("lg", 4))
                    dve.wait_ge(S["ssq_mm"], at("ssq_mm", 1))
                    for h in range(HEADS):
                        ins = dve.tensor_scalar(scr[:, h * SEQ:(h + 1) * SEQ], tri1[:, :, :].rearrange("p a s -> p (a s)"),
                                                lg[:, 0, h:h + 1], None, ALU.mult)
                        ins.then_inc(S["lgu1"], 1)
                    dve.wait_ge(S["lgu1"], at("lgu1", 4))
                    for h in range(HEADS):
                        ins = dve.tensor_scalar(scr[:, 1024 + h * P:1024 + (h + 1) * P], tri, lg[:, 1, h:h + 1], None, ALU.mult)
                        ins.then_inc(S["lgu"], 1)

                def fox_bias():
                    dve.wait_ge(S["rows_mm"], at("rows_mm", 1))
                    dve.tensor_copy(ccol[:, :, :].rearrange("p a h -> p (a h)"), pt[:, 2, 0:16]).then_inc(S["ccol"], 1)
                    dve.wait_ge(S["ccol"], at("ccol", 1))
                    dve.tensor_tensor(dtmp[:, :], pt[:, 2, 16:20], ccol[:, 2, :], ALU.subtract).then_inc(S["dec_arg"], 1)
                    r = pt[:, 0:2, :].rearrange("p b (h s) -> p (b h) s", h=2)
                    for h in range(HEADS):
                        ins = dve.scalar_tensor_tensor(out=scr[:, h * P:(h + 1) * P], in0=r[:, h, 0:P],
                                                       scalar=ccol[:, 0, h:h + 1], in1=foxm[:, 1, :],
                                                       op0=ALU.subtract, op1=ALU.add)
                    ins.then_inc(S["fox_b"], 1)
                    for h in range(HEADS):
                        ins = dve.scalar_tensor_tensor(out=scr[:, 512 + h * SEQ:512 + (h + 1) * SEQ], in0=r[:, h, :],
                                                       scalar=ccol[:, 1, h:h + 1],
                                                       in1=foxm[:, :, :].rearrange("p a s -> p (a s)"),
                                                       op0=ALU.subtract, op1=ALU.add)
                    ins.then_inc(S["fox_b"], 1)

                def fox_softmax():
                    dve.wait_ge(S["fox_mm"], at("fox_mm", 2))
                    dve.wait_ge(S["fox_b"], at("fox_b", 2))
                    dve.scalar_tensor_tensor(out=scr[:, 0:512], in0=pt[:, 0, :], scalar=SCALE, in1=scr[:, 0:512],
                                             op0=ALU.mult, op1=ALU.subtract).then_inc(S["fox_s"], 1)
                    dve.scalar_tensor_tensor(out=scr[:, 512:1536], in0=pt[:, 1:3, :].rearrange("p b s -> p (b s)"),
                                             scalar=SCALE, in1=scr[:, 512:1536], op0=ALU.mult, op1=ALU.subtract).then_inc(S["fox_s"], 1)
                    for t in range(NT):
                        dve.wait_ge(S["fox_s"], at("fox_s", t + 1))
                        s = (scr[:, 0:512] if t == 0 else scr[:, 512:1536]).rearrange("p (h s) -> p h s", h=HEADS)
                        dve.tensor_reduce(fmax[:, 4 * t:4 * t + 4], s, AX.X, ALU.max).then_inc(S["fox_max"], 1)
                        dve.wait_ge(S["fox_max"], at("fox_max", t + 1))
                        dve.tensor_scalar(fneg[:, 4 * t:4 * t + 4], fmax[:, 4 * t:4 * t + 4], -1.0, None, ALU.mult).then_inc(S["fox_neg"], 1)
                    for t in range(NT):
                        dve.wait_ge(S["fox_exp"], at("fox_exp", t + 1))
                        dve.reciprocal(frec[:, 4 * t:4 * t + 4], fsum[:, 4 * t:4 * t + 4]).then_inc(S["fox_rec"], 1)
                        dve.wait_ge(S["fox_rec"], at("fox_rec", t + 1))
                        n = P * (t + 1)
                        for h in range(HEADS):
                            a = scr[:, h * n + 512 * t:(h + 1) * n + 512 * t]
                            ins = dve.tensor_scalar(a, a, frec[:, 4 * t + h:4 * t + h + 1], None, ALU.mult)
                        ins.then_inc(S["fox_p"], 1)

                def sb_z():
                    dve.wait_ge(S["sb_mm"], at("sb_mm", 2))
                    dve.wait_ge(S["fox_pv"], at("fox_pv", 1))
                    z0 = scr[:, 0:1024].rearrange("p (h s) -> p h s", h=HEADS)
                    z1 = scr[:, 1024:1536].rearrange("p (h s) -> p h s", h=HEADS)
                    p0 = pt[:, 0:2, :].rearrange("p b (h s) -> p (b h) s", h=2)
                    m0 = sbm[:, :, :].rearrange("p a s -> p (a s)").unsqueeze(1).broadcast_to((P, HEADS, SEQ))
                    dve.scalar_tensor_tensor(out=z0, in0=p0, scalar=SCALE, in1=m0, op0=ALU.mult, op1=ALU.add).then_inc(S["sb_z"], 1)
                    m1_ = sbm[:, 0, :].unsqueeze(1).broadcast_to((P, HEADS, P))
                    dve.scalar_tensor_tensor(out=z1, in0=pt[:, 2, :].rearrange("p (h s) -> p h s", h=HEADS),
                                             scalar=SCALE, in1=m1_, op0=ALU.mult, op1=ALU.add).then_inc(S["sb_z"], 1)
                    dve.wait_ge(S["sb_z"], at("sb_z", 2))
                    dve.scalar_tensor_tensor(out=scr[:, 1536:3072], in0=scr[:, 0:1536], scalar=-1.0, in1=scr[:, 0:1536],
                                             op0=ALU.mult, op1=ALU.max).then_inc(S["sb_abs"], 1)

                def sb_softplus():
                    dve.wait_ge(S["sb_l"], at("sb_l", 1))
                    dve.scalar_tensor_tensor(out=scr[:, 1536:3072], in0=scr[:, 0:1536], scalar=0.0,
                                             in1=scr[:, 1536:3072], op0=ALU.max, op1=ALU.add).then_inc(S["sb_sp"], 1)

                def sb_arg():
                    dve.wait_ge(S["sb_cum"], at("sb_cum", 1))
                    dve.tensor_tensor(scr[:, 0:1536], scr[:, 0:1536], pt[:, 0:3, :].rearrange("p b s -> p (b s)"),
                                      ALU.subtract).then_inc(S["sb_arg"], 1)

                def hv(a):
                    return a.rearrange("p (h s) -> p h s", h=HEADS)

                def bc(m):
                    return m.unsqueeze(1).broadcast_to((P, HEADS, P))

                def g_rows(t):
                    if t == 0:
                        dve.wait_ge(S["sb_pv"], at("sb_pv", 1))
                    for h in range(HEADS):
                        ins = dve.tensor_scalar(gd(t, "m")[:, h * P:(h + 1) * P], tri, lg[:, t, 4 + h:5 + h], None, ALU.mult)
                    ins.then_inc(S["g_gu"], 1)

                def g_mats(t):
                    dve.wait_ge(S["gram_mm"], at("gram_mm", t + 1))
                    for h in range(HEADS):
                        row = pt[:, 2, h * P:(h + 1) * P]
                        ins = dve.tensor_scalar(gd(t, "ats")[:, h * P:(h + 1) * P], row, ccol[:, 2 + t, h:h + 1], 0.0,
                                                ALU.subtract, ALU.max)
                    ins.then_inc(S["g_diff"], 1)
                    for h in range(HEADS):
                        row = pt[:, 2, h * P:(h + 1) * P]
                        ins = dve.tensor_scalar(gd(t, "it")[:, h * P:(h + 1) * P], row, ccol[:, 2 + t, h:h + 1], 0.0,
                                                ALU.subtract, ALU.min)
                    ins.then_inc(S["g_diff"], 1)
                    dve.wait_ge(S["g_exp"], at("g_exp", 2 * t + 1))
                    dve.tensor_tensor(hv(gd(t, "ats")), hv(gd(t, "ats")), bc(strict[:, :]), ALU.mult).then_inc(S["g_em"], 1)
                    dve.wait_ge(S["g_em"], at("g_em", 2 * t + 1))
                    dve.wait_ge(S["beta"], at("beta", 1))
                    for h in range(HEADS):
                        sl = slice(h * P, (h + 1) * P)
                        ins = dve.scalar_tensor_tensor(out=gd(t, "m")[:, sl], in0=pt[:, 0, sl],
                                                       scalar=beta[:, t, h:h + 1], in1=gd(t, "ats")[:, sl],
                                                       op0=ALU.mult, op1=ALU.mult)
                    ins.then_inc(S["g_a"], 1)
                    dve.wait_ge(S["g_exp"], at("g_exp", 2 * t + 2))
                    dve.tensor_tensor(hv(gd(t, "it")), hv(gd(t, "it")), bc(incl_t[:, :]), ALU.mult).then_inc(S["g_em"], 1)
                    dve.wait_ge(S["g_em"], at("g_em", 2 * t + 2))
                    dve.tensor_tensor(gd(t, "it"), gd(t, "it"), pt[:, 1, :], ALU.mult).then_inc(S["g_mats"], 1)

                def inv_start(t):
                    dve.wait_ge(S["g_a"], at("g_a", t + 1))
                    dve.tensor_tensor(hv(gd(t, "ats")), hv(gd(t, "m")), bc(lev1[:, :]), ALU.mult).then_inc(S["x_tmp"], 1)
                    dve.wait_ge(S["x_tmp"], at("x_tmp", 2 * t + 1))
                    dve.tensor_tensor(hv(gd(t, "x")), bc(ident[:, :]), hv(gd(t, "ats")), ALU.subtract).then_inc(S["x_set"], 1)
                    dve.wait_ge(S["at"], at("at", t + 1))
                    dve.wait_ge(S["x_set"], at("x_set", t + 1))
                    dve.tensor_tensor(hv(gd(t, "ats")), hv(gd(t, "at")), bc(lev_t[:, 0, :]), ALU.mult).then_inc(S["x_tmp"], 1)
                    dve.wait_ge(S["x_tmp"], at("x_tmp", 2 * t + 2))
                    dve.tensor_tensor(hv(gd(t, "xt")), bc(ident[:, :]), hv(gd(t, "ats")), ALU.subtract).then_inc(S["inv_x"], 1)
                    dve.wait_ge(S["inv_x"], at("inv_x", t + 1))
                    dve.tensor_tensor(hv(gd(t, "ats")), hv(gd(t, "at")), bc(lev_t[:, 1, :]), ALU.mult).then_inc(S["ats"], 1)

                def inv_step(lv):
                    for t in range(NT):
                        dve.wait_ge(S["m2_mm"], at("m2_mm", 2 * (lv - 1) + t + 1))
                        b = 2 - 2 * t
                        if lv < 6:
                            dve.tensor_tensor(gd(t, "x"), gd(t, "x"), pt[:, b, :], ALU.subtract).then_inc(S["inv_m"], 1)
                        dve.tensor_tensor(gd(t, "xt"), gd(t, "xt"), pt[:, b + 1, :], ALU.subtract).then_inc(S["inv_x"], 1)
                        if lv < 6:
                            dve.tensor_tensor(hv(gd(t, "ats")), hv(gd(t, "at")), bc(lev_t[:, lv + 1, :]), ALU.mult).then_inc(S["ats"], 1)

                def bv():
                    dve.wait_ge(S["m2_mm"], at("m2_mm", 12))
                    for h in range(HEADS):
                        ins = dve.tensor_scalar(gd(0, "ats")[:, h * P:(h + 1) * P], vn[:, 0, h, :], beta[:, 0, h:h + 1],
                                                None, ALU.mult)
                    ins.then_inc(S["bv"], 1)

                def f1():
                    dve.wait_ge(S["vnew_mm"], at("vnew_mm", 1))
                    dve.wait_ge(S["dec"], at("dec", 1))
                    dve.tensor_copy(scr[:, 3072:3584], pt[:, 0, :]).then_inc(S["vnew"], 1)
                    for h in range(HEADS):
                        sl = slice(h * P, (h + 1) * P)
                        ins = dve.tensor_scalar(scr[:, 3584:4096][:, sl], pt[:, 0, sl], dec[:, h:h + 1], None, ALU.mult)
                    ins.then_inc(S["vnew"], 1)

                def f2():
                    dve.wait_ge(S["o0_mm"], at("o0_mm", 1))
                    dve.tensor_copy(lnw[:, 0, 0:512], pt[:, 2, :]).then_inc(S["o_raw"], 1)

                def f3():
                    dve.wait_ge(S["zq_mm"], at("zq_mm", 1))
                    dve.wait_ge(S["egc"], at("egc", 1))
                    for h in range(HEADS):
                        sl = slice(h * P, (h + 1) * P)
                        ins = dve.scalar_tensor_tensor(out=gd(0, "m")[:, sl], in0=pt[:, 0, sl], scalar=egc[:, h:h + 1],
                                                       in1=vn[:, 1, h, :], op0=ALU.mult, op1=ALU.subtract)
                    ins.then_inc(S["z_v"], 1)
                    dve.wait_ge(S["z_v"], at("z_v", 1))
                    dve.tensor_scalar(beta_t[:, 1, :], beta[:, 1, :], -1.0, None, ALU.mult).then_inc(S["beta_n"], 1)
                    dve.wait_ge(S["beta_n"], at("beta_n", 1))
                    for h in range(HEADS):
                        sl = slice(h * P, (h + 1) * P)
                        ins = dve.tensor_scalar(gd(1, "ats")[:, sl], gd(0, "m")[:, sl], beta_t[:, 1, h:h + 1], None, ALU.mult)
                    ins.then_inc(S["rhs1"], 1)
                    for h in range(HEADS):
                        sl = slice(h * P, (h + 1) * P)
                        ins = dve.tensor_scalar(gd(0, "at")[:, sl], pt[:, 3, sl], egc[:, h:h + 1], None, ALU.mult)
                    ins.then_inc(S["q_s"], 1)

                def f4():
                    dve.wait_ge(S["vnew_mm"], at("vnew_mm", 2))
                    dve.wait_ge(S["o0_mm"], at("o0_mm", 1))
                    dve.tensor_copy(scr[:, 3072:3584], pt[:, 1, :]).then_inc(S["vnew"], 1)

                def o_square(t):
                    dve.wait_ge(S["o_ss"], at("o_ss", t + 1))
                    dve.tensor_scalar(oss[:, 4 * t:4 * t + 4], oss[:, 4 * t:4 * t + 4], 1.0 / P, RMS_EPS,
                                      ALU.mult, ALU.add).then_inc(S["o_ms"], 1)

                def o_gate(t):
                    dve.wait_ge(S["o_rs"], at("o_rs", t + 1))
                    for h in range(HEADS):
                        sl = slice(h * P, (h + 1) * P)
                        ins = dve.scalar_tensor_tensor(out=lnw[:, t, 512:1024][:, sl], in0=lnw[:, t, 0:512][:, sl],
                                                       scalar=ors[:, 4 * t + h:4 * t + h + 1], in1=nrmg[:, :],
                                                       op0=ALU.mult, op1=ALU.mult)
                    ins.then_inc(S["o_n"], 1)
                    dve.wait_ge(S["o_n"], at("o_n", t + 1))
                    dve.tensor_tensor(lnw[:, t, 512:1024], lnw[:, t, 512:1024], ggs[:, t, :], ALU.mult).then_inc(S["o_gated"], 1)

                def f5():
                    dve.wait_ge(S["o1_mm"], at("o1_mm", 1))
                    dve.wait_ge(S["q_s"], at("q_s", 1))
                    dve.tensor_tensor(lnw[:, 1, 0:512], gd(0, "at"), pt[:, 2, :], ALU.add).then_inc(S["o_raw"], 1)
                    o_square(0)
                    o_square(1)
                    o_gate(0)
                    o_gate(1)

                def branch_lo(first, n, k):
                    dve.wait_ge(S["o_hi"], at("o_hi", k))
                    dve.tensor_tensor(hlo[:, first:first + n, :], ot[:, first:first + n, :],
                                      hhi[:, first:first + n, :].bitcast(F32), ALU.subtract).then_inc(S["o_lo"], 1)

                def gated(b):
                    for t in range(NT):
                        for n in (0, 1):
                            if (t, n) == (1, 1):
                                dve.wait_ge(S["w_used"], at("w_used", 2 * (U_M + BR0 + (1, 2, 4)[b])))
                            else:
                                dve.wait_ge(S["yb_mm"], at("yb_mm", 3 * b + 2 * t + n + 1))
                            g = gates[:, t, b * D + n * 512:b * D + (n + 1) * 512]
                            if b == 0:
                                dve.wait_ge(S["gates"], at("gates", 1))
                                dve.wait_ge(S["zq_mm"], at("zq_mm", 1))
                            dve.tensor_tensor(merged[:, t, n * 512:(n + 1) * 512] if b == 0 else g,
                                              pg[:, 2 * t + n, :], g, ALU.mult).then_inc(S["y_ev"], 1)

                def merge(b):
                    for t in range(NT):
                        for n in (0, 1):
                            g = gates[:, t, b * D + n * 512:b * D + (n + 1) * 512]
                            m = merged[:, t, n * 512:(n + 1) * 512]
                            dve.wait_ge(S["y_ev"], at("y_ev", 4 * b + 2 * t + n + 1))
                            if b == 2:
                                dve.wait_ge(S["merged1"], at("merged1", 4))
                            dve.tensor_tensor(m, m, g, ALU.add).then_inc(S["merged" if b == 2 else "merged1"], 1)

                def merged_lo(t):
                    dve.wait_ge(S["m_hi"], at("m_hi", t + 1))
                    dve.tensor_tensor(hlo[:, :, t * P:(t + 1) * P],
                                      pt[:, 2 * t:2 * t + 2, :].rearrange("p b (k s) -> p (b k) s", k=4),
                                      hhi[:, :, t * P:(t + 1) * P].bitcast(F32), ALU.subtract).then_inc(S["m_lo"], 1)

                tasks = {
                    "qk_norm": qk_norm, "params": params, "params2": params2, "rows": fox_bias, "fox_p": fox_softmax,
                    "sb_z": sb_z, "sb_sp": sb_softplus, "sb_r": sb_arg, "kv": lambda: (g_rows(0), g_rows(1)),
                    "dec0": lambda: g_mats(0), "dec1": lambda: (inv_start(0), g_mats(1)), "inv0": lambda: inv_start(1),
                    "f1": f1, "f2": f2, "f3": f3, "f4": f4, "f5": f5,
                    "o_split": lambda: branch_lo(0, 4, 1), "c_split": lambda: branch_lo(4, 4, 2),
                    "mrg": lambda: (merged_lo(0), merged_lo(1)),
                }
                for lv in range(1, 7):
                    tasks[f"mb{lv}"] = lambda lv=lv: (inv_step(lv), bv() if lv == 6 else None)
                for k in range(3):
                    for tap in range(1, TAPS):
                        tasks[f"tap{k}{tap}"] = lambda k=k, tap=tap: conv(k, tap)

                def mixer():
                    pad()
                    for i in range(MIX_U):
                        for half in (0, 1):
                            h = 2 * i + half + 3
                            if i < MIX_U - 1:
                                split(2 * U_M + h, 24 if h // 2 in (8, 9) else 1024)
                            if (i, half) == (1, 1):
                                gate_bc(1, 1.0)
                            if half == 1 and i in (BR0, BR0 + 1, BR0 + 3):
                                gated({0: 0, 1: 1, 3: 2}[i - BR0])
                            if (i, half) in ((BR0 + 2, 0), (BR0 + 3, 1)):
                                merge(i - BR0 - 1)
                            for task in TASKS.get((i, half), ()):
                                if task in tasks:
                                    tasks[task]()
                            if (i, half) == (34, 0):
                                mod_cols(False, at, 1, l * 24 + 8)
                    norm_stage(1, U_B)

                ffn(0, 0, U_A, True)
                mixer()
                ffn(1, 2, U_B, False)


_INS = ["x", "c", "w_ada", "b_ada", "ln_g", "ln_b", "ffn_w_up", "ffn_w_down", "w_in", "b_forget", "conv_w",
        "gdn_a_log", "gdn_dt_bias", "gdn_norm_g", "w_branch", "w_o"]


def kernel(**inputs):
    import numpy as _np
    import concourse.bacc as _bacc
    from concourse import mybir as _mybir
    from concourse.bass_utils import run_bass_kernel_spmd as _run

    nc = _bacc.Bacc("TRN2", target_bir_lowering=False, num_devices=1)
    arrays, args = {}, []
    for name in _INS:
        a = _np.ascontiguousarray(inputs[name])
        arrays[f"in_{name}_dram"] = a
        args.append(nc.dram_tensor(f"in_{name}_dram", a.shape, _mybir.dt.from_np(a.dtype), kind="ExternalInput").ap())
    args.append(nc.dram_tensor("out_0_dram", inputs["x"].shape, _mybir.dt.float32, kind="ExternalOutput").ap())
    trunk(nc, *args)
    r = _run(nc, [arrays], core_ids=[0])
    return r.results[0]["out_0_dram"]
```
